# Optimizing a Trainium2 kernel written in Bass

```python
import math
import jax, jax.numpy as jnp
from jax import lax
import numpy as np

D_MODEL = 1024
BATCH = 1
SEQ = 512
DEPTH = 1

HEAD_DIM = 64
N_FOX_HEADS = 8
N_DIL_HEADS = 8
FOX_WIDTH = N_FOX_HEADS * HEAD_DIM
DIL_WIDTH = N_DIL_HEADS * HEAD_DIM
MIX_WIDTH = FOX_WIDTH + DIL_WIDTH
IN_WIDTH = 3 * FOX_WIDTH + N_FOX_HEADS + 3 * DIL_WIDTH
DILATION_PATTERNS = ((128, 1), (512, 4), (2048, 16))
Q_BLOCK = 128
RMS_EPS = 1e-6
NEG_INF = -1e30

PEER_HEADS = 8
PEER_NKEYS = 128
PEER_EXPERTS = PEER_NKEYS * PEER_NKEYS
PEER_TOPK = 16
PEER_QDIM = 256
PEER_HALF = PEER_QDIM // 2
PEER_CHUNK = 128


def rms_norm(x, g):
    xf = x.astype(jnp.float32)
    y = xf * lax.rsqrt(jnp.mean(xf * xf, axis=-1, keepdims=True) + RMS_EPS)
    return (y * g.astype(jnp.float32)).astype(x.dtype)

def split_heads(a, n_heads):
    b, t, _ = a.shape
    return a.reshape(b, t, n_heads, HEAD_DIM).transpose(0, 2, 1, 3)

def merge_heads(a):
    b, h, t, d = a.shape
    return a.transpose(0, 2, 1, 3).reshape(b, t, h * d)

def alibi_slopes(n):
    return 2.0 ** (-8.0 * jnp.arange(1, n + 1, dtype=jnp.float32) / n)

def fox_attention(q, k, v, log_f):
    b, h, t, hd = q.shape
    c = jnp.cumsum(log_f, axis=-1)
    scale = 1.0 / math.sqrt(hd)
    kpos = jnp.arange(t)

    def block(i):
        t0 = i * Q_BLOCK
        qb = lax.dynamic_slice_in_dim(q, t0, Q_BLOCK, axis=2)
        cq = lax.dynamic_slice_in_dim(c, t0, Q_BLOCK, axis=2)
        s = jnp.einsum('bhqd,bhkd->bhqk', qb, k).astype(jnp.float32) * scale
        s = s + cq[..., :, None] - c[:, :, None, :]
        qpos = t0 + jnp.arange(Q_BLOCK)
        mask = kpos[None, :] <= qpos[:, None]
        s = jnp.where(mask, s, NEG_INF)
        p = jax.nn.softmax(s, axis=-1)
        return jnp.einsum('bhqk,bhkd->bhqd', p.astype(v.dtype), v)

    out = lax.map(block, jnp.arange(t // Q_BLOCK))
    return out.transpose(1, 2, 0, 3, 4).reshape(b, h, t, hd)

def dilated_window_branch(q, k, v, window, dilation, slopes):
    b, h, t, hd = q.shape
    n_steps = window // dilation
    sub_len = t // dilation
    nb = -(-sub_len // Q_BLOCK)
    pad = nb * Q_BLOCK - sub_len

    def to_sub(a):
        a = a.reshape(b, h, sub_len, dilation, hd).transpose(0, 1, 3, 2, 4)
        a = jnp.pad(a, ((0, 0), (0, 0), (0, 0), (0, pad), (0, 0)))
        return a.reshape(b, h, dilation, nb, Q_BLOCK, hd)

    qs, ks, vs = to_sub(q), to_sub(k), to_sub(v)

    def with_prev(a):
        prev = jnp.concatenate([jnp.zeros_like(a[:, :, :, :1]), a[:, :, :, :-1]], axis=3)
        return jnp.concatenate([prev, a], axis=4)

    kc, vc = with_prev(ks), with_prev(vs)
    s = jnp.einsum('bhrnqd,bhrnkd->bhrnqk', qs, kc).astype(jnp.float32) / math.sqrt(hd)

    qi = jnp.arange(Q_BLOCK)[:, None] + Q_BLOCK
    ki = jnp.arange(2 * Q_BLOCK)[None, :]
    steps = qi - ki
    band = (steps >= 0) & (steps <= n_steps)
    key_sub = jnp.arange(nb)[:, None, None] * Q_BLOCK - Q_BLOCK + ki[None]
    valid = band[None] & (key_sub >= 0)
    bias = -slopes[:, None, None, None, None] * (dilation * steps).astype(jnp.float32)[None, None, None]
    s = jnp.where(valid, s + bias, NEG_INF)
    lse = jax.nn.logsumexp(s, axis=-1)
    p = jnp.exp(s - lse[..., None])
    o = jnp.einsum('bhrnqk,bhrnkd->bhrnqd', p.astype(vc.dtype), vc)

    def from_sub(a, tail):
        a = a.reshape((b, h, dilation, nb * Q_BLOCK) + tail)[:, :, :, :sub_len]
        a = jnp.swapaxes(a, 2, 3)
        return a.reshape((b, h, t) + tail)

    return from_sub(o, (hd,)), from_sub(lse, ())

def dilated_attention(q, k, v):
    slopes = alibi_slopes(q.shape[1])
    outs, lses = [], []
    for window, dilation in DILATION_PATTERNS:
        o, l = dilated_window_branch(q, k, v, window, dilation, slopes)
        outs.append(o)
        lses.append(l)
    w = jax.nn.softmax(jnp.stack(lses, axis=0), axis=0)
    o = jnp.stack(outs, axis=0).astype(jnp.float32)
    return jnp.sum(w[..., None] * o, axis=0).astype(q.dtype)

def peer_ffn(xn, wq, subkeys, u_table, v_table):
    b, t, d = xn.shape
    xt = xn.reshape(-1, PEER_CHUNK, d)

    def chunk(xc):
        q = (xc @ wq).reshape(PEER_CHUNK, PEER_HEADS, 2, PEER_HALF)
        s = jnp.einsum('chpd,hpkd->chpk', q, subkeys).astype(jnp.float32)
        s1, i1 = lax.top_k(s[:, :, 0], PEER_TOPK)
        s2, i2 = lax.top_k(s[:, :, 1], PEER_TOPK)
        cand = (s1[..., :, None] + s2[..., None, :]).reshape(PEER_CHUNK, PEER_HEADS, PEER_TOPK * PEER_TOPK)
        cidx = (i1[..., :, None] * PEER_NKEYS + i2[..., None, :]).reshape(PEER_CHUNK, PEER_HEADS, PEER_TOPK * PEER_TOPK)
        cs, ci = lax.top_k(cand, PEER_TOPK)
        eidx = jnp.take_along_axis(cidx, ci, axis=-1)
        g = jax.nn.softmax(cs, axis=-1)
        ug = jnp.take(u_table, eidx, axis=0)
        vg = jnp.take(v_table, eidx, axis=0)
        hid = jnp.einsum('cd,chkd->chk', xc, ug).astype(jnp.float32)
        a = jax.nn.gelu(hid, approximate=False) * g
        return jnp.einsum('chk,chkd->cd', a.astype(vg.dtype), vg)

    out = lax.map(chunk, xt)
    return out.reshape(b, t, d)

def first_inputs(seed: int = 0) -> dict:
    key = jax.random.key(seed)
    ks = jax.random.split(key, 14)
    f32 = jnp.float32
    sd = D_MODEL ** -0.5
    x = jax.random.normal(ks[0], (BATCH, SEQ, D_MODEL), f32)
    norm1_g = 1.0 + 0.05 * jax.random.normal(ks[1], (DEPTH, D_MODEL), f32)
    w_in = jnp.concatenate([
        sd * jax.random.normal(ks[2], (DEPTH, D_MODEL, 3 * FOX_WIDTH), f32),
        0.1 * sd * jax.random.normal(ks[3], (DEPTH, D_MODEL, N_FOX_HEADS), f32),
        sd * jax.random.normal(ks[4], (DEPTH, D_MODEL, 3 * DIL_WIDTH), f32),
    ], axis=-1)
    b_forget = 3.0 + 0.1 * jax.random.normal(ks[5], (DEPTH, N_FOX_HEADS), f32)
    w_out = MIX_WIDTH ** -0.5 * jax.random.normal(ks[6], (DEPTH, MIX_WIDTH, D_MODEL), f32)
    norm2_g = 1.0 + 0.05 * jax.random.normal(ks[7], (DEPTH, D_MODEL), f32)
    peer_wq = sd * jax.random.normal(ks[8], (DEPTH, D_MODEL, PEER_HEADS * PEER_QDIM), f32)
    peer_subkeys = PEER_HALF ** -0.5 * jax.random.normal(ks[9], (DEPTH, PEER_HEADS, 2, PEER_NKEYS, PEER_HALF), f32)
    peer_u = sd * jax.random.normal(ks[10], (DEPTH, PEER_EXPERTS, D_MODEL), f32)
    peer_v = (PEER_HEADS ** -0.5) * jax.random.normal(ks[11], (DEPTH, PEER_EXPERTS, D_MODEL), f32)
    normf_g = 1.0 + 0.05 * jax.random.normal(ks[12], (D_MODEL,), f32)
    return {"x": x, "norm1_g": norm1_g, "w_in": w_in, "b_forget": b_forget, "w_out": w_out,
            "norm2_g": norm2_g, "peer_wq": peer_wq, "peer_subkeys": peer_subkeys,
            "peer_u": peer_u, "peer_v": peer_v, "normf_g": normf_g}

def first_block(x, norm1_g, w_in, b_forget, w_out, norm2_g, peer_wq, peer_subkeys, peer_u, peer_v, normf_g):
    h = x
    for layer in range(DEPTH):
        xn = rms_norm(h, norm1_g[layer])
        proj = xn @ w_in[layer]
        o0 = 3 * FOX_WIDTH
        o1 = o0 + N_FOX_HEADS
        fq = split_heads(proj[..., :FOX_WIDTH], N_FOX_HEADS)
        fk = split_heads(proj[..., FOX_WIDTH:2 * FOX_WIDTH], N_FOX_HEADS)
        fv = split_heads(proj[..., 2 * FOX_WIDTH:o0], N_FOX_HEADS)
        log_f = jax.nn.log_sigmoid(proj[..., o0:o1].astype(jnp.float32)
                                   + b_forget[layer].astype(jnp.float32)).transpose(0, 2, 1)
        dq = split_heads(proj[..., o1:o1 + DIL_WIDTH], N_DIL_HEADS)
        dk = split_heads(proj[..., o1 + DIL_WIDTH:o1 + 2 * DIL_WIDTH], N_DIL_HEADS)
        dv = split_heads(proj[..., o1 + 2 * DIL_WIDTH:o1 + 3 * DIL_WIDTH], N_DIL_HEADS)
        fox_out = fox_attention(fq, fk, fv, log_f)
        dil_out = dilated_attention(dq, dk, dv)
        mixed = jnp.concatenate([merge_heads(fox_out), merge_heads(dil_out)], axis=-1)
        h = h + mixed @ w_out[layer]
        xn2 = rms_norm(h, norm2_g[layer])
        h = h + peer_ffn(xn2, peer_wq[layer], peer_subkeys[layer], peer_u[layer], peer_v[layer])
    return rms_norm(h, normf_g)


N_RET_HEADS = 8
RET_HEAD_DIM = D_MODEL // N_RET_HEADS
RET_WIDTH = N_RET_HEADS * RET_HEAD_DIM
RET_CHUNK = 128
ROPE_BASE = 10000.0
CONV_WIDTH = D_MODEL
CONV_GROUPS = 8
CONV_K = 3
FFN_HIDDEN = -(-8 * D_MODEL // (3 * 256)) * 256
EPS = 1e-6
N_MOD = 6
IN_SPLITS = [RET_WIDTH, RET_WIDTH, RET_WIDTH, RET_WIDTH,
             CONV_WIDTH, CONV_WIDTH, CONV_WIDTH,
             D_MODEL, D_MODEL]
IN_COLS = sum(IN_SPLITS)


def rmsnorm(x, g):
    xf = x.astype(jnp.float32)
    y = xf * lax.rsqrt(jnp.mean(xf * xf, axis=-1, keepdims=True) + EPS)
    return (y * g.astype(jnp.float32)).astype(x.dtype)

def head_layernorm(y):
    yf = y.astype(jnp.float32)
    mu = jnp.mean(yf, axis=-1, keepdims=True)
    var = jnp.mean((yf - mu) ** 2, axis=-1, keepdims=True)
    return ((yf - mu) * lax.rsqrt(var + EPS)).astype(y.dtype)

def modulate(h, shift, scale):
    return h * (1.0 + scale[:, None, :]) + shift[:, None, :]

def rope(t, cos, sin):
    t1, t2 = jnp.split(t, 2, axis=-1)
    out = jnp.concatenate([t1 * cos - t2 * sin, t1 * sin + t2 * cos], axis=-1)
    return out.astype(t.dtype)

def retention_chunkwise(q, k, v, log_gamma):
    B, S, H, d = q.shape
    N = S // RET_CHUNK

    def to_chunks(t):
        return t.reshape(B, N, RET_CHUNK, H, t.shape[-1]).transpose(0, 3, 1, 2, 4)

    qc, kc, vc = to_chunks(q), to_chunks(k), to_chunks(v)
    idx = jnp.arange(RET_CHUNK, dtype=jnp.float32)
    rel = idx[:, None] - idx[None, :]
    lg = log_gamma[:, None, None]
    dmask = jnp.where(rel >= 0, jnp.exp(lg * jnp.maximum(rel, 0.0)), 0.0)
    scores = jnp.einsum('bhncd,bhnmd->bhncm', qc, kc) * dmask[None, :, None]
    inner = jnp.einsum('bhncm,bhnme->bhnce', scores, vc)
    zeta = jnp.exp(log_gamma[:, None] * (RET_CHUNK - 1 - idx)[None, :])
    kv = jnp.einsum('bhncd,bhnce->bhnde', kc * zeta[None, :, None, :, None], vc)
    chunk_decay = jnp.exp(log_gamma * RET_CHUNK)[None, :, None, None]

    def step(R, kv_n):
        return R * chunk_decay + kv_n, R

    _, R_prev = lax.scan(step, jnp.zeros_like(kv[:, :, 0]), kv.transpose(2, 0, 1, 3, 4))
    R_prev = R_prev.transpose(1, 2, 0, 3, 4)
    xi = jnp.exp(log_gamma[:, None] * (idx + 1.0)[None, :])
    cross = jnp.einsum('bhncd,bhnde->bhnce', qc, R_prev) * xi[None, :, None, :, None]
    out = inner + cross
    return out.transpose(0, 2, 3, 1, 4).reshape(B, S, H, vc.shape[-1])

def second_inputs(seed: int = 0) -> dict:
    key = jax.random.key(seed)
    ks = jax.random.split(key, 20)
    D = D_MODEL
    nrm = lambda k, shape, fan_in, s=1.0: s * jax.random.normal(k, shape, jnp.float32) * fan_in ** -0.5
    x = jax.random.normal(ks[0], (BATCH, SEQ, D), jnp.float32)
    c = jax.random.normal(ks[1], (BATCH, D), jnp.float32)
    positions = jnp.broadcast_to(jnp.arange(SEQ, dtype=jnp.int32)[None, :], (BATCH, SEQ))
    return {
        "x": x,
        "c": c,
        "positions": positions,
        "ada_w": nrm(ks[2], (DEPTH, D, N_MOD * D), D, 0.1),
        "ada_b": 0.02 * jax.random.normal(ks[3], (DEPTH, N_MOD * D), jnp.float32),
        "norm_mix_g": 1.0 + 0.02 * jax.random.normal(ks[4], (DEPTH, D), jnp.float32),
        "w_in": nrm(ks[5], (DEPTH, D, IN_COLS), D),
        "conv_w": nrm(ks[6], (DEPTH, CONV_K, CONV_WIDTH), CONV_K),
        "ret_w_out": nrm(ks[7], (DEPTH, RET_WIDTH, D), RET_WIDTH),
        "conv_w_out": nrm(ks[8], (DEPTH, CONV_WIDTH, D), CONV_WIDTH),
        "mix_w_out": nrm(ks[9], (DEPTH, D, D), D),
        "norm_ffn_g": 1.0 + 0.02 * jax.random.normal(ks[10], (DEPTH, D), jnp.float32),
        "ffn_w_gate": nrm(ks[11], (DEPTH, D, FFN_HIDDEN), D),
        "ffn_w_up": nrm(ks[12], (DEPTH, D, FFN_HIDDEN), D),
        "ffn_w_down": nrm(ks[13], (DEPTH, FFN_HIDDEN, D), FFN_HIDDEN),
        "final_norm_g": 1.0 + 0.02 * jax.random.normal(ks[14], (D,), jnp.float32),
    }

def second_block(x, c, positions, ada_w, ada_b, norm_mix_g, w_in, conv_w, ret_w_out,
              conv_w_out, mix_w_out, norm_ffn_g, ffn_w_gate, ffn_w_up, ffn_w_down,
              final_norm_g):
    B, S, D = x.shape
    H, d = N_RET_HEADS, RET_HEAD_DIM
    log_gamma = jnp.log(1.0 - 2.0 ** (-5.0 - jnp.arange(H, dtype=jnp.float32)))
    inv_freq = 1.0 / (ROPE_BASE ** (jnp.arange(0, d, 2, dtype=jnp.float32) / d))
    ang = positions.astype(jnp.float32)[..., None] * inv_freq
    cos, sin = jnp.cos(ang)[:, :, None, :], jnp.sin(ang)[:, :, None, :]
    split_pts = list(np.cumsum(IN_SPLITS)[:-1])
    cs = jax.nn.silu(c)

    for l in range(DEPTH):
        mod = cs @ ada_w[l] + ada_b[l]
        sh_m, sc_m, gt_m, sh_f, sc_f, gt_f = jnp.split(mod, N_MOD, axis=-1)

        h = modulate(rmsnorm(x, norm_mix_g[l]), sh_m, sc_m)
        proj = h @ w_in[l]
        q, k, v, g_ret, b_cv, c_cv, u_cv, g_a, g_b = jnp.split(proj, split_pts, axis=-1)

        q = rope(q.reshape(B, S, H, d), cos, sin)
        k = rope(k.reshape(B, S, H, d), cos, sin) * (d ** -0.5)
        v = v.reshape(B, S, H, d)
        y_ret = head_layernorm(retention_chunkwise(q, k, v, log_gamma)).reshape(B, S, RET_WIDTH)
        y_a = (jax.nn.silu(g_ret) * y_ret) @ ret_w_out[l]

        u = c_cv * u_cv
        u_pad = jnp.pad(u, ((0, 0), (CONV_K - 1, 0), (0, 0)))
        w = conv_w[l]
        conv = u_pad[:, 0:S] * w[0]
        for tap in range(1, CONV_K):
            conv = conv + u_pad[:, tap:tap + S] * w[tap]
        y_b = (b_cv * conv) @ conv_w_out[l]

        merged = jax.nn.sigmoid(g_a) * y_a + jax.nn.sigmoid(g_b) * y_b
        x = x + gt_m[:, None, :] * (merged @ mix_w_out[l])

        h = modulate(rmsnorm(x, norm_ffn_g[l]), sh_f, sc_f)
        f = (jax.nn.silu(h @ ffn_w_gate[l]) * (h @ ffn_w_up[l])) @ ffn_w_down[l]
        x = x + gt_f[:, None, :] * f

    return rmsnorm(x, final_norm_g)


def setup_inputs(seed=0):
    out = dict(first_inputs(seed))
    for name, value in second_inputs(seed + 1).items():
        if name != "x":
            out[name + "_2"] = value
    return out


def reference(
    x, norm1_g, w_in, b_forget, w_out, norm2_g, peer_wq, peer_subkeys, peer_u, peer_v, normf_g,
    c_2, positions_2, ada_w_2, ada_b_2, norm_mix_g_2, w_in_2, conv_w_2, ret_w_out_2,
    conv_w_out_2, mix_w_out_2, norm_ffn_g_2, ffn_w_gate_2, ffn_w_up_2, ffn_w_down_2,
    final_norm_g_2,
):
    x = first_block(
        x, norm1_g, w_in, b_forget, w_out, norm2_g, peer_wq, peer_subkeys, peer_u, peer_v,
        normf_g,
    )
    return second_block(
        x, c_2, positions_2, ada_w_2, ada_b_2, norm_mix_g_2, w_in_2, conv_w_2, ret_w_out_2,
        conv_w_out_2, mix_w_out_2, norm_ffn_g_2, ffn_w_gate_2, ffn_w_up_2, ffn_w_down_2,
        final_norm_g_2,
    )


_drawn_inputs = setup_inputs


def setup_inputs(seed=0):
    import zlib

    import numpy as np

    out = dict(_drawn_inputs(seed))
    spreads = {}
    factors = {'b_forget': 23.696,
     'ada_b_2': 3.128,
     'norm_mix_g_2': 8.0,
     'ret_w_out_2': 2.751,
     'norm_ffn_g_2': 64.0,
     'final_norm_g_2': 7.828}
    for name, (base, spread) in spreads.items():
        noise = np.random.default_rng([zlib.crc32(name.encode()), seed]).standard_normal(out[name].shape)
        drawn = base * np.exp(spread * noise) if base else spread * noise
        out[name] = __import__('jax').numpy.asarray(drawn.astype(out[name].dtype))
    for name, factor in factors.items():
        out[name] = (out[name] * factor).astype(out[name].dtype)
    return out
```

```python
from contextlib import ExitStack

import numpy as np
import concourse.bass as bass
from concourse import mybir

F32 = mybir.dt.float32
F32R = mybir.dt.float32r
BF16 = mybir.dt.bfloat16
I32 = mybir.dt.int32
U32 = mybir.dt.uint32
ALU = mybir.AluOpType
ACT = mybir.ActivationFunctionType
AX = mybir.AxisListType

T = 512
NEG = -1e30
LOWEST = -3.0e38
NRAW = 6
NW = 4
W_BLOCK1 = 49
W_BLOCK2 = 162
EPS = 1e-6


class Queue:

    def __init__(self, sem):
        self.sem, self.n, self.ops, self.seen = sem, 0, [], {}

    def wait(self, *tokens):
        for t in tokens:
            if t is None:
                continue
            if isinstance(t, list):
                self.wait(*t)
                continue
            sem, value = t
            if self.seen.get(sem.num, 0) < value:
                self.seen[sem.num] = value
                self.ops.append(lambda e, s=sem, v=value: e.wait_ge(s, v))

    def quiet(self, fn, *tokens):
        self.wait(*tokens)
        self.ops.append(fn)

    def do(self, fn, *tokens):
        self.wait(*tokens)
        self.n += 1
        self.ops.append(lambda e: fn(e).then_inc(self.sem, 1))
        return (self.sem, self.n)

    def play(self, e):
        for op in self.ops:
            op(e)


class Lane:

    def __init__(self, sem):
        self.sem, self.n = sem, 0


class Slots:

    def __init__(self, bufs):
        self.bufs, self.free, self.i = list(bufs), [[] for _ in bufs], -1

    def take(self):
        assert any(f is not None for f in self.free)
        self.i = (self.i + 1) % len(self.bufs)
        while self.free[self.i] is None:
            self.i = (self.i + 1) % len(self.bufs)
        free, self.free[self.i] = self.free[self.i], None
        return self.i, self.bufs[self.i], free


def build_program(nc, x, wts, ut, vt, skt, small, cst, dmat, augd, pos, adaw, out):
    ctx = ExitStack()
    with ctx:
        def sem(name):
            return ctx.enter_context(nc.semaphore(name))

        base = -(-nc.sbuf_base // 64) * 64

        def at(name, kb, shape, dt):
            return nc.alloc_sbuf_tensor_at(name, shape, dt, offset=base + int(kb * 1024))

        PE, DVE, SC, GP = (Queue(sem(n)) for n in ("s_pe", "s_dve", "s_act", "s_pool"))
        SP = Queue(None)
        lanes = {}

        def dma(name, dst, src, *tokens):
            if name not in lanes:
                lanes[name] = Lane(sem("d_" + name))
            lane = lanes[name]
            if lane.n:
                SP.wait((lane.sem, 16 * lane.n))
            SP.wait(*tokens)
            lane.n += 1
            SP.ops.append(lambda e: e.dma_start(dst, src).then_inc(lane.sem, 16))
            return (lane.sem, 16 * lane.n)

        def copy(dst, src, *tokens, scale=None):
            if scale is None:
                return SC.do(lambda e: e.activation(dst, src, ACT.Copy), *tokens)
            return SC.do(lambda e: e.activation(dst, src, ACT.Copy, scale=scale), *tokens)

        def act(dst, src, func, *tokens, **kw):
            return SC.do(lambda e: e.activation(dst, src, func, **kw), *tokens)

        def tt(dst, a, b, op, *tokens):
            return DVE.do(lambda e: e.tensor_tensor(dst, a, b, op), *tokens)

        def ts(dst, a, s1, s2, op0, op1, *tokens):
            if op1 is None:
                return DVE.do(lambda e: e.tensor_scalar(dst, a, s1, None, op0), *tokens)
            return DVE.do(lambda e: e.tensor_scalar(dst, a, s1, s2, op0, op1), *tokens)

        def stt(dst, a, s, b, op0, op1, *tokens):
            return DVE.do(lambda e: e.scalar_tensor_tensor(out=dst, in0=a, scalar=s, in1=b,
                                                           op0=op0, op1=op1), *tokens)

        def mm(dst, lhs, rhs, start, stop, *tokens, last=False, skip=False):
            def fn(e):
                return e.matmul(dst, lhs, rhs, start=start, stop=stop, skip_group_check=skip)
            return PE.do(fn, *tokens) if last else PE.quiet(fn, *tokens)

        def vcopy(dst, src, *tokens):
            return DVE.do(lambda e: e.tensor_copy(dst, src), *tokens)

        def vset(dst, value, *tokens):
            return DVE.do(lambda e: e.memset(dst, value), *tokens)

        def recip(dst, src, *tokens):
            return DVE.do(lambda e: e.reciprocal(dst, src), *tokens)

        def reduce(dst, src, op, *tokens):
            return DVE.do(lambda e: e.tensor_reduce(dst, src, AX.X, op), *tokens)

        def turned(dst, src, *tokens):
            return PE.do(lambda e: e.transpose(dst, src, ident[:, :]), *tokens)

        def split(H, L, src, *tokens, scale=None):
            a = copy(H, src, *tokens, scale=scale)
            if scale is None:
                return [a, tt(L, src, H.bitcast(F32), ALU.subtract, a, *tokens)]
            return [a, stt(L, src, scale, H.bitcast(F32), ALU.mult, ALU.subtract, a, *tokens)]

        RAW = [at(f"raw{i}", 4 * i, [128, 1024], F32) for i in range(NRAW)]
        WH = [at(f"wh{i}", 24 + 4 * i, [128, 1024], F32R) for i in range(NW)]
        WL = [at(f"wl{i}", 40 + 4 * i, [128, 1024], F32R) for i in range(NW)]
        ident = at("ident", 56, [128, 128], F32)
        iota = at("iota", 56.5, [128, 128], F32)
        ones = at("ones", 57, [128, 128], F32)
        identb = at("identb", 57.5, [128, 128], BF16)
        sm = at("sm", 57.75, [128, 144], F32)
        csil = at("csil", 58.3125, [128, 8], F32)
        mod = at("mod", 58.375, [128, 48], F32)
        gmod = at("gmod", 58.5625, [128, 16], F32)
        st = at("st", 58.625, [128, 64], F32)
        invf = at("invf", 58.875, [128, 1], F32)
        XH = at("XH", 60, [128, 8, T], F32R)
        XL = at("XL", 76, [128, 8, T], F32R)
        Tb = Slots([at(f"T{i}", 92 + 2 * i, [128, T], F32) for i in range(7)])
        F = 106
        P = [ctx.enter_context(nc.psum_tensor(f"P{i}", [128, T], F32)) for i in range(8)]
        pfree = [[] for _ in range(8)]

        def take(b):
            free, pfree[b] = pfree[b], None
            assert free is not None, b
            return P[b], free

        class Banks:
            def __init__(self, ids):
                self.ids, self.i = ids, -1

            def next(self):
                self.i = (self.i + 1) % len(self.ids)
                b = self.ids[self.i]
                return (b, *take(b))

        def everyone():
            now = [(q.sem, q.n) for q in (PE, DVE, SC, GP) if q.n]
            for q in (PE, DVE, SC, GP, SP):
                q.wait(*now)

        stream = ([wts[i] for i in range(W_BLOCK1)] + [ut[i] for i in range(128)]
                  + [vt[i] for i in range(128)] + [wts[W_BLOCK1 + i] for i in range(W_BLOCK2)])
        raw_tok, split_tok, used_tok = {}, {}, {}
        state = {"dma": 0, "split": 0, "unit": 0}

        def load_to(n):
            while state["dma"] < min(n, len(stream)):
                i = state["dma"]
                free = split_tok.get(i - NRAW)
                raw_tok[i] = dma(f"w{i % NRAW}", RAW[i % NRAW][:, :], stream[i], free)
                state["dma"] += 1

        def split_to(n):
            while state["split"] < min(n, len(stream)):
                i = state["split"]
                load_to(i + 1)
                s = i % NW
                split_tok[i] = split(WH[s][:, :], WL[s][:, :], RAW[i % NRAW][:, :],
                                     raw_tok[i], used_tok.get(i - NW))
                load_to(i + NRAW)
                state["split"] += 1

        def next_unit():
            i = state["unit"]
            state["unit"] += 1
            split_to(i + NW)
            PE.wait(split_tok[i])
            return i, WH[i % NW], WL[i % NW]

        def unit_mms(bank, H, L, toks, free, first=True, final=True, k0=0, count=8, w0=0):
            i, wh, wl = cur
            PE.wait(free)
            for c in range(count):
                k = k0 + c
                w = slice((w0 + c) * 128, (w0 + c + 1) * 128)
                PE.wait(toks[k])
                mm(bank[:, :], wh[:, w], H[:, k, :], first and c == 0, False)
                mm(bank[:, :], wh[:, w], L[:, k, :], False, False)
                end = final and c == count - 1
                t = mm(bank[:, :], wl[:, w], H[:, k, :], False, end,
                       last=end or w0 + c == 7)
                if w0 + c == 7:
                    used_tok[i] = t
            return t

        cur = None

        def feature_major(b, H, L, toks):
            nonlocal cur
            bank, free = take(b)
            cur = next_unit()
            return unit_mms(bank, H, L, toks, free)

        def token_major(ids, H, L, toks):
            banks = [take(b) for b in ids]
            for u in range(4):
                i, wh, wl = next_unit()
                for tb in range(4):
                    PE.wait(banks[tb][1])
                    for c in range(2):
                        k = 2 * u + c
                        PE.wait(toks[k])
                        s = slice(tb * 128, (tb + 1) * 128)
                        w = slice(c * 512, (c + 1) * 512)
                        d = banks[tb][0][:, :]
                        mm(d, H[:, k, s], wh[:, w], k == 0, False)
                        mm(d, H[:, k, s], wl[:, w], False, False)
                        end = c == 1 and (u == 3 or tb == 3)
                        t = mm(d, L[:, k, s], wh[:, w], False, k == 7, last=end)
                        if end and u == 3:
                            if tb == 0:
                                done = []
                            done.append(t)
                        if c == 1 and tb == 3:
                            used_tok[i] = t
            return done

        CNT = at("CNT", F + 96, [128, T], F32)
        MDB = at("MDB", F + 98, [128, T], BF16)
        MCB = at("MCB", F + 99, [128, T], BF16)
        CS = at("CS", F + 48, [128, 1793], F32)
        k_c = dma("c0", CS[:, :], cst)
        k_s = dma("c1", sm[:, :], small)
        XIN = at("XIN", F, [128, 8, T], F32)
        xt = x.rearrange("(k p) t -> p k t", p=128)
        k_x = [dma(f"x{j}", XIN[:, 2 * j:2 * j + 2, :], xt[:, 2 * j:2 * j + 2, :]) for j in range(4)]
        AD = at("AD", F + 16, [8, 4, T], F32)
        k_ad = dma("c2", AD[:, :, :], augd)
        load_to(NRAW)
        d1 = vset(ones[:, :], 1.0)
        vcopy(ident[:, :], CS[:, 0:128], k_c)
        vcopy(identb[:, :], CS[:, 0:128])
        vcopy(iota[:, :], CS[:, 128:256])
        vcopy(CNT[:, :], CS[:, 256:768])
        vcopy(MDB[:, :], CS[:, 768:1280])
        vcopy(MCB[:, :], CS[:, 1280:1792])
        k_k = vcopy(invf[:, :], CS[:, 1792:1793])
        PE.wait(k_k)
        SC.wait(k_k)
        G1, G2, GF, GM, GN, GE = (sm[:, 8 * i:8 * i + 8] for i in range(6))
        ADB = sm[:, 48:96]
        CW = sm[:, 96:120]
        CV = sm[:, 120:128]
        BF = sm[0:8, 128:129]

        def rms(src, toks, b):
            bank, free = take(b)
            for k in range(8):
                i, sq, sf = Tb.take()
                a = act(sq[:, :], src[:, k, :], ACT.Square, toks[k], sf)
                p = mm(bank[:, :], ones[:, :], sq[:, :], k == 0, k == 7, a, free, d1, last=True)
                Tb.free[i] = [p]
            i1, r, f1 = Tb.take()
            i2, q, f2 = Tb.take()
            v = ts(q[:, :], bank[:, :], 1.0 / 1024, EPS, ALU.mult, ALU.add, p, f2)
            pfree[b] = [v]
            v = recip(r[:, :], q[:, :], v, f1)
            Tb.free[i2] = [v]
            s = act(r[:, :], r[:, :], ACT.Sqrt, v)
            return i1, r, s

        def norm_split(src, toks, gain, shift, b, *more):
            i1, r, s = rms(src, toks, b)
            outt = []
            pend = None
            for k in range(8):
                i, t, f = Tb.take()
                v = stt(t[:, :], src[:, k, :], gain[:, k:k + 1], r[:, :], ALU.mult, ALU.mult, s, f, k_s, *more)
                if shift is not None:
                    v = ts(t[:, :], t[:, :], shift[:, k:k + 1], None, ALU.add, None, v)
                if pend:
                    pend()
                a = copy(XH[:, k, :], t[:, :], v)

                def pend(k=k, i=i, t=t, a=a):
                    w = tt(XL[:, k, :], t[:, :], XH[:, k, :].bitcast(F32), ALU.subtract, a)
                    Tb.free[i] = [w]
                    outt.append([a, w])
                last = v
            pend()
            Tb.free[i1] = [last]
            return outt

        xin_t = [k_x[k // 2] for k in range(8)]
        split_to(NW)
        xtok = norm_split(XIN, xin_t, G1, None, 0)

        CA = [at(f"CA{i}", F + 24 + 2 * i, [8, T], F32) for i in range(4)]
        CR = [at(f"CR{i}", F + 32 + 2 * i, [8, T], F32R) for i in range(8)]
        cd = nc.dram_tensor("cdram", [2, 4, 8, T], F32, kind="Internal").ap()
        t = feature_major(1, XH, XL, xtok)
        v = ts(CA[0][:, :], P[1][0:8, :], BF, None, ALU.add, None, t, k_s)
        pfree[1] = [v]
        v2 = stt(CA[1][:, :], CA[0][:, :], -1.0, CA[0][:, :], ALU.mult, ALU.min, v)
        a = act(CA[1][:, :], CA[1][:, :], ACT.Exp, v2)
        a = act(CA[2][:, :], CA[1][:, :], ACT.Ln, a, bias=1.0)
        v = stt(CA[3][:, :], CA[0][:, :], 0.0, CA[2][:, :], ALU.min, ALU.subtract, a)
        v0 = vset(CA[1][:, :], 1.0, a)
        v = DVE.do(lambda e: e.tensor_tensor_scan(CA[0][:, :], CA[1][:, :], CA[3][:, :], 0.0,
                                                  ALU.mult, ALU.add), v, v0)
        w0 = vcopy(CR[0][:, :], CA[0][:, :], v)
        w1 = tt(CR[1][:, :], CA[0][:, :], CR[0][:, :].bitcast(F32), ALU.subtract, w0)
        w2 = ts(CR[2][:, :], CR[0][:, :].bitcast(F32), -1.0, None, ALU.mult, None, w0)
        w3 = ts(CR[3][:, :], CR[1][:, :].bitcast(F32), -1.0, None, ALU.mult, None, w1)
        w = w3
        for i in range(4):
            w = vcopy(CR[4 + i][:, :], AD[:, i, :], k_ad)
        cd_tok = []
        for br in range(2):
            for i in range(4):
                cd_tok.append(dma(f"cd{4 * br + i}", cd[br, i], CR[4 * br + i][:, :].bitcast(F32), w3 if br == 0 else w))

        MH = at("MH", F + 16, [128, 8, T], F32R)
        ML = at("ML", F + 32, [128, 8, T], F32R)
        QH = at("QH", F + 48, [128, 4, T], F32R)
        QL = at("QL", F + 56, [128, 4, T], F32R)
        KH = at("KH", F + 64, [128, 4, T], F32R)
        KL = at("KL", F + 72, [128, 4, T], F32R)
        VH = at("VH", F + 80, [128, 4, T], F32R)
        VL = at("VL", F + 88, [128, 4, T], F32R)
        PTH = at("PTH", F, [128, 4, T], F32R)
        PTL = at("PTL", F + 8, [128, 4, T], F32R)
        z = []
        for X in (QL, KL, QH, KH):
            z.append(vset(X[64:128, :, :].bitcast(F32), 0.0, k_k))
        zo = []
        for X in (QH, KH):
            zo.append(vset(X[64:68, :, :].bitcast(F32), 1.0, z))
        head_tok = {"pt": [], "m": [], "qk": [], "v": []}
        mtok = [[] for _ in range(8)]
        for br in range(2):
            done = token_major([2, 3, 4, 5], XH, XL, xtok)
            vtok = []
            for tb in range(4):
                vtok.append(split(VH[:, tb, :], VL[:, tb, :], P[2 + tb][:, :], done[tb], head_tok["v"]))
                pfree[2 + tb] = vtok[-1]
            for g in range(2):
                qk = []
                for j in range(4):
                    H, L = (QH, QL) if j < 2 else (KH, KL)
                    b = j % 2
                    t = feature_major(b, XH, XL, xtok)
                    toks = []
                    for half in range(2):
                        hh = 2 * (j % 2) + half
                        toks += split(H[0:64, hh, :], L[0:64, hh, :], P[b][64 * half:64 * half + 64, :],
                                      t, head_tok["qk"], scale=0.125 if j < 2 else None)
                    pfree[b] = toks
                    qk += toks
                qk.append(dma("bq", QH[64:66, :, :].bitcast(F32), cd[br, 0:2, 4 * g:4 * g + 4, :], cd_tok, zo, head_tok["qk"]))
                qk.append(dma("bk", KH[66:68, :, :].bitcast(F32), cd[br, 2:4, 4 * g:4 * g + 4, :], cd_tok, zo, head_tok["qk"]))
                steps = [(h, qb) for h in range(4) for qb in range(4)]
                sb_banks = Banks([2, 3, 4])
                tr_banks = Banks([5, 6])
                S, E, N = {}, {}, {}

                def scores(n):
                    h, qb = steps[n]
                    kw = 128 * (qb + 1)
                    b, bank, free = sb_banks.next()
                    qs = slice(qb * 128, qb * 128 + 128)
                    PE.wait(free, qk, z)
                    mm(bank[:, 0:kw], QH[:, h, qs], KH[:, h, 0:kw], True, False)
                    mm(bank[:, 0:kw], QH[:, h, qs], KL[:, h, 0:kw], False, False)
                    mm(bank[:, 0:kw], QL[:, h, qs], KH[:, h, 0:kw], False, False)
                    mask = MCB if br == 0 else MDB
                    t = mm(bank[:, 0:kw], identb[:, :], mask[:, (3 - qb) * 128:T], False, True, last=True)
                    S[n] = (b, t)
                    return t

                def soft(n):
                    h, qb = steps[n]
                    kw = 128 * (qb + 1)
                    b, t = S[n]
                    c = 4 * (n % 4)
                    m = reduce(st[:, c:c + 1], P[b][:, 0:kw], ALU.max, t)
                    m = ts(st[:, c + 1:c + 2], st[:, c:c + 1], -1.0, None, ALU.mult, None, m)
                    i, pbuf, pf = Tb.take()
                    if br == 0:
                        a = SC.do(lambda e: e.activation(pbuf[:, 0:kw], P[b][:, 0:kw], ACT.Exp,
                                                         bias=st[:, c + 1:c + 2],
                                                         accum_out=st[:, c + 2:c + 3]), m, pf)
                    else:
                        a = SC.do(lambda e: e.activation(pbuf[:, 0:kw], P[b][:, 0:kw], ACT.Exp,
                                                         bias=st[:, c + 1:c + 2]), m, pf)
                    pfree[b] = [m, a]
                    E[n] = (i, pbuf, a)

                def normal(n):
                    h, qb = steps[n]
                    kw = 128 * (qb + 1)
                    i, pbuf, a = E[n]
                    c = 4 * (n % 4)
                    if br == 1:
                        a = DVE.do(lambda e: e.tensor_tensor_reduce(
                            out=pbuf[:, 0:kw], in0=pbuf[:, 0:kw], in1=CNT[:, (3 - qb) * 128:T], scale=1.0,
                            scalar=0.0, op0=ALU.mult, op1=ALU.add, accum_out=st[:, c + 2:c + 3]), a)
                    v = recip(st[:, c + 3:c + 4], st[:, c + 2:c + 3], a)
                    v = ts(pbuf[:, 0:kw], pbuf[:, 0:kw], st[:, c + 3:c + 4], None, ALU.mult, None, v)
                    N[n] = (i, pbuf, v)

                def turn(n):
                    h, qb = steps[n]
                    i, pbuf, v = N[n]
                    b, bank, free = tr_banks.next()
                    for kb in range(qb + 1):
                        t = turned(bank[:, kb * 128:kb * 128 + 128], pbuf[:, kb * 128:kb * 128 + 128], v, free)
                    Tb.free[i] = [t]
                    qs = slice(qb * 128, qb * 128 + 128)
                    src = bank[:, 0:128 * (qb + 1)].rearrange("p (k q) -> p k q", q=128)
                    pt = split(PTH[:, 0:qb + 1, qs], PTL[:, 0:qb + 1, qs], src, t, head_tok["pt"])
                    pfree[b] = pt
                    if qb == 3:
                        return pt

                def values(n, pt):
                    h, _ = steps[n]
                    hg = 4 * g + h
                    cs = slice(128 * (hg // 2), 128 * (hg // 2) + 128)
                    bank, free = take(7)
                    PE.wait(free, pt, vtok)
                    for kb in range(4):
                        d = bank[:, kb * 128:T]
                        r = slice(kb * 128, T)
                        mm(d, VH[:, kb, cs], PTH[:, kb, r], kb == 0, False)
                        mm(d, VH[:, kb, cs], PTL[:, kb, r], False, False)
                        t = mm(d, VL[:, kb, cs], PTH[:, kb, r], False, kb == 3, last=kb == 3)
                    head_tok["pt"] = [t]
                    rows = slice(64 * (hg % 2), 64 * (hg % 2) + 64)
                    mt = 4 * br + hg // 2
                    s = split(MH[rows, mt, :], ML[rows, mt, :], bank[rows, :], t, cd_tok)
                    mtok[mt] += s
                    pfree[7] = s
                    return t

                ns = len(steps)
                for n in range(ns + 4):
                    if n < ns:
                        qk_last = scores(n)
                    if 0 <= n - 1 < ns:
                        soft(n - 1)
                    if 0 <= n - 2 < ns:
                        normal(n - 2)
                    if 0 <= n - 3 < ns:
                        pt = turn(n - 3)
                        if pt:
                            v_last = values(n - 3, pt)
                head_tok["qk"] = [qk_last]
                head_tok["v"] = [v_last]

        hT = at("hT", F, [128, 8, T], F32)
        hx = [dma(f"x{j}", hT[:, 2 * j:2 * j + 2, :], xt[:, 2 * j:2 * j + 2, :], head_tok["pt"], mtok) for j in range(4)]
        htok = []
        for m in range(8):
            t = feature_major(m % 4, MH, ML, mtok)
            v = tt(hT[:, m, :], P[m % 4][:, :], hT[:, m, :], ALU.add, t, hx[m // 2])
            pfree[m % 4] = [v]
            htok.append([v])
        everyone()
        for b in range(8):
            pfree[b] = []
        xtok = norm_split(hT, htok, G2, None, 4)

        S = at("S", F + 16, [128, 16, 4, 128], F32)
        VAL = at("VAL", F + 48, [128, 4, 16, 16], F32)
        IDX = at("IDX", F + 52, [128, 4, 16, 16], U32)
        CSV = at("CSV", F + 56, [128, 4, 8, 16], F32)
        CIX = at("CIX", F + 58, [128, 4, 8, 16], U32)
        D1 = at("D1", F + 60, [128, 1024], F32)
        D2 = at("D2", F + 64, [128, 1024], F32)
        SKR = at("SKR", F + 68, [128, 2048], F32)
        SKH = at("SKH", F + 76, [128, 2048], F32R)
        SKL = at("SKL", F + 84, [128, 2048], F32R)
        QPH = [at(f"QPH{i}", F + 92 + 4 * i, [128, T], F32R) for i in range(2)]
        QPL = [at(f"QPL{i}", F + 94 + 4 * i, [128, T], F32R) for i in range(2)]
        k_sk = dma("c0", SKR[:, :], skt)
        sk = split(SKH[:, 0:1024], SKL[:, 0:1024], SKR[:, 0:1024], k_sk)
        sk += split(SKH[:, 1024:2048], SKL[:, 1024:2048], SKR[:, 1024:2048], k_sk)
        qfree = [[], []]
        stok = {}

        def key_scores(hp, qt):
            bank, free = take(4 + hp % 2)
            PE.wait(free, qt, sk)
            ks = slice(hp * 128, hp * 128 + 128)
            for tb in range(4):
                d = bank[:, tb * 128:tb * 128 + 128]
                q = slice(tb * 128, tb * 128 + 128)
                mm(d, QPH[hp % 2][:, q], SKH[:, ks], True, False)
                mm(d, QPH[hp % 2][:, q], SKL[:, ks], False, False)
                t = mm(d, QPL[hp % 2][:, q], SKH[:, ks], False, True, last=tb == 3)
            qfree[hp % 2] = [t]
            a = copy(S[:, hp, :, :], bank[:, :].rearrange("p (b k) -> p b k", b=4), t)
            pfree[4 + hp % 2] = [a]
            stok[hp] = a

        toptok = {}

        def top16(src, val, idx, tok):
            a = DVE.do(lambda e: e.max(val[:, 0:8], src), tok)
            b = DVE.do(lambda e: e.max_index(idx[:, 0:8], val[:, 0:8], src), a)
            c = DVE.do(lambda e: e.match_replace(src, val[:, 0:8], src, LOWEST), b)
            d = DVE.do(lambda e: e.max(val[:, 8:16], src), c)
            return DVE.do(lambda e: e.max_index(idx[:, 8:16], val[:, 8:16], src), d)

        def route():
            for hp in range(16):
                for tb in range(4):
                    toptok[hp, tb] = top16(S[:, hp, tb, :], VAL[:, tb, hp, :], IDX[:, tb, hp, :], stok[hp])
                    yield 1.0
            for tb in range(4):
                for h in range(8):
                    i, c, f = Tb.take()
                    c = c[:, 0:256]
                    v1 = VAL[:, tb, 2 * h, :].unsqueeze(2).to_broadcast([128, 16, 16])
                    v2 = VAL[:, tb, 2 * h + 1, :].unsqueeze(1).to_broadcast([128, 16, 16])
                    t = tt(c.rearrange("p (a b) -> p a b", a=16), v1, v2, ALU.add,
                           toptok[2 * h, tb], toptok[2 * h + 1, tb], f)
                    t = top16(c, CSV[:, tb, h, :], CIX[:, tb, h, :], t)
                    Tb.free[i] = [t]
                    toptok["c", tb, h] = t
                    yield 2.0

        GR = at("GR", F + 68, [128, 4, 128], F32)
        U1 = at("U1", F + 70, [128, 128], U32)
        AF = at("AF", F + 70.5, [128, 128], F32)
        IF = at("IF", F + 71, [128, 8, 16], F32)
        IS = at("IS", F + 71.5, [128, 2, 128], F32)
        I1T = at("I1T", F + 72.5, [128, T], F32)
        I2T = at("I2T", F + 74.5, [128, T], F32)
        GTH = at("GTH", F + 76.5, [128, T], F32R)
        GTL = at("GTL", F + 78.5, [128, T], F32R)
        OA = [at(f"OA{i}", F + 80.5 + 4 * i, [128, 2, 4, 128], F32R) for i in range(2)]
        OB = [at(f"OB{i}", F + 88.5 + 2 * i, [128, 4, 128], F32R) for i in range(2)]
        HID = Slots([at(f"HID{i}", F + 92.5 + 4 * i, [128, 2, T], F32) for i in range(2)])
        GS = [at(f"GS{i}", F + 16 + 16 * i, [128, 128, 32], F32) for i in range(2)]
        dg = nc.dram_tensor("gdram", [16, 128, 128, 32], F32, kind="Internal").ap()
        dh = nc.dram_tensor("hdram", [32, 128, 4, T], F32, kind="Internal").ap()
        dg_tok, dh_tok = [], {}

        def gates():
            ittok = []
            for tb in range(4):
                c = CSV[:, tb, :, :]
                gr = GR[:, tb, :].rearrange("p (h k) -> p h k", h=8)
                tops = [toptok["c", tb, h] for h in range(8)]
                v = tt(gr, c, CSV[:, tb, :, 0:1].to_broadcast([128, 8, 16]), ALU.subtract, tops)
                a = act(gr, gr, ACT.Exp, v)
                v = reduce(st[:, 32:40], gr, ALU.add, a)
                v = recip(st[:, 40:48], st[:, 32:40], v)
                vg = tt(gr, gr, st[:, 40:48].unsqueeze(2).to_broadcast([128, 8, 16]), ALU.mult, v)
                yield 1.0
                fin = []
                for p in range(2):
                    ci = CIX[:, tb, :, :].rearrange("p h k -> p (h k)")
                    if p == 0:
                        v = ts(U1[:, :], ci, 4, None, ALU.logical_shift_right, None)
                    else:
                        v = ts(U1[:, :], ci, 15, None, ALU.bitwise_and, None, v)
                    v1 = vcopy(AF[:, :], U1[:, :], v)
                    idv = IDX[:, tb, :, :].rearrange("p (h q) a -> p h q a", q=2)[:, :, p, :]
                    v2 = vcopy(IF[:, :, :], idv)
                    for hh in range(2):
                        d1v = D1[:, :].rearrange("p (s a) -> p s a", a=16)
                        v = tt(d1v, AF[:, 64 * hh:64 * hh + 64].unsqueeze(2).to_broadcast([128, 64, 16]),
                               iota[:, 0:16].unsqueeze(1).to_broadcast([128, 64, 16]), ALU.is_equal, v1)
                        d1q = D1[:, :].rearrange("p (h k a) -> p h k a", h=4, a=16)
                        d2q = D2[:, :].rearrange("p (h k a) -> p h k a", h=4, a=16)
                        v = tt(d2q, d1q, IF[:, 4 * hh:4 * hh + 4, :].unsqueeze(2).to_broadcast([128, 4, 16, 16]),
                               ALU.mult, v, v2)
                        v = reduce(IS[:, p, 64 * hh:64 * hh + 64],
                                   D2[:, :].rearrange("p (s a) -> p s a", a=16), ALU.add, v)
                        yield 3.3
                    fin.append(v)
                bank, free = take(6)
                t = None
                for n, s in enumerate((IS[:, 0, :], IS[:, 1, :], GR[:, tb, :])):
                    t = turned(bank[:, n * 128:n * 128 + 128], s, fin, vg, free)
                q = slice(tb * 128, tb * 128 + 128)
                a1 = copy(I1T[:, q], bank[:, 0:128], t)
                a2 = copy(I2T[:, q], bank[:, 128:256], t)
                a3 = copy(GTH[:, q], bank[:, 256:384], t)
                v = tt(GTL[:, q], bank[:, 256:384], GTH[:, q].bitcast(F32), ALU.subtract, a3)
                pfree[6] = [a3, v]
                DVE.wait(t)
                ittok.append([a1, a2, a3, v])
                yield 0.3
            oa_free, ob_free = [[], []], [[], []]
            gs_free = [[], []]
            sdone = toptok["c", 3, 7]
            for n in range(128):
                s = n % 2
                tb = n // 32
                for j in range(4):
                    t = 4 * n + j
                    for half, g in enumerate((GTH, GTL)):
                        va = DVE.do(lambda e, t=t, j=j, half=half, g=g, s=s: e.tensor_scalar(
                            OA[s][:, half, j, :], iota[:, :], I1T[:, t:t + 1], g[:, t:t + 1].bitcast(F32),
                            ALU.is_equal, ALU.mult), ittok[tb], oa_free[s])
                    vb = GP.do(lambda e, t=t, j=j, s=s: e.tensor_scalar(
                        OB[s][:, j, :], iota[:, :], I2T[:, t:t + 1], None, ALU.is_equal), ittok[tb], ob_free[s])
                b = 6 + n % 2
                bank, free = take(b)
                PE.wait(va, vb, free)
                for j in range(4):
                    d = bank[:, j * 128:j * 128 + 128]
                    mm(d, OA[s][:, 0, j, :], OB[s][:, j, :], True, False)
                    tk = mm(d, OA[s][:, 1, j, :], OB[s][:, j, :], False, True, last=j == 3)
                oa_free[s], ob_free[s] = [tk], [tk]
                g, o = n // 8, 4 * (n % 8)
                dst = GS[g % 2][:, :, o:o + 4].rearrange("p i t -> p t i")
                a = copy(dst, bank[:, :].rearrange("p (t i) -> p t i", t=4), tk, gs_free[g % 2], sdone)
                pfree[b] = [a]
                if n % 8 == 7:
                    tk = dma(f"g{g % 2}", dg[g], GS[g % 2][:, :, :], a)
                    gs_free[g % 2] = [tk]
                    dg_tok.append(tk)
                yield 1.2

        bg = route()
        for hp in range(16):
            b = hp % 2
            t = feature_major(b, XH, XL, xtok)
            qt = split(QPH[b][:, :], QPL[b][:, :], P[b][:, :], t, qfree[b])
            pfree[b] = qt
            key_scores(hp, qt)
            for _ in range(4 if hp else 0):
                next(bg)

        def background():
            yield from bg
            DVE.wait((PE.sem, PE.n))
            yield from gates()

        wq_end = [(PE.sem, PE.n), (DVE.sem, DVE.n), (SC.sem, SC.n)]
        for q in (PE, DVE, SC, GP):
            q.wait(wq_end)
        work = background()
        spare = 0.0
        hb = Banks([0, 1, 2, 3])
        for i2 in range(128):
            b, bank, free = hb.next()
            cur = next_unit()
            t = unit_mms(bank, XH, XL, xtok, free)
            if i2 % 2 == 0:
                hi, hbuf, hf = HID.take()
            a = act(hbuf[:, i2 % 2, :], bank[:, :], ACT.Gelu, t, hf)
            pfree[b] = [a]
            if i2 % 2 == 1:
                tk = dma(f"h{hi}", dh[i2 // 4, :, 2 * (i2 // 2 % 2):2 * (i2 // 2 % 2) + 2, :], hbuf[:, :, :], a)
                HID.free[hi] = [tk]
                dh_tok[i2 // 2] = tk
            spare += 2.9
            while spare > 0:
                c = next(work, None)
                if c is None:
                    break
                spare -= c
        for _ in work:
            pass

        everyone()
        for b in range(8):
            pfree[b] = []
        GI = [at(f"GI{i}", F + 16 + 8 * i, [128, 16, 128], F32) for i in range(2)]
        HI = [at(f"HI{i}", F + 32 + 8 * i, [128, 4, T], F32) for i in range(2)]
        AH = [at(f"AH{i}", F + 48 + 2 * i, [128, T], F32R) for i in range(3)]
        AL = [at(f"AL{i}", F + 54 + 2 * i, [128, T], F32R) for i in range(3)]
        ACC = at("ACC", 60, [128, 6144], F32)
        AW = [at(f"AW{i}", 84 + 4 * i, [128, 1024], F32) for i in range(2)]
        gi_free = [[], []]
        gi_tok = {}

        def fetch(g):
            s = g % 2
            gi_tok[g] = [
                dma(f"gi{s}", GI[s][:, :, :], dg[:, :, 4 * g:4 * g + 4, :].rearrange("g p i t -> p g (i t)"),
                    gi_free[s], dg_tok),
                dma(f"hi{s}", HI[s][:, :, :], dh[g], gi_free[s], dh_tok[2 * g], dh_tok[2 * g + 1])]

        acc_tok = {}
        k_cs = act(csil[:, :], CV, ACT.Silu, k_s)

        def modulation():
            aw_free = [[], []]
            for k in range(8):
                for c in range(6):
                    s = c % 2
                    w = dma(f"aw{s}", AW[s][:, :], adaw[k, :, 1024 * c:1024 * c + 1024], aw_free[s])
                    dst = ACC[:, 1024 * c:1024 * c + 1024]
                    if k == 0:
                        v = ts(dst, AW[s][:, :], csil[:, 0:1], None, ALU.mult, None, w, k_cs)
                    else:
                        v = stt(dst, AW[s][:, :], csil[:, k:k + 1], dst, ALU.mult, ALU.add, w, acc_tok[c])
                    aw_free[s] = [v]
                    acc_tok[c] = v
                    yield

        a_free = [[], [], []]
        mods = modulation()
        a_ready = {}

        def activate(i2):
            g, j = divmod(i2, 4)
            if j == 0 and g + 1 < 32:
                fetch(g + 1)
            i, t, f = Tb.take()
            gv = GI[g % 2][:, :, 32 * j:32 * j + 32]
            v = tt(t[:, :].rearrange("p (g t) -> p g t", g=16),
                   HI[g % 2][:, j, :].rearrange("p (g t) -> p g t", g=16), gv, ALU.mult, gi_tok[g], f)
            if j == 3:
                gi_free[g % 2] = [v]
            r = split(AH[i2 % 3][:, :], AL[i2 % 3][:, :], t[:, :], v, a_free[i2 % 3])
            Tb.free[i] = r
            a_ready[i2] = r

        fetch(0)
        activate(0)
        activate(1)
        for i2 in range(128):
            i, wh, wl = next_unit()
            s = i2 % 3
            PE.wait(a_ready[i2])
            for d in range(8):
                w = slice(d * 128, d * 128 + 128)
                mm(P[d][:, :], wh[:, w], AH[s][:, :], i2 == 0, False)
                mm(P[d][:, :], wh[:, w], AL[s][:, :], False, False)
                t = mm(P[d][:, :], wl[:, w], AH[s][:, :], False, i2 == 127, last=(d == 7 or i2 == 127))
                if i2 == 127:
                    if d == 0:
                        ydone = []
                    ydone.append(t)
            used_tok[i] = t
            a_free[s] = [t]
            if i2 + 2 < 128:
                activate(i2 + 2)
            if i2 % 5 in (0, 2):
                next(mods, None)
        for _ in mods:
            pass
        htok = []
        for d in range(8):
            v = tt(hT[:, d, :], P[d][:, :], hT[:, d, :], ALU.add, ydone[d])
            pfree[d] = [v]
            htok.append([v])
        bank, free = take(7)
        PE.wait(free)
        for n in range(48):
            t = mm(bank[:, n:n + 1], ACC[:, n * 128:n * 128 + 128], ones[:, 0:1], True, True,
                   acc_tok[n // 8], last=n == 47)
        v = tt(mod[:, :], bank[:, 0:48], ADB, ALU.add, t)
        pfree[7] = [v]
        v = ts(gmod[:, 0:8], mod[:, 8:16], 1.0, None, ALU.add, None, v)
        v = tt(gmod[:, 0:8], gmod[:, 0:8], GM, ALU.mult, v)
        v = ts(gmod[:, 8:16], mod[:, 32:40], 1.0, None, ALU.add, None, v)
        k_mod = tt(gmod[:, 8:16], gmod[:, 8:16], GN, ALU.mult, v)
        SH_M, GT_M, SH_F, GT_F = mod[:, 0:8], mod[:, 16:24], mod[:, 24:32], mod[:, 40:48]

        everyone()
        i1, r, s = rms(hT, htok, 0)
        for k in range(8):
            v = stt(hT[:, k, :], hT[:, k, :], GF[:, k:k + 1], r[:, :], ALU.mult, ALU.mult, s)
            htok[k] = [v]
        Tb.free[i1] = [v]
        xtok = norm_split(hT, htok, gmod[:, 0:8], SH_M, 1, k_mod)

        VRH = at("VRH", F + 16, [128, 4, T], F32R)
        VRL = at("VRL", F + 24, [128, 4, T], F32R)
        RH = at("RH", F + 32, [128, 8, T], F32R)
        RL = at("RL", F + 48, [128, 8, T], F32R)
        QR = [[at(f"QR{i}{j}", F + 64 + 8 * i + 2 * j, [128, T], F32R) for j in range(4)] for i in range(2)]
        offs = [0, 512, 896, 1152, 1280]
        SRH = at("SRH", F + 80, [128, 1280], F32R)
        SRL = at("SRL", F + 85, [128, 1280], F32R)
        COS = at("COS", F + 90, [128, T], F32)
        SIN = at("SIN", F + 92, [128, T], F32)
        DM = [at(f"DM{i}", F + 94 + 2 * i, [128, T], F32) for i in range(2)]
        PI = at("PI", F + 98, [128, T], I32)
        k_p = dma("c0", PI[:, :], pos.partition_broadcast(128))
        ia, ang, fa = Tb.take()
        ib, qn, fb = Tb.take()
        v = vcopy(ang[:, :], PI[:, :], k_p, fa)
        v = ts(ang[:, :], ang[:, :], invf[:, 0:1], None, ALU.mult, None, v)
        for dst, shift in ((SIN, 0.0), (COS, 0.25)):
            v = ts(qn[:, :], ang[:, :], float(1.0 / (2 * np.pi)), shift, ALU.mult, ALU.add, v, fb)
            v = ts(qn[:, :], qn[:, :], 12582912.0, None, ALU.add, None, v)
            v = ts(qn[:, :], qn[:, :], -12582912.0, None, ALU.add, None, v)
            v = stt(dst[:, :], qn[:, :], -6.28125, ang[:, :], ALU.mult, ALU.add, v)
            v = stt(dst[:, :], qn[:, :], -float(np.float32(0.0019350051879882812)), dst[:, :], ALU.mult, ALU.add, v)
            rest = 2 * np.pi - 6.28125 - 0.0019350051879882812
            v = stt(dst[:, :], qn[:, :], -float(rest), dst[:, :], ALU.mult, ALU.add, v)
            if shift:
                v = ts(dst[:, :], dst[:, :], float(np.pi / 2), None, ALU.add, None, v)
            v = ts(dst[:, :], dst[:, :], float(np.float32(3.1415925)), float(np.float32(-3.1415925)),
                   ALU.min, ALU.max, v)
            a = act(dst[:, :], dst[:, :], ACT.Sin, v)
        k_cos = a
        k_sin = ts(SIN[64:128, :], SIN[64:128, :], -1.0, None, ALU.mult, None, a)
        Tb.free[ia] = [v]
        Tb.free[ib] = [v]

        qr_free = [[], []]
        dm_free = [[], []]
        sr_free = []
        vr_free = []
        rtok = [[] for _ in range(8)]
        heads = {}

        def rope(b, H, L, t, free):
            i, u, f = Tb.take()
            j, w, f2 = Tb.take()
            v1 = tt(u[:, :], P[b][:, :], COS[:, :], ALU.mult, t, f, k_cos)
            v2 = tt(w[0:64, :], P[b][64:128, :], SIN[64:128, :], ALU.mult, f2, k_sin)
            v3 = tt(w[64:128, :], P[b][0:64, :], SIN[0:64, :], ALU.mult)
            pfree[b] = [v3]
            v = tt(u[:, :], u[:, :], w[:, :], ALU.add, v1, v2, v3)
            Tb.free[j] = [v]
            r = split(H[:, :], L[:, :], u[:, :], v, free)
            Tb.free[i] = r
            return r

        def project(h):
            q = QR[h % 2]
            t = feature_major(0, XH, XL, xtok)
            rq = rope(0, q[0], q[1], t, qr_free[h % 2])
            t = feature_major(1, XH, XL, xtok)
            rk = rope(1, q[2], q[3], t, qr_free[h % 2])
            t = feature_major(0, XH, XL, xtok)
            i, sg, f = Tb.take()
            a = act(sg[:, :], P[0][:, :], ACT.Silu, t, f)
            pfree[0] = [a]
            kd = dma(f"dm{h % 2}", DM[h % 2][:, :], dmat[:, T * h:T * h + T], dm_free[h % 2])
            heads[h] = (rq + rk, i, sg, a, kd)

        def retain(h):
            nonlocal sr_free, vr_free
            qk, gi, sg, ga, kd = heads[h]
            q = QR[h % 2]
            pts = []
            for kb in range(4):
                n = T - 128 * kb
                b = 2 + kb % 2
                bank, free = take(b)
                ks = slice(128 * kb, 128 * kb + 128)
                mm(bank[:, 0:n], q[2][:, ks], q[0][:, 128 * kb:T], True, False, free, qk)
                mm(bank[:, 0:n], q[2][:, ks], q[1][:, 128 * kb:T], False, False)
                t = mm(bank[:, 0:n], q[3][:, ks], q[0][:, 128 * kb:T], False, True, last=True)
                i, u, f = Tb.take()
                v = tt(u[:, 0:n], bank[:, 0:n], DM[h % 2][:, 0:n], ALU.mult, t, f, kd)
                pfree[b] = [v]
                s = slice(offs[kb], offs[kb + 1])
                r = split(SRH[:, s], SRL[:, s], u[:, 0:n], v, sr_free)
                Tb.free[i] = r
                pts.append(r)
            qr_free[h % 2] = [t]
            dm_free[h % 2] = [v]
            bank, free = take(4)
            PE.wait(free)
            cs = slice(128 * (h % 4), 128 * (h % 4) + 128)
            for kb in range(4):
                d = bank[:, 128 * kb:T]
                s = slice(offs[kb], offs[kb + 1])
                mm(d, VRH[:, kb, cs], SRH[:, s], kb == 0, False, pts[kb], vtok)
                mm(d, VRH[:, kb, cs], SRL[:, s], False, False)
                t = mm(d, VRL[:, kb, cs], SRH[:, s], False, kb == 3, last=kb == 3)
            sr_free = [t]
            vr_free = [t]
            i, y, f = Tb.take()
            a = copy(y[:, :], bank[:, :], t, f)
            pfree[4] = [a]
            heads[h] = (i, y, a, gi, sg, ga)

        def layernorm(h):
            i, y, a, gi, sg, ga = heads[h]
            bank, free = take(5)
            t = mm(bank[:, :], ones[:, :], y[:, :], True, True, a, free, last=True)
            v = stt(y[:, :], bank[:, :], -1.0 / 128, y[:, :], ALU.mult, ALU.add, t)
            pfree[5] = [v]
            j, q, f = Tb.take()
            a = act(q[:, :], y[:, :], ACT.Square, v, f)
            bank, free = take(6)
            t = mm(bank[:, :], ones[:, :], q[:, :], True, True, a, free, last=True)
            v2 = ts(q[:, :], bank[:, :], 1.0 / 128, EPS, ALU.mult, ALU.add, t)
            pfree[6] = [v2]
            v2 = recip(q[:, :], q[:, :], v2)
            a = act(q[:, :], q[:, :], ACT.Sqrt, v2)
            v = tt(y[:, :], y[:, :], sg[:, :], ALU.mult, v, ga)
            Tb.free[gi] = [v]
            v = tt(y[:, :], y[:, :], q[:, :], ALU.mult, v, a)
            Tb.free[j] = [v]
            r = split(RH[:, h, :], RL[:, h, :], y[:, :], v)
            Tb.free[i] = r
            rtok[h] = r

        for half in range(2):
            done = token_major([4, 5, 6, 7], XH, XL, xtok)
            vtok = []
            for tb in range(4):
                vtok.append(split(VRH[:, tb, :], VRL[:, tb, :], P[4 + tb][:, :], done[tb], vr_free))
                pfree[4 + tb] = vtok[-1]
            for n in range(6):
                h = 4 * half + n
                if n < 4:
                    project(h)
                if 1 <= n < 5:
                    retain(h - 1)
                if n >= 2:
                    layernorm(h - 2)

        MG = at("MG", F + 64, [128, 8, T], F32)
        U = [at(f"UC{i}", F + 80 + 3 * i, [128, 516], F32) for i in range(2)]
        over = [(PE.sem, PE.n), (DVE.sem, DVE.n), (SC.sem, SC.n)]
        DVE.wait(over)
        SC.wait(over)
        uz = [vset(U[i][:, 0:2], 0.0) for i in range(2)]
        mgt = [None] * 8

        def gated(m, H, L, toks, first):
            b = 2 * (m % 2)
            t = feature_major(b, XH, XL, xtok)
            i, sg, f = Tb.take()
            a = act(sg[:, :], P[b][:, :], ACT.Sigmoid, t, f)
            pfree[b] = [a]
            t = feature_major(b + 1, H, L, toks)
            if first:
                v = tt(MG[:, m, :], P[b + 1][:, :], sg[:, :], ALU.mult, t, a)
                mgt[m] = v
            else:
                v = tt(sg[:, :], P[b + 1][:, :], sg[:, :], ALU.mult, t, a)
                v = tt(MG[:, m, :], MG[:, m, :], sg[:, :], ALU.add, v, mgt[m])
                mgt[m] = v
            pfree[b + 1] = [v]
            Tb.free[i] = [v]

        for m in range(8):
            gated(m, RH, RL, rtok, True)
        r_read = [(PE.sem, PE.n)]
        ctok = []
        uf = [[], []]
        for m in range(8):
            o = 3 * (m % 2)
            tb_ = feature_major(o, XH, XL, xtok)
            tc = feature_major(o + 1, XH, XL, xtok)
            i, c, f = Tb.take()
            a = copy(c[:, :], P[o + 1][:, :], tc, f)
            pfree[o + 1] = [a]
            tu = feature_major(o + 2, XH, XL, xtok)
            u = U[m % 2]
            v = tt(u[:, 2:514], P[o + 2][:, :], c[:, :], ALU.mult, tu, a, uf[m % 2], uz)
            pfree[o + 2] = [v]
            v = ts(c[:, :], u[:, 0:512], CW[:, m:m + 1], None, ALU.mult, None, v)
            v = stt(c[:, :], u[:, 1:513], CW[:, 8 + m:9 + m], c[:, :], ALU.mult, ALU.add, v)
            v = stt(c[:, :], u[:, 2:514], CW[:, 16 + m:17 + m], c[:, :], ALU.mult, ALU.add, v)
            uf[m % 2] = [v]
            v = tt(c[:, :], P[o][:, :], c[:, :], ALU.mult, v, tb_)
            pfree[o] = [v]
            r = split(RH[:, m, :], RL[:, m, :], c[:, :], v, r_read)
            Tb.free[i] = r
            ctok.append(r)
        for m in range(8):
            gated(m, RH, RL, ctok, False)
        x_read = [(PE.sem, PE.n)]
        gtok = [split(XH[:, m, :], XL[:, m, :], MG[:, m, :], mgt[m], x_read) for m in range(8)]
        htok2 = []
        for m in range(8):
            t = feature_major(m % 4, XH, XL, gtok)
            v = stt(hT[:, m, :], P[m % 4][:, :], GT_M[:, m:m + 1], hT[:, m, :], ALU.mult, ALU.add, t)
            pfree[m % 4] = [v]
            htok2.append([v])

        everyone()
        xtok = norm_split(hT, htok2, gmod[:, 8:16], SH_F, 4)
        FH = at("FH", F + 16, [128, 11, T], F32R)
        FL = at("FL", F + 38, [128, 11, T], F32R)
        NF = 22
        FHb = at("FHb", F + 60, [128, 11, T], F32R)
        FLb = [at(f"FLb{i}", F + 82 + 2 * i, [128, 1, T], F32R) for i in range(9)]
        ftok = []

        def fpart(k):
            if k < 11:
                return FH[:, k, :], FL[:, k, :]
            if k - 11 < 9:
                return FHb[:, k - 11, :], FLb[k - 11][:, 0, :]
            return FHb[:, k - 11, :], tail[k - 20]

        tail = []
        for _ in range(2):
            i, t_, f = Tb.take()
            tail.append((i, f))
        tl = [at(f"TL{n}", 92 + 2 * i, [128, T], F32R) for n, (i, f) in enumerate(tail)]
        tl_free = [f for _, f in tail]
        keep = sorted(i for i, _ in tail)
        rest = [i for i in range(7) if i not in keep]
        sub = Slots([Tb.bufs[i] for i in rest])
        sub.free = [Tb.free[i] for i in rest]
        tail = [tl[0][:, :], tl[1][:, :]]
        for m in range(NF):
            b = 2 * (m % 2)
            t = feature_major(b, XH, XL, xtok)
            i, g_, f = sub.take()
            a = act(g_[:, :], P[b][:, :], ACT.Silu, t, f)
            pfree[b] = [a]
            t = feature_major(b + 1, XH, XL, xtok)
            v = tt(g_[:, :], P[b + 1][:, :], g_[:, :], ALU.mult, t, a)
            pfree[b + 1] = [v]
            H, L = fpart(m)
            r = split(H, L, g_[:, :], v, tl_free)
            sub.free[i] = r
            ftok.append(r)
        n = 0
        htok = []
        for m in range(8):
            bank, free = take(m % 4)
            PE.wait(free)
            for k in range(NF):
                if n % 8 == 0:
                    cur = next_unit()
                i, wh, wl = cur
                w = slice((n % 8) * 128, (n % 8) * 128 + 128)
                H, L = fpart(k)
                PE.wait(ftok[k])
                mm(bank[:, :], wh[:, w], H, k == 0, False)
                mm(bank[:, :], wh[:, w], L, False, False)
                end = n % 8 == 7 or k == NF - 1
                t = mm(bank[:, :], wl[:, w], H, False, k == NF - 1, last=end)
                if n % 8 == 7:
                    used_tok[i] = t
                n += 1
            v = stt(hT[:, m, :], bank[:, :], GT_F[:, m:m + 1], hT[:, m, :], ALU.mult, ALU.add, t)
            pfree[m % 4] = [v]
            htok.append([v])

        everyone()
        i1, r, s = rms(hT, htok, 5)
        ot = out.rearrange("(k p) t -> p k t", p=128)
        last = []
        for k in range(8):
            v = stt(hT[:, k, :], hT[:, k, :], GE[:, k:k + 1], r[:, :], ALU.mult, ALU.mult, s)
            last.append(dma(f"o{k % 4}", ot[:, k, :], hT[:, k, :], v))
        SP.wait(last)

        block = ctx.enter_context(nc.Block())

        @block.sync
        def _(e):
            SP.play(e)

        @block.tensor
        def _(e):
            PE.play(e)

        @block.vector
        def _(e):
            DVE.play(e)

        @block.scalar
        def _(e):
            SC.play(e)

        @block.gpsimd
        def _(e):
            GP.play(e)


def feature_units(w):
    k, n = w.shape
    return w.reshape(k // 128, 128, n // 128, 128).transpose(2, 1, 0, 3).reshape(n // 128, 128, k)


def token_units(w):
    return w.reshape(4, 2, 128, 512).transpose(0, 2, 1, 3).reshape(4, 128, 1024)


def columns(g):
    return g.reshape(-1, 128).T


def constants():
    i = np.arange(128)[:, None]
    j = np.arange(512)[None, :]
    d = i + 384 - j
    count = ((d >= 0) & (d <= 128)).astype(np.float32)
    count += (d >= 0) & (d % 4 == 0)
    count += (d >= 0) & (d % 16 == 0)
    c = np.zeros((128, 1793), np.float32)
    c[:, 0:128] = np.eye(128)
    c[:, 128:256] = np.arange(128)[None, :]
    c[:, 256:768] = count
    c[:, 768:1280] = np.where(count > 0, 0.0, NEG)
    c[:, 1280:1792] = np.where(d >= 0, 0.0, NEG)
    inv = 1.0 / (np.float32(10000.0) ** (np.arange(0, 128, 2, dtype=np.float32) / np.float32(128)))
    c[:, 1792] = np.concatenate([inv, inv])
    lg = np.log(1.0 - 2.0 ** (-5.0 - np.arange(8)))
    rel = np.arange(512)[None, :] - np.arange(128)[:, None]
    dm = np.where(rel[None] >= 0, np.exp(lg[:, None, None] * np.maximum(rel, 0)[None]), 0.0) * 128 ** -0.5
    dm = dm.transpose(1, 0, 2).reshape(128, 8 * 512).astype(np.float32)
    slope = 2.0 ** -np.arange(1, 9, dtype=np.float32)[:, None]
    t = np.arange(512, dtype=np.float32)[None, :]
    aug = np.stack([-slope * t, 0 * slope * t, slope * t, 0 * slope * t], axis=1).astype(np.float32)
    return c, dm, aug


def kernel(**inputs):
    import concourse.bacc as bacc
    from concourse.bass_utils import run_bass_kernel_spmd as run

    a = {k: np.asarray(v) for k, v in inputs.items()}
    w = a["w_in"][0]
    fq, fk, fv, ff = w[:, 0:512], w[:, 512:1024], w[:, 1024:1536], w[:, 1536:1544]
    dq, dk, dv = w[:, 1544:2056], w[:, 2056:2568], w[:, 2568:3080]
    parts = [feature_units(np.pad(ff, ((0, 0), (0, 120))))]
    for q, k, v in ((fq, fk, fv), (dq, dk, dv)):
        parts.append(token_units(v))
        for g in range(2):
            s = slice(256 * g, 256 * g + 256)
            parts += [feature_units(q[:, s]), feature_units(k[:, s])]
    parts += [feature_units(a["w_out"][0]), feature_units(a["peer_wq"][0])]
    w2 = a["w_in_2"][0]
    q, k, v, gr, b, c, u, ga, gb = (w2[:, 1024 * i:1024 * i + 1024] for i in range(9))
    col = lambda m, h: m[:, 128 * h:128 * h + 128]
    for half in range(2):
        parts.append(token_units(v[:, 512 * half:512 * half + 512]))
        for h in range(4 * half, 4 * half + 4):
            parts += [feature_units(col(m, h)) for m in (q, k, gr)]
    for h in range(8):
        parts += [feature_units(col(ga, h)), feature_units(col(a["ret_w_out_2"][0], h))]
    for h in range(8):
        parts += [feature_units(col(m, h)) for m in (b, c, u)]
    for h in range(8):
        parts += [feature_units(col(gb, h)), feature_units(col(a["conv_w_out_2"][0], h))]
    parts.append(feature_units(a["mix_w_out_2"][0]))
    for h in range(22):
        parts += [feature_units(col(a["ffn_w_gate_2"][0], h)), feature_units(col(a["ffn_w_up_2"][0], h))]
    down = feature_units(a["ffn_w_down_2"][0])
    down = down.reshape(8, 128, 22, 128).transpose(0, 2, 1, 3).reshape(22, 8, 128, 128)
    parts.append(down.transpose(0, 2, 1, 3).reshape(22, 128, 1024))
    wts = np.concatenate(parts)
    ut = np.ascontiguousarray(a["peer_u"][0].reshape(128, 128, 8, 128).transpose(1, 3, 2, 0)).reshape(128, 128, 1024)
    vt = np.ascontiguousarray(a["peer_v"][0].reshape(128, 128, 1024).transpose(1, 0, 2))
    skt = a["peer_subkeys"][0].reshape(16, 128, 128).transpose(2, 0, 1).reshape(128, 2048)
    small = np.zeros((128, 144), np.float32)
    for n, name in enumerate(("norm1_g", "norm2_g", "normf_g", "norm_mix_g_2", "norm_ffn_g_2", "final_norm_g_2")):
        small[:, 8 * n:8 * n + 8] = columns(a[name])
    small[:, 48:96] = columns(a["ada_b_2"])
    small[:, 96:120] = columns(a["conv_w_2"])
    small[:, 120:128] = columns(a["c_2"])
    small[0:8, 128] = a["b_forget"][0]
    cst, dmat, augd = constants()
    feeds = {
        "x": a["x"][0].T, "wts": wts, "ut": ut, "vt": vt, "skt": skt, "small": small, "cst": cst,
        "dmat": dmat, "augd": augd, "pos": a["positions_2"][0], "adaw": a["ada_w_2"][0].reshape(8, 128, 6144),
    }
    feeds = {n: np.ascontiguousarray(v) for n, v in feeds.items()}
    nc = bacc.Bacc("TRN2", target_bir_lowering=False, num_devices=1)
    args = [nc.dram_tensor(n, v.shape, mybir.dt.from_np(v.dtype), kind="ExternalInput").ap()
            for n, v in feeds.items()]
    out = nc.dram_tensor("out", (1024, T), F32, kind="ExternalOutput").ap()
    build_program(nc, *args, out)
    r = run(nc, [feeds], core_ids=[0])
    return np.ascontiguousarray(r.results[0]["out"].T)[None]
```

```python
from contextlib import ExitStack

import numpy as np
import concourse.bass as bass
from concourse import mybir

F32 = mybir.dt.float32
F32R = mybir.dt.float32r
BF16 = mybir.dt.bfloat16
I32 = mybir.dt.int32
U32 = mybir.dt.uint32
ALU = mybir.AluOpType
ACT = mybir.ActivationFunctionType
AX = mybir.AxisListType

T = 512
NEG = -1e30
LOWEST = -3.0e38
NRAW = 6
NW = 4
W_BLOCK1 = 49
W_BLOCK2 = 162
EPS = 1e-6


class Queue:

    def __init__(self, sem):
        self.sem, self.n, self.ops, self.seen = sem, 0, [], {}

    def wait(self, *tokens):
        for t in tokens:
            if t is None:
                continue
            if isinstance(t, list):
                self.wait(*t)
                continue
            sem, value = t
            if self.seen.get(sem.num, 0) < value:
                self.seen[sem.num] = value
                self.ops.append(lambda e, s=sem, v=value: e.wait_ge(s, v))

    def quiet(self, fn, *tokens):
        self.wait(*tokens)
        self.ops.append(fn)

    def do(self, fn, *tokens):
        self.wait(*tokens)
        self.n += 1
        self.ops.append(lambda e: fn(e).then_inc(self.sem, 1))
        return (self.sem, self.n)

    def play(self, e):
        for op in self.ops:
            op(e)


class Lane:

    def __init__(self, sem):
        self.sem, self.n = sem, 0


class Slots:

    def __init__(self, bufs):
        self.bufs, self.free, self.i = list(bufs), [[] for _ in bufs], -1

    def take(self):
        assert any(f is not None for f in self.free)
        self.i = (self.i + 1) % len(self.bufs)
        while self.free[self.i] is None:
            self.i = (self.i + 1) % len(self.bufs)
        free, self.free[self.i] = self.free[self.i], None
        return self.i, self.bufs[self.i], free


def build_program(nc, x, wts, ut, vt, skt, small, cst, dmat, augd, pos, adaw, out):
    ctx = ExitStack()
    with ctx:
        def sem(name):
            return ctx.enter_context(nc.semaphore(name))

        base = -(-nc.sbuf_base // 64) * 64

        def at(name, kb, shape, dt):
            return nc.alloc_sbuf_tensor_at(name, shape, dt, offset=base + int(kb * 1024))

        PE, DVE, SC, GP = (Queue(sem(n)) for n in ("s_pe", "s_dve", "s_act", "s_pool"))
        SP = Queue(None)
        lanes = {}

        def dma(name, dst, src, *tokens):
            if name not in lanes:
                lanes[name] = Lane(sem("d_" + name))
            lane = lanes[name]
            if lane.n:
                SP.wait((lane.sem, 16 * lane.n))
            SP.wait(*tokens)
            lane.n += 1
            SP.ops.append(lambda e: e.dma_start(dst, src).then_inc(lane.sem, 16))
            return (lane.sem, 16 * lane.n)

        def copy(dst, src, *tokens, scale=None):
            if scale is None:
                return SC.do(lambda e: e.activation(dst, src, ACT.Copy), *tokens)
            return SC.do(lambda e: e.activation(dst, src, ACT.Copy, scale=scale), *tokens)

        def act(dst, src, func, *tokens, **kw):
            return SC.do(lambda e: e.activation(dst, src, func, **kw), *tokens)

        def tt(dst, a, b, op, *tokens):
            return DVE.do(lambda e: e.tensor_tensor(dst, a, b, op), *tokens)

        def ts(dst, a, s1, s2, op0, op1, *tokens):
            if op1 is None:
                return DVE.do(lambda e: e.tensor_scalar(dst, a, s1, None, op0), *tokens)
            return DVE.do(lambda e: e.tensor_scalar(dst, a, s1, s2, op0, op1), *tokens)

        def stt(dst, a, s, b, op0, op1, *tokens):
            return DVE.do(lambda e: e.scalar_tensor_tensor(out=dst, in0=a, scalar=s, in1=b,
                                                           op0=op0, op1=op1), *tokens)

        def mm(dst, lhs, rhs, start, stop, *tokens, last=False, skip=False):
            def fn(e):
                return e.matmul(dst, lhs, rhs, start=start, stop=stop, skip_group_check=skip)
            return PE.do(fn, *tokens) if last else PE.quiet(fn, *tokens)

        def vcopy(dst, src, *tokens):
            return DVE.do(lambda e: e.tensor_copy(dst, src), *tokens)

        def vset(dst, value, *tokens):
            return DVE.do(lambda e: e.memset(dst, value), *tokens)

        def recip(dst, src, *tokens):
            return DVE.do(lambda e: e.reciprocal(dst, src), *tokens)

        def reduce(dst, src, op, *tokens):
            return DVE.do(lambda e: e.tensor_reduce(dst, src, AX.X, op), *tokens)

        def turned(dst, src, *tokens):
            return PE.do(lambda e: e.transpose(dst, src, ident[:, :]), *tokens)

        def split(H, L, src, *tokens, scale=None):
            a = copy(H, src, *tokens, scale=scale)
            if scale is None:
                return [a, tt(L, src, H.bitcast(F32), ALU.subtract, a, *tokens)]
            return [a, stt(L, src, scale, H.bitcast(F32), ALU.mult, ALU.subtract, a, *tokens)]

        RAW = [at(f"raw{i}", 4 * i, [128, 1024], F32) for i in range(NRAW)]
        WH = [at(f"wh{i}", 24 + 4 * i, [128, 1024], F32R) for i in range(NW)]
        WL = [at(f"wl{i}", 40 + 4 * i, [128, 1024], F32R) for i in range(NW)]
        ident = at("ident", 56, [128, 128], F32)
        iota = at("iota", 56.5, [128, 128], F32)
        ones = at("ones", 57, [128, 128], F32)
        identb = at("identb", 57.5, [128, 128], BF16)
        sm = at("sm", 57.75, [128, 144], F32)
        csil = at("csil", 58.3125, [128, 8], F32)
        mod = at("mod", 58.375, [128, 48], F32)
        gmod = at("gmod", 58.5625, [128, 16], F32)
        st = at("st", 58.625, [128, 64], F32)
        invf = at("invf", 58.875, [128, 1], F32)
        XH = at("XH", 60, [128, 8, T], F32R)
        XL = at("XL", 76, [128, 8, T], F32R)
        Tb = Slots([at(f"T{i}", 92 + 2 * i, [128, T], F32) for i in range(7)])
        F = 106
        P = [ctx.enter_context(nc.psum_tensor(f"P{i}", [128, T], F32)) for i in range(8)]
        pfree = [[] for _ in range(8)]

        def take(b):
            free, pfree[b] = pfree[b], None
            assert free is not None, b
            return P[b], free

        class Banks:
            def __init__(self, ids):
                self.ids, self.i = ids, -1

            def next(self):
                self.i = (self.i + 1) % len(self.ids)
                b = self.ids[self.i]
                return (b, *take(b))

        def everyone():
            now = [(q.sem, q.n) for q in (PE, DVE, SC, GP) if q.n]
            for q in (PE, DVE, SC, GP, SP):
                q.wait(*now)

        stream = ([wts[i] for i in range(W_BLOCK1)] + [ut[i] for i in range(128)]
                  + [vt[i] for i in range(128)] + [wts[W_BLOCK1 + i] for i in range(W_BLOCK2)])
        raw_tok, split_tok, used_tok = {}, {}, {}
        high_tok = {}
        state = {"dma": 0, "high": 0, "split": 0, "unit": 0}

        def load_to(n):
            while state["dma"] < min(n, len(stream)):
                i = state["dma"]
                free = split_tok.get(i - NRAW)
                raw_tok[i] = dma(f"w{i % NRAW}", RAW[i % NRAW][:, :], stream[i], free)
                state["dma"] += 1

        def given_back(i):
            return i < NW or i - NW in used_tok

        def high_to(n):
            while state["high"] < min(n, len(stream)) and given_back(state["high"]):
                i = state["high"]
                load_to(i + 1)
                high_tok[i] = copy(WH[i % NW][:, :], RAW[i % NRAW][:, :], raw_tok[i], used_tok.get(i - NW))
                state["high"] += 1

        def split_to(n):
            while state["split"] < min(n, len(stream)) and given_back(state["split"]):
                i = state["split"]
                high_to(i + 1)
                s = i % NW
                split_tok[i] = [high_tok[i], tt(WL[s][:, :], RAW[i % NRAW][:, :], WH[s][:, :].bitcast(F32),
                                                ALU.subtract, high_tok[i], used_tok.get(i - NW))]
                load_to(i + NRAW)
                state["split"] += 1

        def split_ahead():
            high_to(state["unit"] + NW)
            split_to(state["unit"] + NW)

        def next_unit():
            i = state["unit"]
            state["unit"] += 1
            high_to(i + NW)
            split_to(i + NW - 1)
            assert i in split_tok
            PE.wait(split_tok[i])
            return i, WH[i % NW], WL[i % NW]

        side = {"work": None, "credit": 0.0}

        def beside(work):
            side["work"], side["credit"] = work, 0.0

        def tick():
            if side["work"] is None:
                return
            side["credit"] += 1.0
            while side["credit"] > 0:
                cost = next(side["work"], "end")
                if cost == "end":
                    side["work"] = None
                    return
                if cost is None:
                    side["credit"] = 0.0
                    return
                side["credit"] -= cost

        def finish_side():
            while side["work"] is not None:
                if next(side["work"], "end") == "end":
                    side["work"] = None

        def tile(bank, unit, c, H, L, start, stop, last=False):
            i, wh, wl = unit
            w = slice(c * 128, c * 128 + 128)
            mm(bank[:, :], wh[:, w], H, start, False)
            mm(bank[:, :], wh[:, w], L, False, False)
            t = mm(bank[:, :], wl[:, w], H, False, stop, last=last or c == 7)
            if c == 7:
                used_tok[i] = t
            return t

        def feature_major(b, H, L, toks):
            bank, free = take(b)
            unit = next_unit()
            PE.wait(free)
            for k in range(8):
                PE.wait(toks[k])
                t = tile(bank, unit, k, H[:, k, :], L[:, k, :], k == 0, k == 7)
                tick()
            return t

        def feature_major_abreast(bs, H, L, toks):
            banks = [take(b) for b in bs]
            units = [next_unit() for _ in bs]
            done = [None] * len(bs)
            for k in range(8):
                PE.wait(toks[k])
                for n, (bank, free) in enumerate(banks):
                    PE.wait(free)
                    done[n] = tile(bank, units[n], k, H[:, k, :], L[:, k, :], k == 0, k == 7)
            return done

        CNT = at("CNT", F + 96, [128, T], F32)
        MDB = at("MDB", F + 98, [128, T], BF16)
        MCB = at("MCB", F + 99, [128, T], BF16)
        CS = at("CS", F + 48, [128, 1793], F32)
        XIN = at("XIN", F, [128, 8, T], F32)
        xt = x.rearrange("(k p) t -> p k t", p=128)
        k_x = [dma(f"x{j}", XIN[:, 2 * j:2 * j + 2, :], xt[:, 2 * j:2 * j + 2, :]) for j in range(4)]
        k_s = dma("c1", sm[:, :], small)
        k_c = dma("c0", CS[:, :], cst)
        AD = at("AD", F + 16, [8, 4, T], F32)
        k_ad = dma("c2", AD[:, :, :], augd)
        load_to(NRAW)
        d1 = vset(ones[:, :], 1.0)
        vcopy(ident[:, :], CS[:, 0:128], k_c)
        vcopy(identb[:, :], CS[:, 0:128])
        vcopy(iota[:, :], CS[:, 128:256])
        vcopy(CNT[:, :], CS[:, 256:768])
        vcopy(MDB[:, :], CS[:, 768:1280])
        vcopy(MCB[:, :], CS[:, 1280:1792])
        k_k = vcopy(invf[:, :], CS[:, 1792:1793])
        PE.wait(k_k)
        SC.wait(k_k)
        G1, G2, GF, GM, GN, GE = (sm[:, 8 * i:8 * i + 8] for i in range(6))
        ADB = sm[:, 48:96]
        CW = sm[:, 96:120]
        CV = sm[:, 120:128]
        BF = sm[0:8, 128:129]

        def diagonal(b, col, p):
            i, q, f = Tb.take()
            v = []
            for c in range(4):
                s = slice(128 * c, 128 * c + 128)
                v.append(DVE.do(lambda e, c=c, s=s: e.tensor_tensor_reduce(
                    out=q[:, s], in0=P[b][:, s], in1=ident[:, :], scale=1.0, scalar=0.0,
                    op0=ALU.mult, op1=ALU.add, accum_out=st[:, col + c:col + c + 1]), p, f))
            pfree[b] = [v[-1]]
            return i, q, v

        def diagonals(q, col, tok):
            return [ts(q[:, 128 * c:128 * c + 128], ident[:, :], st[:, col + c:col + c + 1], None,
                       ALU.mult, None, tok) for c in range(4)]

        def spread(dst, part, *free):
            i, q, v = part
            t = mm(P[dst][:, :], ones[:, :], q[:, :], True, True, v, *free, last=True)
            Tb.free[i] = [t]
            return t

        def inverse_root(b, scale, p):
            i, q, v = diagonal(b, 48, p)
            v = ts(st[:, 52:56], st[:, 48:52], scale, EPS, ALU.mult, ALU.add, v)
            v = recip(st[:, 56:60], st[:, 52:56], v)
            a = act(st[:, 60:64], st[:, 56:60], ACT.Sqrt, v)
            return i, q, diagonals(q, 60, a)

        class Rms:

            def __init__(self, b, groups=(7, 1), gain=None):
                self.b, self.groups, self.gain = b, groups, gain
                self.k, self.n, self.g = 0, 0, 0
                self.acc, self.new, self.ready = None, None, None
                self.bank, self.free = take(b)

            def product(self):
                if self.ready:
                    i, sq, a = self.ready
                    self.p = mm(self.bank[:, :], ones[:, :], sq[:, :], self.g == 0,
                                self.g == len(self.groups) - 1, a, self.free, d1, last=True)
                    Tb.free[i] = [self.p]
                    self.g += 1
                    self.ready = None

            def settle(self):
                if self.new:
                    i, sq, a = self.new
                    self.new = None
                    if self.acc is None:
                        self.acc = (i, sq, a)
                    else:
                        j, acc, b = self.acc
                        v = tt(acc[:, :], acc[:, :], sq[:, :], ALU.add, a, b)
                        Tb.free[i] = [v]
                        self.acc = (j, acc, v)
                    self.n += 1
                    if self.n == self.groups[self.k]:
                        self.ready, self.acc, self.n = self.acc, None, 0
                        self.k += 1

            def add(self, k, src, tok):
                i, sq, sf = Tb.take()
                kw = {} if self.gain is None else {"scale": self.gain[:, k:k + 1]}
                a = act(sq[:, :], src, ACT.Square, tok, sf, **kw)
                self.product()
                self.settle()
                self.new = (i, sq, a)

            def total(self):
                self.product()
                self.settle()
                self.product()
                return self.p

            def end(self, b):
                part = inverse_root(self.b, 1.0 / 1024, self.total())
                bank, free = take(b)
                return bank, spread(b, part, free)

        def norm_split(src, factor, gain, shift, b, *more):
            r, s = factor
            outt = []
            pend = None
            for k in range(8):
                i, t, f = Tb.take()
                v = last = stt(t[:, :], src[:, k, :], gain[:, k:k + 1], r[:, :], ALU.mult, ALU.mult, s, f, k_s, *more)
                if shift is not None:
                    v = ts(t[:, :], t[:, :], shift[:, k:k + 1], None, ALU.add, None, v)
                if pend:
                    pend()
                a = copy(XH[:, k, :], t[:, :], v)

                def pend(k=k, i=i, t=t, a=a):
                    w = tt(XL[:, k, :], t[:, :], XH[:, k, :].bitcast(F32), ALU.subtract, a)
                    Tb.free[i] = [w]
                    outt.append([a, w])
            pend()
            pfree[b] = [last]
            return outt

        xin_t = [k_x[k // 2] for k in range(8)]
        high_to(NW)
        split_to(NW - 1)
        rms = Rms(0)
        for k in range(8):
            rms.add(k, XIN[:, k, :], xin_t[k])
        xtok = norm_split(XIN, rms.end(1), G1, None, 1)

        CA = [at(f"CA{i}", F + 24 + 2 * i, [8, T], F32) for i in range(4)]
        CR = [at(f"CR{i}", F + 32 + 2 * i, [8, T], F32R) for i in range(8)]
        cd = nc.dram_tensor("cdram", [2, 4, 8, T], F32, kind="Internal").ap()
        t, *first_qk = feature_major_abreast([1, 2, 3], XH, XL, xtok)
        v = ts(CA[0][:, :], P[1][0:8, :], BF, None, ALU.add, None, t, k_s)
        pfree[1] = [v]
        v2 = stt(CA[1][:, :], CA[0][:, :], -1.0, CA[0][:, :], ALU.mult, ALU.min, v)
        a = act(CA[1][:, :], CA[1][:, :], ACT.Exp, v2)
        a = act(CA[2][:, :], CA[1][:, :], ACT.Ln, a, bias=1.0)
        v = stt(CA[3][:, :], CA[0][:, :], 0.0, CA[2][:, :], ALU.min, ALU.subtract, a)
        v0 = vset(CA[1][:, :], 1.0, a)
        v = DVE.do(lambda e: e.tensor_tensor_scan(CA[0][:, :], CA[1][:, :], CA[3][:, :], 0.0,
                                                  ALU.mult, ALU.add), v, v0)
        w0 = vcopy(CR[0][:, :], CA[0][:, :], v)
        w1 = tt(CR[1][:, :], CA[0][:, :], CR[0][:, :].bitcast(F32), ALU.subtract, w0)
        w2 = ts(CR[2][:, :], CR[0][:, :].bitcast(F32), -1.0, None, ALU.mult, None, w0)
        w3 = ts(CR[3][:, :], CR[1][:, :].bitcast(F32), -1.0, None, ALU.mult, None, w1)
        w = w3
        for i in range(4):
            w = vcopy(CR[4 + i][:, :], AD[:, i, :], k_ad)
        cd_tok = []
        for br in range(2):
            for i in range(4):
                cd_tok.append(dma(f"cd{4 * br + i}", cd[br, i], CR[4 * br + i][:, :].bitcast(F32), w3 if br == 0 else w))

        PTH = at("PTH", F, [128, 4, T], F32R)
        PTL = at("PTL", F + 8, [128, 4, T], F32R)
        MH = at("MH", F + 16, [128, 8, T], F32R)
        ML = at("ML", F + 32, [128, 8, T], F32R)
        QK = [[at(f"QK{g}{i}", F + 48 + 16 * g + 4 * i, [128, 2, T], F32R) for i in range(4)] for g in range(2)]
        VV = [[at(f"VV{g}{i}", F + 80 + 4 * g + 2 * i, [128, 4, 128], F32R) for i in range(2)] for g in range(2)]
        fill = []
        for g in range(2):
            for i in range(4):
                fill.append(GP.do(lambda e, q=QK[g][i]: e.memset(q[64:128, :, :].bitcast(F32), 0.0), k_k))
        ones_tok = [GP.do(lambda e, q=QK[g][i]: e.memset(q[64:68, :, :].bitcast(F32), 1.0), fill)
                    for g in range(2) for i in (0, 2)]
        mtok = [[] for _ in range(8)]
        qk_tok, v_tok, qk_read, v_read = {}, {}, {}, {}
        ready = {"groups": 0}

        def heads_in(g):
            q = QK[g % 2]
            toks = []
            for j in range(2):
                if g == 0:
                    b, t = 2 + j, first_qk[j]
                else:
                    b = j
                    t = feature_major(b, XH, XL, xtok)
                before = qk_read[g - 2] if g >= 2 else None
                for half in range(2):
                    toks += split(q[2 * j][0:64, half, :], q[2 * j + 1][0:64, half, :],
                                  P[b][64 * half:64 * half + 64, :], t, before, scale=None if j else 0.125)
                pfree[b] = toks[-4:]
            br, h0 = g // 4, 2 * (g % 4)
            toks.append(dma("bq", q[0][64:66, :, :].bitcast(F32), cd[br, 0:2, h0:h0 + 2, :], cd_tok, ones_tok, before))
            toks.append(dma("bk", q[2][66:68, :, :].bitcast(F32), cd[br, 2:4, h0:h0 + 2, :], cd_tok, ones_tok, before))
            qk_tok[g] = toks
            t = feature_major(0, XH, XL, xtok)
            i, u, f = Tb.take()
            a = copy(u[:, :], P[0][:, :], t, f)
            pfree[0] = [a]
            bank, free = take(7)
            for c in range(4):
                t = turned(bank[:, 128 * c:128 * c + 128], u[:, 128 * c:128 * c + 128], a, free)
            Tb.free[i] = [t]
            v_tok[g] = split(VV[g % 2][0][:, :, :], VV[g % 2][1][:, :, :],
                             bank[:, :].rearrange("p (b c) -> p b c", b=4), t, v_read[g - 2] if g >= 2 else None)
            pfree[7] = v_tok[g]
            ready["groups"] = g + 1

        def attend():
            steps = [(g, h, qb) for g in range(8) for h in range(2) for qb in range(4)]
            sb, tr = Banks([2, 3]), Banks([4, 5])
            S, E, N, R, PT = {}, {}, {}, {}, {}
            pt_read = []

            def scores(n):
                g, h, qb = steps[n]
                q = QK[g % 2]
                kw = 128 * (qb + 1)
                b, bank, free = sb.next()
                qs = slice(qb * 128, qb * 128 + 128)
                PE.wait(free, qk_tok[g], fill)
                mm(bank[:, 0:kw], q[0][:, h, qs], q[2][:, h, 0:kw], True, False)
                mm(bank[:, 0:kw], q[0][:, h, qs], q[3][:, h, 0:kw], False, False)
                mm(bank[:, 0:kw], q[1][:, h, qs], q[2][:, h, 0:kw], False, False)
                mask = MCB if g < 4 else MDB
                t = mm(bank[:, 0:kw], identb[:, :], mask[:, (3 - qb) * 128:T], False, True, last=True)
                qk_read[g] = [t]
                S[n] = (b, t)

            def soft(n):
                g, h, qb = steps[n]
                kw = 128 * (qb + 1)
                b, t = S[n]
                c = 4 * (n % 4)
                m = reduce(st[:, c:c + 1], P[b][:, 0:kw], ALU.max, t)
                m = ts(st[:, c + 1:c + 2], st[:, c:c + 1], -1.0, None, ALU.mult, None, m)
                i, pbuf, pf = Tb.take()
                kw_args = {"accum_out": st[:, c + 2:c + 3]} if g < 4 else {}
                a = act(pbuf[:, 0:kw], P[b][:, 0:kw], ACT.Exp, m, pf, bias=st[:, c + 1:c + 2], **kw_args)
                pfree[b] = [m, a]
                E[n] = (i, pbuf, a)

            def normal(n):
                g, h, qb = steps[n]
                kw = 128 * (qb + 1)
                i, pbuf, a = E[n]
                c = 4 * (n % 4)
                if g >= 4:
                    a = DVE.do(lambda e: e.tensor_tensor_reduce(
                        out=pbuf[:, 0:kw], in0=pbuf[:, 0:kw], in1=CNT[:, (3 - qb) * 128:T], scale=1.0,
                        scalar=0.0, op0=ALU.mult, op1=ALU.add, accum_out=st[:, c + 2:c + 3]), a)
                v = recip(st[:, c + 3:c + 4], st[:, c + 2:c + 3], a)
                v = ts(pbuf[:, 0:kw], pbuf[:, 0:kw], st[:, c + 3:c + 4], None, ALU.mult, None, v)
                N[n] = (i, pbuf, v)

            def turn(n):
                g, h, qb = steps[n]
                i, pbuf, v = N[n]
                b, bank, free = tr.next()
                for kb in range(qb + 1):
                    t = turned(bank[:, kb * 128:kb * 128 + 128], pbuf[:, kb * 128:kb * 128 + 128], v, free)
                Tb.free[i] = [t]
                src = bank[:, 0:128 * (qb + 1)].rearrange("p (k q) -> p k q", q=128)
                R[n] = (b, src, copy(PTH[:, 0:qb + 1, qb * 128:qb * 128 + 128], src, t, pt_read))

            def turn_low(n):
                g, h, qb = steps[n]
                b, src, a = R[n]
                d = (slice(None), slice(0, qb + 1), slice(qb * 128, qb * 128 + 128))
                v = tt(PTL[d], src, PTH[d].bitcast(F32), ALU.subtract, a, pt_read)
                pfree[b] = [v]
                PT[n] = [a, v]

            def values(n):
                nonlocal pt_read
                g, h, _ = steps[n]
                bank, free = take(6)
                PE.wait(free, PT[n - 3], PT[n - 2], PT[n - 1], PT[n], v_tok[g])
                vh, vl = VV[g % 2]
                for kb in range(4):
                    d = bank[:, kb * 128:T]
                    r = slice(kb * 128, T)
                    mm(d, vh[:, kb, :], PTH[:, kb, r], kb == 0, False)
                    mm(d, vh[:, kb, :], PTL[:, kb, r], False, False)
                    t = mm(d, vl[:, kb, :], PTH[:, kb, r], False, kb == 3, last=kb == 3)
                pt_read = [t]
                v_read[g] = [t]
                rows = slice(64 * h, 64 * h + 64)
                r = split(MH[rows, g, :], ML[rows, g, :], bank[rows, :], t, cd_tok)
                mtok[g] += r
                pfree[6] = r

            ns = len(steps)
            for n in range(ns + 5):
                while n < ns and ready["groups"] <= steps[n][0]:
                    yield None
                if 0 <= n - 4 < ns:
                    turn_low(n - 4)
                if n < ns:
                    scores(n)
                if 0 <= n - 1 < ns:
                    soft(n - 1)
                if 0 <= n - 2 < ns:
                    normal(n - 2)
                yield 1.5
                if 0 <= n - 4 < ns and steps[n - 4][2] == 3:
                    values(n - 4)
                if 0 <= n - 3 < ns:
                    turn(n - 3)
                yield 1.4

        heads_in(0)
        beside(attend())
        for g in range(1, 8):
            heads_in(g)
        finish_side()

        hT = at("hT", F, [128, 8, T], F32)
        hx = [dma(f"x{j}", hT[:, 2 * j:2 * j + 2, :], xt[:, 2 * j:2 * j + 2, :], mtok) for j in range(4)]
        rms = Rms(4)
        for m in range(8):
            t = feature_major(m % 4, MH, ML, mtok)
            v = tt(hT[:, m, :], P[m % 4][:, :], hT[:, m, :], ALU.add, t, hx[m // 2])
            pfree[m % 4] = [v]
            rms.add(m, hT[:, m, :], v)
        split_ahead()
        factor = rms.end(5)
        everyone()
        xtok = norm_split(hT, factor, G2, None, 5)

        S = at("S", F + 16, [128, 16, 4, 128], F32)
        VAL = at("VAL", F + 48, [128, 4, 16, 16], F32)
        IDX = at("IDX", F + 52, [128, 4, 16, 16], U32)
        CSV = at("CSV", F + 56, [128, 4, 8, 16], F32)
        CIX = at("CIX", F + 58, [128, 4, 8, 16], U32)
        D1 = at("D1", F + 60, [128, 1024], F32)
        D2 = at("D2", F + 64, [128, 1024], F32)
        SKR = at("SKR", F + 68, [128, 2048], F32)
        SKH = at("SKH", F + 76, [128, 2048], F32R)
        SKL = at("SKL", F + 84, [128, 2048], F32R)
        QPH = [at(f"QPH{i}", F + 92 + 4 * i, [128, T], F32R) for i in range(2)]
        QPL = [at(f"QPL{i}", F + 94 + 4 * i, [128, T], F32R) for i in range(2)]
        k_sk = dma("c0", SKR[:, :], skt)
        sk = split(SKH[:, 0:1024], SKL[:, 0:1024], SKR[:, 0:1024], k_sk)
        sk += split(SKH[:, 1024:2048], SKL[:, 1024:2048], SKR[:, 1024:2048], k_sk)
        qfree = [[], []]
        stok = {}

        def key_scores(hp, qt):
            bank, free = take(6 + hp % 2)
            PE.wait(free, qt, sk)
            ks = slice(hp * 128, hp * 128 + 128)
            for tb in range(4):
                d = bank[:, tb * 128:tb * 128 + 128]
                q = slice(tb * 128, tb * 128 + 128)
                mm(d, QPH[hp % 2][:, q], SKH[:, ks], True, False)
                mm(d, QPH[hp % 2][:, q], SKL[:, ks], False, False)
                t = mm(d, QPL[hp % 2][:, q], SKH[:, ks], False, True, last=tb == 3)
            qfree[hp % 2] = [t]
            a = copy(S[:, hp, :, :], bank[:, :].rearrange("p (b k) -> p b k", b=4), t)
            pfree[6 + hp % 2] = [a]
            stok[hp] = a

        toptok = {}

        def top16(src, val, idx, tok):
            a = DVE.do(lambda e: e.max(val[:, 0:8], src), tok)
            b = DVE.do(lambda e: e.max_index(idx[:, 0:8], val[:, 0:8], src), a)
            c = DVE.do(lambda e: e.match_replace(src, val[:, 0:8], src, LOWEST), b)
            d = DVE.do(lambda e: e.max(val[:, 8:16], src), c)
            return DVE.do(lambda e: e.max_index(idx[:, 8:16], val[:, 8:16], src), d)

        def route():
            for hp in range(16):
                while hp not in stok:
                    yield None
                for tb in range(4):
                    toptok[hp, tb] = top16(S[:, hp, tb, :], VAL[:, tb, hp, :], IDX[:, tb, hp, :], stok[hp])
                    yield 1.9
            for tb in range(4):
                for h in range(8):
                    i, c, f = Tb.take()
                    c = c[:, 0:256]
                    v1 = VAL[:, tb, 2 * h, :].unsqueeze(2).to_broadcast([128, 16, 16])
                    v2 = VAL[:, tb, 2 * h + 1, :].unsqueeze(1).to_broadcast([128, 16, 16])
                    t = tt(c.rearrange("p (a b) -> p a b", a=16), v1, v2, ALU.add,
                           toptok[2 * h, tb], toptok[2 * h + 1, tb], f)
                    t = top16(c, CSV[:, tb, h, :], CIX[:, tb, h, :], t)
                    Tb.free[i] = [t]
                    toptok["c", tb, h] = t
                    yield 6.0

        GR = at("GR", F + 68, [128, 4, 128], F32)
        U1 = at("U1", F + 70, [128, 128], U32)
        AF = at("AF", F + 70.5, [128, 128], F32)
        IF = at("IF", F + 71, [128, 8, 16], F32)
        IS = at("IS", F + 71.5, [128, 2, 128], F32)
        IT = at("IT", F + 72.5, [128, 2, T], BF16)
        GT = at("GT", F + 74.5, [128, 3, T], BF16)
        IOT = at("IOT", F + 77.5, [128, 128, 4], BF16)
        GRT = at("GRT", F + 78.5, [128, 2, 128], F32)
        OE = [at(f"OE{i}", F + 79.5 + 2 * i, [128, 2, 128, 4], BF16) for i in range(3)]
        OM = [at(f"OM{i}", F + 85.5 + 3 * i, [128, 3, 128, 4], BF16) for i in range(2)]
        HID = Slots([at(f"HID{i}", F + 92.5 + 4 * i, [128, 2, T], F32) for i in range(2)])
        GS = [at(f"GS{i}", F + 16 + 16 * i, [128, 128, 32], F32) for i in range(2)]
        dg = nc.dram_tensor("gdram", [16, 128, 128, 32], F32, kind="Internal").ap()
        dh = nc.dram_tensor("hdram", [32, 128, 4, T], F32, kind="Internal").ap()
        dg_tok, dh_tok = [], {}

        def gates():
            ittok = []
            for tb in range(4):
                c = CSV[:, tb, :, :]
                gr = GR[:, tb, :].rearrange("p (h k) -> p h k", h=8)
                tops = [toptok["c", tb, h] for h in range(8)]
                v = tt(gr, c, CSV[:, tb, :, 0:1].to_broadcast([128, 8, 16]), ALU.subtract, tops)
                a = act(gr, gr, ACT.Exp, v)
                v = reduce(st[:, 32:40], gr, ALU.add, a)
                v = recip(st[:, 40:48], st[:, 32:40], v)
                vg = tt(gr, gr, st[:, 40:48].unsqueeze(2).to_broadcast([128, 8, 16]), ALU.mult, v)
                yield 3.0
                fin = []
                for p in range(2):
                    ci = CIX[:, tb, :, :].rearrange("p h k -> p (h k)")
                    if p == 0:
                        v = ts(U1[:, :], ci, 4, None, ALU.logical_shift_right, None)
                    else:
                        v = ts(U1[:, :], ci, 15, None, ALU.bitwise_and, None, v)
                    v1 = vcopy(AF[:, :], U1[:, :], v)
                    idv = IDX[:, tb, :, :].rearrange("p (h q) a -> p h q a", q=2)[:, :, p, :]
                    v2 = vcopy(IF[:, :, :], idv)
                    for hh in range(2):
                        d1v = D1[:, :].rearrange("p (s a) -> p s a", a=16)
                        v = tt(d1v, AF[:, 64 * hh:64 * hh + 64].unsqueeze(2).to_broadcast([128, 64, 16]),
                               iota[:, 0:16].unsqueeze(1).to_broadcast([128, 64, 16]), ALU.is_equal, v1)
                        d1q = D1[:, :].rearrange("p (h k a) -> p h k a", h=4, a=16)
                        d2q = D2[:, :].rearrange("p (h k a) -> p h k a", h=4, a=16)
                        v = tt(d2q, d1q, IF[:, 4 * hh:4 * hh + 4, :].unsqueeze(2).to_broadcast([128, 4, 16, 16]),
                               ALU.mult, v, v2)
                        v = reduce(IS[:, p, 64 * hh:64 * hh + 64],
                                   D2[:, :].rearrange("p (s a) -> p s a", a=16), ALU.add, v)
                        yield 9.5
                    fin.append(v)
                bank, free = take(6)
                t = None
                for n, s in enumerate((IS[:, 0, :], IS[:, 1, :], GR[:, tb, :])):
                    t = turned(bank[:, n * 128:n * 128 + 128], s, fin, vg, free)
                q = slice(tb * 128, tb * 128 + 128)
                a2 = copy(IT[:, :, q], bank[:, 0:256].rearrange("p (a b) -> p a b", a=2), t)
                v = vcopy(GT[:, 0, q], bank[:, 256:384], a2)
                v = tt(GRT[:, 0, :], bank[:, 256:384], GT[:, 0, q], ALU.subtract, v)
                pfree[6] = [a2, v]
                v = vcopy(GT[:, 1, q], GRT[:, 0, :], v)
                v = tt(GRT[:, 1, :], GRT[:, 0, :], GT[:, 1, q], ALU.subtract, v)
                v = vcopy(GT[:, 2, q], GRT[:, 1, :], v)
                DVE.wait(t)
                ittok.append([a2, v])
                yield 1.0
            oe_free, om_free = [[], [], []], [[], []]
            gs_free = [[], []]
            sdone = toptok["c", 3, 7]
            for j in range(4):
                v = vcopy(IOT[:, :, j], iota[:, :])
            same, scaled = {-1: v}, {}

            def hot(n):
                q = slice(4 * n, 4 * n + 4)
                same[n] = tt(OE[n % 3][:, :, :, :], IOT[:, :, :].unsqueeze(1).to_broadcast([128, 2, 128, 4]),
                             IT[:, :, q].unsqueeze(2).to_broadcast([128, 2, 128, 4]), ALU.is_equal,
                             same[-1], ittok[n // 32], oe_free[n % 3])

            def weigh(n):
                q = slice(4 * n, 4 * n + 4)
                scaled[n] = tt(OM[n % 2][:, :, :, :],
                               OE[n % 3][:, 0, :, :].unsqueeze(1).to_broadcast([128, 3, 128, 4]),
                               GT[:, :, q].unsqueeze(2).to_broadcast([128, 3, 128, 4]), ALU.mult,
                               same[n], om_free[n % 2])

            def grid(n):
                b = 6 + n % 2
                bank, free = take(b)
                PE.wait(scaled[n], free)
                for j in range(4):
                    d = bank[:, j * 128:j * 128 + 128]
                    for k in range(3):
                        tk = mm(d, OM[n % 2][:, k, :, j], OE[n % 3][:, 1, :, j], k == 0, k == 2, last=j == 3 and k == 2)
                oe_free[n % 3], om_free[n % 2] = [tk], [tk]
                g, o = n // 8, 4 * (n % 8)
                dst = GS[g % 2][:, :, o:o + 4].rearrange("p i t -> p t i")
                a = copy(dst, bank[:, :].rearrange("p (t i) -> p t i", t=4), tk, gs_free[g % 2], sdone)
                pfree[b] = [a]
                if n % 8 == 7:
                    tk = dma(f"g{g % 2}", dg[g], GS[g % 2][:, :, :], a)
                    gs_free[g % 2] = [tk]
                    dg_tok.append(tk)

            for n in range(130):
                if n < 128:
                    hot(n)
                if 0 <= n - 1 < 128:
                    weigh(n - 1)
                if n > 1:
                    grid(n - 2)
                yield 4.1

        def queries(hp, b, t):
            qt = split(QPH[hp % 2][:, :], QPL[hp % 2][:, :], P[b][:, :], t, qfree[hp % 2])
            pfree[b] = qt
            return hp, qt

        bg = route()
        ts3 = feature_major_abreast([0, 1, 2], XH, XL, xtok)
        behind = queries(0, 0, ts3[0])
        for hp in range(1, 3):
            now = queries(hp, hp, ts3[hp])
            key_scores(*behind)
            behind = now
        beside(bg)
        for hp in range(3, 16):
            b = hp % 4
            t = feature_major(b, XH, XL, xtok)
            now = queries(hp, b, t)
            key_scores(*behind)
            behind = now
        key_scores(*behind)

        wq_end = [(PE.sem, PE.n), (DVE.sem, DVE.n), (SC.sem, SC.n)]

        def background():
            yield from bg
            for q in (PE, DVE, SC, GP):
                q.wait(wq_end)
            yield from gates()

        beside(background())
        hb = Banks([0, 1, 2, 3])
        GI = [at(f"GI{i}", F + 16 + 8 * i, [128, 16, 128], F32) for i in range(2)]
        HI = [at(f"HI{i}", F + 32 + 8 * i, [128, 4, T], F32) for i in range(2)]
        AH = [at(f"AH{i}", F + 48 + 2 * i, [128, T], F32R) for i in range(3)]
        AL = [at(f"AL{i}", F + 54 + 2 * i, [128, T], F32R) for i in range(3)]
        ACC = at("ACC", F + 60, [128, 6144], F32)
        ACL = at("ACL", F + 60, [128, 6144], F32R)
        ACH = at("ACH", 60, [128, 6144], F32R)
        ONE = at("ONE", F + 84, [128, 2], F32R)
        AW = [at(f"AW{i}", 84 + 4 * i, [128, 1024], F32) for i in range(2)]
        gi_free = [[], []]
        gi_tok = {}
        a_free = [[], [], []]
        a_ready = {}

        def fetch(g):
            s = g % 2
            gi_tok[g] = [
                dma(f"gi{s}", GI[s][:, :, :], dg[:, :, 4 * g:4 * g + 4, :].rearrange("g p i t -> p g (i t)"),
                    gi_free[s], dg_tok),
                dma(f"hi{s}", HI[s][:, :, :], dh[g], gi_free[s], dh_tok[2 * g], dh_tok[2 * g + 1])]

        def activate(i2):
            g, j = divmod(i2, 4)
            if j == 0 and g + 1 < 32:
                fetch(g + 1)
            i, t, f = Tb.take()
            gv = GI[g % 2][:, :, 32 * j:32 * j + 32]
            v = tt(t[:, :].rearrange("p (g t) -> p g t", g=16),
                   HI[g % 2][:, j, :].rearrange("p (g t) -> p g t", g=16), gv, ALU.mult, gi_tok[g], f)
            if j == 3:
                gi_free[g % 2] = [v]
            r = split(AH[i2 % 3][:, :], AL[i2 % 3][:, :], t[:, :], v, a_free[i2 % 3])
            Tb.free[i] = r
            a_ready[i2] = r

        for i2 in range(128):
            if i2 == 124:
                finish_side()
                region = [(DVE.sem, DVE.n), (PE.sem, PE.n)]
                SC.wait(region)
                SP.wait(region)
                fetch(0)
            b, bank, free = hb.next()
            unit = next_unit()
            PE.wait(free)
            for k in range(8):
                PE.wait(xtok[k])
                t = tile(bank, unit, k, XH[:, k, :], XL[:, k, :], k == 0, k == 7)
                tick()
            if i2 % 2 == 0:
                hi, hbuf, hf = HID.take()
            a = act(hbuf[:, i2 % 2, :], bank[:, :], ACT.Gelu, t, hf)
            pfree[b] = [a]
            if i2 % 2 == 1:
                tk = dma(f"h{hi}", dh[i2 // 4, :, 2 * (i2 // 2 % 2):2 * (i2 // 2 % 2) + 2, :], hbuf[:, :, :], a)
                HID.free[hi] = [tk]
                dh_tok[i2 // 2] = tk
            if i2 == 126:
                activate(0)
                activate(1)
        u_end = (PE.sem, PE.n)

        acc_tok = {}
        k_cs = act(csil[:, :], CV, ACT.Silu, k_s)

        ach_tok = []

        def modulation():
            aw_free = [[], []]
            for k in range(8):
                for c in range(6):
                    s = c % 2
                    w = dma(f"aw{s}", AW[s][:, :], adaw[k, :, 1024 * c:1024 * c + 1024], aw_free[s], u_end)
                    dst = ACC[:, 1024 * c:1024 * c + 1024]
                    if k == 0:
                        v = ts(dst, AW[s][:, :], csil[:, 0:1], None, ALU.mult, None, w, k_cs, u_end)
                    else:
                        v = stt(dst, AW[s][:, :], csil[:, k:k + 1], dst, ALU.mult, ALU.add, w, acc_tok[c])
                    aw_free[s] = [v]
                    acc_tok[c] = v
                    yield 16
            for c in range(12):
                q = slice(512 * c, 512 * c + 512)
                a = copy(ACH[:, q], ACC[:, q], acc_tok[c // 2], u_end)
                ach_tok.append([a, tt(ACL[:, q], ACC[:, q], ACH[:, q].bitcast(F32), ALU.subtract, a)])
                yield 8

        beside(modulation())
        banks = {}
        for i2 in range(128):
            unit = next_unit()
            s = i2 % 3
            PE.wait(a_ready[i2])
            ydone = []
            for d in range(8):
                if i2 == 0:
                    banks[d], free = take(d)
                    PE.wait(free)
                ydone.append(tile(banks[d], unit, d, AH[s][:, :], AL[s][:, :], i2 == 0, i2 == 127, last=i2 == 127))
                if i2 > 3:
                    tick()
            a_free[s] = [(PE.sem, PE.n)]
            if i2 + 2 < 128:
                activate(i2 + 2)
        finish_side()
        one = vset(ONE[:, :].bitcast(F32), 1.0)
        split_ahead()

        for d in range(8):
            v = tt(hT[:, d, :], P[d][:, :], hT[:, d, :], ALU.add, ydone[d])
            pfree[d] = [v]
            if d == 0:
                mbank, free = take(0)
                PE.wait(free, one, ach_tok)
                for n in range(48):
                    w = slice(n * 128, n * 128 + 128)
                    mm(mbank[:, 2 * n:2 * n + 2], ACH[:, w], ONE[:, :], True, False)
                    tm = mm(mbank[:, 2 * n:2 * n + 2], ACL[:, w], ONE[:, :], False, True, last=n == 47)
            if d == 1:
                rms1 = Rms(1, (2, 2, 2, 1, 1))
            if d == 2:
                rms2 = Rms(2, (2, 2, 2, 1, 1), GF)
                for k in range(2):
                    rms1.add(k, hT[:, k, :], v)
                    rms2.add(k, hT[:, k, :], v)
            if d > 1:
                rms1.add(d, hT[:, d, :], v)
                rms2.add(d, hT[:, d, :], v)
        everyone()
        v = tt(mod[:, :], mbank[:, 0:96].rearrange("p (n c) -> p n c", c=2)[:, :, 0], ADB, ALU.add, tm)
        pfree[0] = [v]
        p1, p2 = rms1.total(), rms2.total()
        i1_, q1, v1 = diagonal(1, 32, p1)
        i2_, q2, v2 = diagonal(2, 48, p2)
        va = ts(st[:, 36:40], st[:, 32:36], 1.0 / 1024, EPS, ALU.mult, ALU.add, v1)
        va = recip(st[:, 40:44], st[:, 36:40], va)
        vb = tt(st[:, 52:56], st[:, 48:52], st[:, 40:44], ALU.mult, va, v2)
        vb = ts(st[:, 52:56], st[:, 52:56], 1.0 / 1024, EPS, ALU.mult, ALU.add, vb)
        vb = recip(st[:, 56:60], st[:, 52:56], vb)
        vb = tt(st[:, 56:60], st[:, 56:60], st[:, 40:44], ALU.mult, vb)
        ab = act(st[:, 60:64], st[:, 56:60], ACT.Sqrt, vb)
        aa = act(st[:, 44:48], st[:, 40:44], ACT.Sqrt, va)
        v = ts(gmod[:, 0:8], mod[:, 8:16], 1.0, None, ALU.add, None, v)
        v = tt(gmod[:, 0:8], gmod[:, 0:8], GM, ALU.mult, v)
        v = tt(gmod[:, 0:8], gmod[:, 0:8], GF, ALU.mult, v)
        vn = ts(gmod[:, 8:16], mod[:, 32:40], 1.0, None, ALU.add, None, v)
        k_mod = tt(gmod[:, 8:16], gmod[:, 8:16], GN, ALU.mult, vn)
        SH_M, GT_M, SH_F, GT_F = mod[:, 0:8], mod[:, 16:24], mod[:, 24:32], mod[:, 40:48]
        bank, free = take(4)
        factor = bank, spread(4, (i2_, q2, diagonals(q2, 60, ab)), free)
        _, free = take(3)
        t_r1 = spread(3, (i1_, q1, diagonals(q1, 44, aa)), free)
        xtok = norm_split(hT, factor, gmod[:, 0:8], SH_M, 4, k_mod)
        h_read = xtok[-1]

        VR = [[at(f"VR{i}{j}", F + 16 + 4 * i + 2 * j, [128, 4, 128], F32R) for j in range(2)] for i in range(2)]
        RH = at("RH", F + 32, [128, 8, T], F32R)
        RL = at("RL", F + 48, [128, 8, T], F32R)
        QR = [[at(f"QR{i}{j}", F + 64 + 8 * i + 2 * j, [128, T], F32R) for j in range(4)] for i in range(2)]
        offs = [0, 512, 896, 1152, 1280]
        SRH = at("SRH", F + 80, [128, 1280], F32R)
        SRL = at("SRL", F + 85, [128, 1280], F32R)
        COS = at("COS", F + 90, [128, T], F32)
        SIN = at("SIN", F + 92, [128, T], F32)
        DM = [at(f"DM{i}", F + 94 + 2 * i, [128, T], F32) for i in range(2)]
        PI = at("PI", F + 98, [128, T], I32)
        k_p = dma("c0", PI[:, :], pos.partition_broadcast(128))
        ia, ang, fa = Tb.take()
        ib, qn, fb = Tb.take()
        v = vcopy(ang[:, :], PI[:, :], k_p, fa)
        v = ts(ang[:, :], ang[:, :], invf[:, 0:1], None, ALU.mult, None, v)
        for dst, shift in ((SIN, 0.0), (COS, 0.25)):
            v = ts(qn[:, :], ang[:, :], float(1.0 / (2 * np.pi)), shift, ALU.mult, ALU.add, v, fb)
            v = ts(qn[:, :], qn[:, :], 12582912.0, None, ALU.add, None, v)
            v = ts(qn[:, :], qn[:, :], -12582912.0, None, ALU.add, None, v)
            v = stt(dst[:, :], qn[:, :], -6.28125, ang[:, :], ALU.mult, ALU.add, v)
            v = stt(dst[:, :], qn[:, :], -float(np.float32(0.0019350051879882812)), dst[:, :], ALU.mult, ALU.add, v)
            rest = 2 * np.pi - 6.28125 - 0.0019350051879882812
            v = stt(dst[:, :], qn[:, :], -float(rest), dst[:, :], ALU.mult, ALU.add, v)
            if shift:
                v = ts(dst[:, :], dst[:, :], float(np.pi / 2), None, ALU.add, None, v)
            v = ts(dst[:, :], dst[:, :], float(np.float32(3.1415925)), float(np.float32(-3.1415925)),
                   ALU.min, ALU.max, v)
            a = act(dst[:, :], dst[:, :], ACT.Sin, v)
        k_cos = a
        k_sin = ts(SIN[64:128, :], SIN[64:128, :], -1.0, None, ALU.mult, None, a)
        Tb.free[ia] = [v]
        Tb.free[ib] = [v]

        qr_free, dm_free, vr_free = [[], []], [[], []], [[], []]
        rtok = [[] for _ in range(8)]
        heads = {}

        def rope(b, H, L, t, free):
            i, u, f = Tb.take()
            j, w, f2 = Tb.take()
            v1 = tt(u[:, :], P[b][:, :], COS[:, :], ALU.mult, t, f, k_cos)
            v2 = tt(w[0:64, :], P[b][64:128, :], SIN[64:128, :], ALU.mult, f2, k_sin)
            v3 = tt(w[64:128, :], P[b][0:64, :], SIN[0:64, :], ALU.mult)
            pfree[b] = [v3]
            v = tt(u[:, :], u[:, :], w[:, :], ALU.add, v1, v2, v3)
            Tb.free[j] = [v]
            r = split(H[:, :], L[:, :], u[:, :], v, free)
            Tb.free[i] = r
            return r

        def project(h):
            q = QR[h % 2]
            if h == 0:
                tq, tk, tv = feature_major_abreast([0, 1, 7], XH, XL, xtok)
                rq = rope(0, q[0], q[1], tq, qr_free[h % 2])
                rk = rope(1, q[2], q[3], tk, qr_free[h % 2])
                bv = 7
            else:
                tq = feature_major(0, XH, XL, xtok)
                rq = rope(0, q[0], q[1], tq, qr_free[h % 2])
                tk = feature_major(1, XH, XL, xtok)
                rk = rope(1, q[2], q[3], tk, qr_free[h % 2])
                tv = feature_major(0, XH, XL, xtok)
                bv = 0
            i, u, f = Tb.take()
            a = copy(u[:, :], P[bv][:, :], tv, f)
            pfree[bv] = [a]
            t = feature_major(1, XH, XL, xtok)
            bank, free = take(7)
            for c in range(4):
                tv = turned(bank[:, 128 * c:128 * c + 128], u[:, 128 * c:128 * c + 128], a, free)
            Tb.free[i] = [tv]
            b4 = bank[:, :].rearrange("p (b c) -> p b c", b=4)
            c = 8 * (h % 2)
            v = reduce(st[:, c:c + 4], b4, ALU.add, tv)
            v = ts(st[:, c + 4:c + 8], st[:, c:c + 4], -1.0 / 128, None, ALU.mult, None, v)
            i, u, f = Tb.take()
            u4 = u[:, :].rearrange("p (b c) -> p b c", b=4)
            v = tt(u4, b4, st[:, c + 4:c + 8].unsqueeze(2).to_broadcast([128, 4, 128]), ALU.add, v, f)
            pfree[7] = [v]
            rv = split(VR[h % 2][0][:, :, :], VR[h % 2][1][:, :, :], u4, v, vr_free[h % 2])
            Tb.free[i] = rv
            i, sg, f = Tb.take()
            a = act(sg[:, :], P[1][:, :], ACT.Silu, t, f)
            pfree[1] = [a]
            kd = dma(f"dm{h % 2}", DM[h % 2][:, :], dmat[:, T * h:T * h + T], dm_free[h % 2])
            heads[h] = (rq + rk, rv, i, sg, a, kd)

        def retain():
            sr_free = []
            sb = Banks([2, 3])
            ending = None

            def normal(h, i, y, part):
                def end():
                    _, free = take(6)
                    t = spread(6, part, free)
                    v = tt(y[:, :], y[:, :], P[6][:, :], ALU.mult, t)
                    pfree[6] = [v]
                    r = split(RH[:, h, :], RL[:, h, :], y[:, :], v)
                    Tb.free[i] = r
                    rtok[h] = r
                return end

            for h in range(8):
                while h not in heads:
                    yield None
                qk, rv, gi, sg, ga, kd = heads[h]
                q = QR[h % 2]
                lows, pts = None, []
                for kb in range(4):
                    n = T - 128 * kb
                    b, bank, free = sb.next()
                    ks = slice(128 * kb, 128 * kb + 128)
                    mm(bank[:, 0:n], q[2][:, ks], q[0][:, 128 * kb:T], True, False, free, qk)
                    mm(bank[:, 0:n], q[2][:, ks], q[1][:, 128 * kb:T], False, False)
                    t = mm(bank[:, 0:n], q[3][:, ks], q[0][:, 128 * kb:T], False, True, last=True)
                    if lows:
                        lows()
                    i, u, f = Tb.take()
                    v = tt(u[:, 0:n], bank[:, 0:n], DM[h % 2][:, 0:n], ALU.mult, t, f, kd)
                    pfree[b] = [v]
                    s = slice(offs[kb], offs[kb + 1])
                    a = copy(SRH[:, s], u[:, 0:n], v, sr_free)

                    def lows(i=i, u=u, s=s, n=n, a=a):
                        w = tt(SRL[:, s], u[:, 0:n], SRH[:, s].bitcast(F32), ALU.subtract, a, sr_free)
                        Tb.free[i] = [w]
                        pts.append([a, w])
                    if kb == 0 and ending:
                        ending()
                    yield 3.6
                lows()
                qr_free[h % 2] = [t]
                dm_free[h % 2] = [v]
                yield 3.6
                bank, free = take(4)
                PE.wait(free, rv)
                vh, vl = VR[h % 2]
                for kb in range(4):
                    d = bank[:, 128 * kb:T]
                    s = slice(offs[kb], offs[kb + 1])
                    mm(d, vh[:, kb, :], SRH[:, s], kb == 0, False, pts[kb])
                    mm(d, vh[:, kb, :], SRL[:, s], False, False)
                    t = mm(d, vl[:, kb, :], SRH[:, s], False, kb == 3, last=kb == 3)
                sr_free = [t]
                vr_free[h % 2] = [t]
                j, sq, f = Tb.take()
                a = act(sq[:, :], bank[:, :], ACT.Square, t, f)
                v = tt(sg[:, :], bank[:, :], sg[:, :], ALU.mult, ga, a)
                pfree[4] = [a, v]
                yield 3.6
                bank, free = take(5)
                t = mm(bank[:, :], ones[:, :], sq[:, :], True, True, a, free, last=True)
                Tb.free[j] = [t]
                ending = normal(h, gi, sg, inverse_root(5, 1.0 / 128, t))
                yield 3.6
            ending()

        project(0)
        for k in range(8):
            v = stt(hT[:, k, :], hT[:, k, :], GF[:, k:k + 1], P[3][:, :], ALU.mult, ALU.mult, t_r1, h_read)
        pfree[3] = [v]
        h_tok = v
        beside(retain())
        for h in range(1, 8):
            project(h)

        CH = at("CH", F + 64, [128, 8, T], F32R)
        CL = at("CL", F + 80, [128, 8, T], F32R)
        U = [at(f"UC{i}", F + 96 + 2.0625 * i, [128, 516], F32) for i in range(2)]
        MG = at("MG", F + 16, [128, 8, T], F32)
        mgt = [None] * 8
        ctok = []
        uf = [[], []]
        for m in range(8):
            bb, bc, bu = ((0, 1, 7), (2, 3, 4), (0, 1, 5))[0 if m == 0 else 2 - m % 2]
            tb_ = feature_major(bb, XH, XL, xtok)
            tc = feature_major(bc, XH, XL, xtok)
            i, c, f = Tb.take()
            a = copy(c[:, :], P[bc][:, :], tc, f)
            pfree[bc] = [a]
            tu = feature_major(bu, XH, XL, xtok)
            if m == 0:
                finish_side()
                over = [(PE.sem, PE.n), (DVE.sem, DVE.n), (SC.sem, SC.n)]
                DVE.wait(over)
                SC.wait(over)
                uz = [vset(U[i][:, 0:2], 0.0) for i in range(2)]
            u = U[m % 2]
            v = tt(u[:, 2:514], P[bu][:, :], c[:, :], ALU.mult, tu, a, uf[m % 2], uz)
            pfree[bu] = [v]
            v = ts(c[:, :], u[:, 0:512], CW[:, m:m + 1], None, ALU.mult, None, v)
            v = stt(c[:, :], u[:, 1:513], CW[:, 8 + m:9 + m], c[:, :], ALU.mult, ALU.add, v)
            v = stt(c[:, :], u[:, 2:514], CW[:, 16 + m:17 + m], c[:, :], ALU.mult, ALU.add, v)
            uf[m % 2] = [v]
            v = tt(c[:, :], P[bb][:, :], c[:, :], ALU.mult, v, tb_)
            pfree[bb] = [v]
            r = split(CH[:, m, :], CL[:, m, :], c[:, :], v)
            Tb.free[i] = r
            ctok.append(r)

        def gate(b):
            t = feature_major(b, XH, XL, xtok)
            i, sg, f = Tb.take()
            a = act(sg[:, :], P[b][:, :], ACT.Sigmoid, t, f)
            pfree[b] = [a]
            return i, sg, a

        def merge(m):
            b = 4 * (m % 2)
            ia, sa, aa = gate(b)
            if m == 7:
                ib, sb_, ab = gate(b + 2)
                x_read = [(PE.sem, PE.n)]
                for n in range(7):
                    merged(n, x_read)
            t = feature_major(b + 1, RH, RL, rtok)
            v1 = tt(MG[:, m, :], P[b + 1][:, :], sa[:, :], ALU.mult, t, aa)
            pfree[b + 1] = [v1]
            Tb.free[ia] = [v1]
            if m < 7:
                ib, sb_, ab = gate(b + 2)
            t = feature_major(b + 3, CH, CL, ctok)
            v = tt(sb_[:, :], P[b + 3][:, :], sb_[:, :], ALU.mult, t, ab)
            pfree[b + 3] = [v]
            mgt[m] = tt(MG[:, m, :], MG[:, m, :], sb_[:, :], ALU.add, v, v1)
            Tb.free[ib] = [mgt[m]]
            if m == 7:
                merged(7, x_read)

        gtok = []

        def merged(m, x_read):
            gtok.append(split(XH[:, m, :], XL[:, m, :], MG[:, m, :], mgt[m], x_read))

        for m in range(7):
            merge(m)
        merge(7)
        rms = Rms(4)
        hb = Banks([0, 1, 2, 3])
        for m in range(8):
            b = m % 4
            if m == 0:
                ts3 = feature_major_abreast([0, 1, 2], XH, XL, gtok)
            t = ts3[m] if m < 3 else feature_major(b, XH, XL, gtok)
            v = stt(hT[:, m, :], P[b][:, :], GT_M[:, m:m + 1], hT[:, m, :], ALU.mult, ALU.add, t)
            pfree[b] = [v]
            rms.add(m, hT[:, m, :], v)

        split_ahead()
        factor = rms.end(5)
        everyone()
        xtok = norm_split(hT, factor, gmod[:, 8:16], SH_F, 5)
        FH = at("FH", F + 16, [128, 11, T], F32R)
        FL = at("FL", F + 38, [128, 11, T], F32R)
        NF = 22
        FHb = at("FHb", F + 60, [128, 11, T], F32R)
        FLb = [at(f"FLb{i}", F + 82 + 2 * i, [128, 1, T], F32R) for i in range(9)]
        ftok = []

        def fpart(k):
            if k < 11:
                return FH[:, k, :], FL[:, k, :]
            if k - 11 < 9:
                return FHb[:, k - 11, :], FLb[k - 11][:, 0, :]
            return FHb[:, k - 11, :], tail[k - 20]

        tail = []
        for _ in range(2):
            i, t_, f = Tb.take()
            tail.append((i, f))
        tl = [at(f"TL{n}", 92 + 2 * i, [128, T], F32R) for n, (i, f) in enumerate(tail)]
        tl_free = [f for _, f in tail]
        keep = sorted(i for i, _ in tail)
        rest = [i for i in range(7) if i not in keep]
        sub = Slots([Tb.bufs[i] for i in rest])
        sub.free = [Tb.free[i] for i in rest]
        tail = [tl[0][:, :], tl[1][:, :]]
        for m in range(NF):
            b = 2 * (m % 2)
            if m == 0:
                t3 = feature_major_abreast([0, 1, 2], XH, XL, xtok)
            t = t3[2 * m] if m < 2 else feature_major(b, XH, XL, xtok)
            i, g_, f = sub.take()
            a = act(g_[:, :], P[b][:, :], ACT.Silu, t, f)
            pfree[b] = [a]
            t = t3[1] if m == 0 else feature_major(b + 1, XH, XL, xtok)
            v = tt(g_[:, :], P[b + 1][:, :], g_[:, :], ALU.mult, t, a)
            pfree[b + 1] = [v]
            H, L = fpart(m)
            r = split(H, L, g_[:, :], v, tl_free)
            sub.free[i] = r
            ftok.append(r)
        n = 0
        for i, f in zip(rest, sub.free):
            Tb.free[i] = f
        rms = Rms(4)
        for m in range(8):
            bank, free = take(m % 4)
            PE.wait(free)
            for k in range(NF):
                if n % 8 == 0:
                    unit = next_unit()
                H, L = fpart(k)
                PE.wait(ftok[k])
                t = tile(bank, unit, n % 8, H, L, k == 0, k == NF - 1, last=k == NF - 1)
                n += 1
            v = stt(hT[:, m, :], bank[:, :], GT_F[:, m:m + 1], hT[:, m, :], ALU.mult, ALU.add, t)
            pfree[m % 4] = [v]
            rms.add(m, hT[:, m, :], v)

        r, s_ = rms.end(5)
        ot = out.rearrange("(k p) t -> p k t", p=128)
        last = []
        for k in range(8):
            v = stt(hT[:, k, :], hT[:, k, :], GE[:, k:k + 1], r[:, :], ALU.mult, ALU.mult, s_)
            last.append(dma(f"o{k % 4}", ot[:, k, :], hT[:, k, :], v))
        SP.wait(last)

        block = ctx.enter_context(nc.Block())

        @block.sync
        def _(e):
            SP.play(e)

        @block.tensor
        def _(e):
            PE.play(e)

        @block.vector
        def _(e):
            DVE.play(e)

        @block.scalar
        def _(e):
            SC.play(e)

        @block.gpsimd
        def _(e):
            GP.play(e)


def feature_units(w):
    k, n = w.shape
    return w.reshape(k // 128, 128, n // 128, 128).transpose(2, 1, 0, 3).reshape(n // 128, 128, k)


def columns(g):
    return g.reshape(-1, 128).T


def constants():
    i = np.arange(128)[:, None]
    j = np.arange(512)[None, :]
    d = i + 384 - j
    count = ((d >= 0) & (d <= 128)).astype(np.float32)
    count += (d >= 0) & (d % 4 == 0)
    count += (d >= 0) & (d % 16 == 0)
    c = np.zeros((128, 1793), np.float32)
    c[:, 0:128] = np.eye(128)
    c[:, 128:256] = np.arange(128)[None, :]
    c[:, 256:768] = count
    c[:, 768:1280] = np.where(count > 0, 0.0, NEG)
    c[:, 1280:1792] = np.where(d >= 0, 0.0, NEG)
    inv = 1.0 / (np.float32(10000.0) ** (np.arange(0, 128, 2, dtype=np.float32) / np.float32(128)))
    c[:, 1792] = np.concatenate([inv, inv])
    lg = np.log(1.0 - 2.0 ** (-5.0 - np.arange(8)))
    rel = np.arange(512)[None, :] - np.arange(128)[:, None]
    dm = np.where(rel[None] >= 0, np.exp(lg[:, None, None] * np.maximum(rel, 0)[None]), 0.0) * 128 ** -0.5
    dm = dm.transpose(1, 0, 2).reshape(128, 8 * 512).astype(np.float32)
    slope = 2.0 ** -np.arange(1, 9, dtype=np.float32)[:, None]
    t = np.arange(512, dtype=np.float32)[None, :]
    aug = np.stack([-slope * t, 0 * slope * t, slope * t, 0 * slope * t], axis=1).astype(np.float32)
    return c, dm, aug


def kernel(**inputs):
    import concourse.bacc as bacc
    from concourse.bass_utils import run_bass_kernel_spmd as run

    a = {k: np.asarray(v) for k, v in inputs.items()}
    w = a["w_in"][0]
    fq, fk, fv, ff = w[:, 0:512], w[:, 512:1024], w[:, 1024:1536], w[:, 1536:1544]
    dq, dk, dv = w[:, 1544:2056], w[:, 2056:2568], w[:, 2568:3080]
    col = lambda m, h: m[:, 128 * h:128 * h + 128]
    parts = [feature_units(np.pad(ff, ((0, 0), (0, 120))))]
    for trio in ((fq, fk, fv), (dq, dk, dv)):
        for g in range(4):
            parts += [feature_units(col(m, g)) for m in trio]
    parts += [feature_units(a["w_out"][0]), feature_units(a["peer_wq"][0])]
    w2 = a["w_in_2"][0]
    q, k, v, gr, b, c, u, ga, gb = (w2[:, 1024 * i:1024 * i + 1024] for i in range(9))
    for h in range(8):
        parts += [feature_units(col(m, h)) for m in (q, k, v, gr)]
    for h in range(8):
        parts += [feature_units(col(m, h)) for m in (b, c, u)]
    ro, co = a["ret_w_out_2"][0], a["conv_w_out_2"][0]
    for h in range(8):
        order = (ga, gb, ro, co) if h == 7 else (ga, ro, gb, co)
        parts += [feature_units(col(m, h)) for m in order]
    parts.append(feature_units(a["mix_w_out_2"][0]))
    for h in range(22):
        parts += [feature_units(col(a["ffn_w_gate_2"][0], h)), feature_units(col(a["ffn_w_up_2"][0], h))]
    down = feature_units(a["ffn_w_down_2"][0])
    down = down.reshape(8, 128, 22, 128).transpose(0, 2, 1, 3).reshape(22, 8, 128, 128)
    parts.append(down.transpose(0, 2, 1, 3).reshape(22, 128, 1024))
    wts = np.concatenate(parts)
    ut = np.ascontiguousarray(a["peer_u"][0].reshape(128, 128, 8, 128).transpose(1, 3, 2, 0)).reshape(128, 128, 1024)
    vt = np.ascontiguousarray(a["peer_v"][0].reshape(128, 128, 1024).transpose(1, 0, 2))
    skt = a["peer_subkeys"][0].reshape(16, 128, 128).transpose(2, 0, 1).reshape(128, 2048)
    small = np.zeros((128, 144), np.float32)
    for n, name in enumerate(("norm1_g", "norm2_g", "normf_g", "norm_mix_g_2", "norm_ffn_g_2", "final_norm_g_2")):
        small[:, 8 * n:8 * n + 8] = columns(a[name])
    small[:, 48:96] = columns(a["ada_b_2"])
    small[:, 96:120] = columns(a["conv_w_2"])
    small[:, 120:128] = columns(a["c_2"])
    small[0:8, 128] = a["b_forget"][0]
    cst, dmat, augd = constants()
    feeds = {
        "x": a["x"][0].T, "wts": wts, "ut": ut, "vt": vt, "skt": skt, "small": small, "cst": cst,
        "dmat": dmat, "augd": augd, "pos": a["positions_2"][0], "adaw": a["ada_w_2"][0].reshape(8, 128, 6144),
    }
    feeds = {n: np.ascontiguousarray(v) for n, v in feeds.items()}
    nc = bacc.Bacc("TRN2", target_bir_lowering=False, num_devices=1)
    args = [nc.dram_tensor(n, v.shape, mybir.dt.from_np(v.dtype), kind="ExternalInput").ap()
            for n, v in feeds.items()]
    out = nc.dram_tensor("out", (1024, T), F32, kind="ExternalOutput").ap()
    build_program(nc, *args, out)
    r = run(nc, [feeds], core_ids=[0])
    return np.ascontiguousarray(r.results[0]["out"].T)[None]
```

```python
from contextlib import ExitStack

import numpy as np
import concourse.bass as bass
from concourse import mybir

F32 = mybir.dt.float32
F32R = mybir.dt.float32r
BF16 = mybir.dt.bfloat16
I32 = mybir.dt.int32
U32 = mybir.dt.uint32
ALU = mybir.AluOpType
ACT = mybir.ActivationFunctionType
AX = mybir.AxisListType

T = 512
FAR = 1e30
LOWEST = -3.0e38
NRAW = 6
NW = 4
W_BLOCK1 = 49
W_BLOCK2 = 162
EPS = 1e-6
ON_POOL = ((0, W_BLOCK1 + 96), (W_BLOCK1 + 258, W_BLOCK1 + 288))


class Queue:

    def __init__(self, sem):
        self.sem, self.n, self.ops, self.seen = sem, 0, [], {}

    def wait(self, *tokens):
        for t in tokens:
            if t is None:
                continue
            if isinstance(t, list):
                self.wait(*t)
                continue
            sem, value = t
            if self.seen.get(sem.num, 0) < value:
                self.seen[sem.num] = value
                self.ops.append(lambda e, s=sem, v=value: e.wait_ge(s, v))

    def quiet(self, fn, *tokens):
        self.wait(*tokens)
        self.ops.append(fn)

    def do(self, fn, *tokens):
        self.wait(*tokens)
        self.n += 1
        self.ops.append(lambda e: fn(e).then_inc(self.sem, 1))
        return (self.sem, self.n)

    def play(self, e):
        for op in self.ops:
            op(e)


class Lane:

    def __init__(self, sem):
        self.sem, self.n = sem, 0


class Slots:

    def __init__(self, bufs):
        self.bufs, self.free, self.i = list(bufs), [[] for _ in bufs], -1

    def take(self):
        assert any(f is not None for f in self.free)
        self.i = (self.i + 1) % len(self.bufs)
        while self.free[self.i] is None:
            self.i = (self.i + 1) % len(self.bufs)
        free, self.free[self.i] = self.free[self.i], None
        return self.i, self.bufs[self.i], free


def build_program(nc, x, wts, ut, vt, skt, small, cst, dmat, augd, pos, adaw, out):
    ctx = ExitStack()
    with ctx:
        def sem(name):
            return ctx.enter_context(nc.semaphore(name))

        base = -(-nc.sbuf_base // 64) * 64

        def at(name, kb, shape, dt):
            return nc.alloc_sbuf_tensor_at(name, shape, dt, offset=base + int(kb * 1024))

        PE, DVE, SC, GP = (Queue(sem(n)) for n in ("s_pe", "s_dve", "s_act", "s_pool"))
        SP = Queue(None)
        lanes = {}

        def dma(name, dst, src, *tokens):
            if name not in lanes:
                lanes[name] = Lane(sem("d_" + name))
            lane = lanes[name]
            if lane.n:
                SP.wait((lane.sem, 16 * lane.n))
            SP.wait(*tokens)
            lane.n += 1
            SP.ops.append(lambda e: e.dma_start(dst, src).then_inc(lane.sem, 16))
            return (lane.sem, 16 * lane.n)

        def copy(dst, src, *tokens, scale=None):
            if scale is None:
                return SC.do(lambda e: e.activation(dst, src, ACT.Copy), *tokens)
            return SC.do(lambda e: e.activation(dst, src, ACT.Copy, scale=scale), *tokens)

        def act(dst, src, func, *tokens, **kw):
            return SC.do(lambda e: e.activation(dst, src, func, **kw), *tokens)

        def tt(dst, a, b, op, *tokens):
            return DVE.do(lambda e: e.tensor_tensor(dst, a, b, op), *tokens)

        def ts(dst, a, s1, s2, op0, op1, *tokens):
            if op1 is None:
                return DVE.do(lambda e: e.tensor_scalar(dst, a, s1, None, op0), *tokens)
            return DVE.do(lambda e: e.tensor_scalar(dst, a, s1, s2, op0, op1), *tokens)

        def stt(dst, a, s, b, op0, op1, *tokens):
            return DVE.do(lambda e: e.scalar_tensor_tensor(out=dst, in0=a, scalar=s, in1=b,
                                                           op0=op0, op1=op1), *tokens)

        def mm(dst, lhs, rhs, start, stop, *tokens, last=False, skip=False):
            def fn(e):
                return e.matmul(dst, lhs, rhs, start=start, stop=stop, skip_group_check=skip)
            return PE.do(fn, *tokens) if last else PE.quiet(fn, *tokens)

        def vcopy(dst, src, *tokens):
            return DVE.do(lambda e: e.tensor_copy(dst, src), *tokens)

        def vset(dst, value, *tokens):
            return DVE.do(lambda e: e.memset(dst, value), *tokens)

        def gp(fn, *tokens):
            return GP.do(fn, *tokens, (GP.sem, GP.n) if GP.n else None)

        def recip(dst, src, *tokens):
            return DVE.do(lambda e: e.reciprocal(dst, src), *tokens)

        def reduce(dst, src, op, *tokens):
            return DVE.do(lambda e: e.tensor_reduce(dst, src, AX.X, op), *tokens)

        def turned(dst, src, *tokens):
            return PE.do(lambda e: e.transpose(dst, src, ident[:, :]), *tokens)

        def split(H, L, src, *tokens, scale=None):
            a = copy(H, src, *tokens, scale=scale)
            if scale is None:
                return [a, tt(L, src, H.bitcast(F32), ALU.subtract, a, *tokens)]
            return [a, stt(L, src, scale, H.bitcast(F32), ALU.mult, ALU.subtract, a, *tokens)]

        RAW = [at(f"raw{i}", 4 * i, [128, 1024], F32) for i in range(NRAW)]
        WH = [at(f"wh{i}", 24 + 4 * i, [128, 1024], F32R) for i in range(NW)]
        WL = [at(f"wl{i}", 40 + 4 * i, [128, 1024], F32R) for i in range(NW)]
        ident = at("ident", 56, [128, 128], F32)
        iota = at("iota", 56.5, [128, 128], F32)
        ones = at("ones", 57, [128, 128], F32)
        identb = at("identb", 57.5, [128, 128], BF16)
        sm = at("sm", 57.75, [128, 144], F32)
        csil = at("csil", 58.3125, [128, 8], F32)
        mod = at("mod", 58.375, [128, 48], F32)
        gmod = at("gmod", 58.5625, [128, 16], F32)
        st = at("st", 58.625, [128, 64], F32)
        invf = at("invf", 58.875, [128, 1], F32)
        XH = at("XH", 60, [128, 8, T], F32R)
        XL = at("XL", 76, [128, 8, T], F32R)
        Tb = Slots([at(f"T{i}", 92 + 2 * i, [128, T], F32) for i in range(7)])
        F = 106
        P = [ctx.enter_context(nc.psum_tensor(f"P{i}", [128, T], F32)) for i in range(8)]
        pfree = [[] for _ in range(8)]

        def take(b):
            free, pfree[b] = pfree[b], None
            assert free is not None, b
            return P[b], free

        class Banks:
            def __init__(self, ids):
                self.ids, self.i = ids, -1

            def next(self):
                self.i = (self.i + 1) % len(self.ids)
                b = self.ids[self.i]
                return (b, *take(b))

        def everyone():
            now = [(q.sem, q.n) for q in (PE, DVE, SC, GP) if q.n]
            for q in (PE, DVE, SC, GP, SP):
                q.wait(*now)

        stream = ([wts[i] for i in range(W_BLOCK1)] + [ut[i] for i in range(128)]
                  + [vt[i] for i in range(128)] + [wts[W_BLOCK1 + i] for i in range(W_BLOCK2)])
        raw_tok, split_tok, used_tok = {}, {}, {}
        high_tok = {}
        state = {"dma": 0, "high": 0, "split": 0, "unit": 0}

        def load_to(n):
            while state["dma"] < min(n, len(stream)):
                i = state["dma"]
                free = split_tok.get(i - NRAW)
                raw_tok[i] = dma(f"w{i % NRAW}", RAW[i % NRAW][:, :], stream[i], free)
                state["dma"] += 1

        def given_back(i):
            return i < NW or i - NW in used_tok

        def high_to(n):
            while state["high"] < min(n, len(stream)) and given_back(state["high"]):
                i = state["high"]
                load_to(i + 1)
                high_tok[i] = copy(WH[i % NW][:, :], RAW[i % NRAW][:, :], raw_tok[i], used_tok.get(i - NW))
                state["high"] += 1

        def split_to(n):
            while state["split"] < min(n, len(stream)) and given_back(state["split"]):
                i = state["split"]
                high_to(i + 1)
                s = i % NW
                on = gp if any(a <= i < b for a, b in ON_POOL) else DVE.do
                low = on(lambda e, i=i, s=s: e.tensor_tensor(WL[s][:, :], RAW[i % NRAW][:, :],
                                                             WH[s][:, :].bitcast(F32), ALU.subtract),
                         high_tok[i], used_tok.get(i - NW))
                split_tok[i] = [high_tok[i], low]
                load_to(i + NRAW)
                state["split"] += 1

        def split_ahead():
            high_to(state["unit"] + NW)
            split_to(state["unit"] + NW)

        def next_unit():
            i = state["unit"]
            state["unit"] += 1
            high_to(i + NW)
            split_to(i + NW - 1)
            assert i in split_tok
            PE.wait(split_tok[i])
            return i, WH[i % NW], WL[i % NW]

        side = {"work": None, "credit": 0.0}

        def beside(work):
            side["work"], side["credit"] = work, 0.0

        def tick():
            if side["work"] is None:
                return
            side["credit"] += 1.0
            while side["credit"] > 0:
                cost = next(side["work"], "end")
                if cost == "end":
                    side["work"] = None
                    return
                if cost is None:
                    side["credit"] = 0.0
                    return
                side["credit"] -= cost

        def finish_side():
            while side["work"] is not None:
                if next(side["work"], "end") == "end":
                    side["work"] = None

        def tile(bank, unit, c, H, L, start, stop, last=False, back=7):
            i, wh, wl = unit
            w = slice(c * 128, c * 128 + 128)
            mm(bank[:, :], wh[:, w], H, start, False)
            mm(bank[:, :], wh[:, w], L, False, False)
            t = mm(bank[:, :], wl[:, w], H, False, stop, last=last or c == back)
            if c == back:
                used_tok[i] = t
            return t

        def feature_major(b, H, L, toks):
            bank, free = take(b)
            unit = next_unit()
            PE.wait(free)
            for k in range(8):
                PE.wait(toks[k])
                t = tile(bank, unit, k, H[:, k, :], L[:, k, :], k == 0, k == 7)
                tick()
            return t

        def feature_major_abreast(bs, H, L, toks):
            banks = [take(b) for b in bs]
            units = [next_unit() for _ in bs]
            done = [None] * len(bs)
            for k in range(8):
                PE.wait(toks[k])
                for n, (bank, free) in enumerate(banks):
                    PE.wait(free)
                    done[n] = tile(bank, units[n], k, H[:, k, :], L[:, k, :], k == 0, k == 7)
            return done

        CNT = at("CNT", F + 96, [128, T], F32)
        MDB = at("MDB", F + 98, [128, T], BF16)
        MCB = at("MCB", F + 99, [128, T], BF16)
        CS = at("CS", F + 48, [128, 1793], F32)
        XIN = at("XIN", F, [128, 8, T], F32)
        xt = x.rearrange("(k p) t -> p k t", p=128)
        k_x = [dma(f"x{j}", XIN[:, 2 * j:2 * j + 2, :], xt[:, 2 * j:2 * j + 2, :]) for j in range(4)]
        k_s = dma("c1", sm[:, :], small)
        k_c = dma("c0", CS[:, 0:256], cst[:, 0:256])
        load_to(3)
        k_c2 = dma("c0", CS[:, 256:1793], cst[:, 256:1793])
        AD = at("AD", F + 16, [8, T], F32)
        k_ad = dma("c2", AD[:, :], augd)
        load_to(NRAW)
        d1 = vset(ones[:, :], 1.0)
        vcopy(ident[:, :], CS[:, 0:128], k_c)
        vcopy(identb[:, :], CS[:, 0:128])
        k_k = vcopy(iota[:, :], CS[:, 128:256])
        PE.wait(k_k)
        G1, G2, GF, GM, GN, GE = (sm[:, 8 * i:8 * i + 8] for i in range(6))
        ADB = sm[:, 48:96]
        CW = sm[:, 96:120]
        CV = sm[:, 120:128]
        BF = sm[0:8, 128:129]

        def diagonal(b, col, p):
            i, q, f = Tb.take()
            v = []
            for c in range(4):
                s = slice(128 * c, 128 * c + 128)
                v.append(DVE.do(lambda e, c=c, s=s: e.tensor_tensor_reduce(
                    out=q[:, s], in0=P[b][:, s], in1=ident[:, :], scale=1.0, scalar=0.0,
                    op0=ALU.mult, op1=ALU.add, accum_out=st[:, col + c:col + c + 1]), p, f))
            pfree[b] = [v[-1]]
            return i, q, v

        def diagonals(q, col, tok):
            return [ts(q[:, 128 * c:128 * c + 128], ident[:, :], st[:, col + c:col + c + 1], None,
                       ALU.mult, None, tok) for c in range(4)]

        def spread(dst, part, *free):
            i, q, v = part
            t = mm(P[dst][:, :], ones[:, :], q[:, :], True, True, v, *free, last=True)
            Tb.free[i] = [t]
            return t

        def inverse_root(b, scale, p):
            i, q, v = diagonal(b, 48, p)
            v = ts(st[:, 52:56], st[:, 48:52], scale, EPS, ALU.mult, ALU.add, v)
            v = recip(st[:, 56:60], st[:, 52:56], v)
            a = act(st[:, 60:64], st[:, 56:60], ACT.Sqrt, v)
            return i, q, diagonals(q, 60, a)

        class Rms:

            def __init__(self, b, groups=(7, 1), gain=None):
                self.b, self.groups, self.gain = b, groups, gain
                self.k, self.n, self.g = 0, 0, 0
                self.acc, self.new, self.ready = None, None, None
                self.bank, self.free = take(b)

            def product(self):
                if self.ready:
                    i, sq, a = self.ready
                    self.p = mm(self.bank[:, :], ones[:, :], sq[:, :], self.g == 0,
                                self.g == len(self.groups) - 1, a, self.free, d1, last=True)
                    Tb.free[i] = [self.p]
                    self.g += 1
                    self.ready = None

            def settle(self):
                if self.new:
                    i, sq, a = self.new
                    self.new = None
                    if self.acc is None:
                        self.acc = (i, sq, a)
                    else:
                        j, acc, b = self.acc
                        v = tt(acc[:, :], acc[:, :], sq[:, :], ALU.add, a, b)
                        Tb.free[i] = [v]
                        self.acc = (j, acc, v)
                    self.n += 1
                    if self.n == self.groups[self.k]:
                        self.ready, self.acc, self.n = self.acc, None, 0
                        self.k += 1

            def add(self, k, src, tok):
                i, sq, sf = Tb.take()
                kw = {} if self.gain is None else {"scale": self.gain[:, k:k + 1]}
                a = act(sq[:, :], src, ACT.Square, tok, sf, **kw)
                self.product()
                self.settle()
                self.new = (i, sq, a)

            def total(self):
                self.product()
                self.settle()
                self.product()
                return self.p

            def end(self, b):
                part = inverse_root(self.b, 1.0 / 1024, self.total())
                bank, free = take(b)
                return bank, spread(b, part, free)

        def norm_split(src, factor, gain, shift, b, *more):
            r, s = factor
            outt = []
            pend = None
            for k in range(8):
                i, t, f = Tb.take()
                v = last = stt(t[:, :], src[:, k, :], gain[:, k:k + 1], r[:, :], ALU.mult, ALU.mult, s, f, k_s, *more)
                if shift is not None:
                    v = ts(t[:, :], t[:, :], shift[:, k:k + 1], None, ALU.add, None, v)
                if pend:
                    pend()
                a = copy(XH[:, k, :], t[:, :], v)

                def pend(k=k, i=i, t=t, a=a):
                    w = tt(XL[:, k, :], t[:, :], XH[:, k, :].bitcast(F32), ALU.subtract, a)
                    Tb.free[i] = [w]
                    outt.append([a, w])
            pend()
            pfree[b] = [last]
            return outt

        xin_t = [k_x[k // 2] for k in range(8)]
        AR = [at(f"AR{i}", F + 20 + 2 * i, [8, T], F32R) for i in range(2)]
        adr = nc.dram_tensor("adram", [2, 8, T], F32, kind="Internal").ap()
        v0 = vset(AR[1][:, :].bitcast(F32), 0.0)
        ad_tok = [dma("ad0", adr[1], AR[1][:, :].bitcast(F32), v0)]
        rms = Rms(0)
        for k in range(8):
            rms.add(k, XIN[:, k, :], xin_t[k])
        v = vcopy(AR[0][:, :], AD[:, :], k_ad)
        ad_tok.append(dma("ad1", adr[0], AR[0][:, :].bitcast(F32), v))
        split_to(3)
        xtok = norm_split(XIN, rms.end(1), G1, None, 1)
        vcopy(CNT[:, :], CS[:, 256:768], k_c2)
        vcopy(MDB[:, :], CS[:, 768:1280])
        vcopy(MCB[:, :], CS[:, 1280:1792])
        k_masks = vcopy(invf[:, :], CS[:, 1792:1793])

        CA = [at(f"CA{i}", F + 24 + 2 * i, [8, T], F32) for i in range(4)]
        CR = [at(f"CR{i}", F + 32 + 2 * i, [8, T], F32R) for i in range(2)]
        cd = nc.dram_tensor("cdram", [2, 8, T], F32, kind="Internal").ap()
        t_f, *first_qk = feature_major_abreast([4, 2, 3], XH, XL, xtok)
        cd_tok = []

        def forget():
            v = ts(CA[0][:, :], P[4][0:8, :], BF, None, ALU.add, None, t_f, k_s)
            pfree[4] = [v]
            v2 = stt(CA[1][:, :], CA[0][:, :], -1.0, CA[0][:, :], ALU.mult, ALU.min, v)
            a = act(CA[1][:, :], CA[1][:, :], ACT.Exp, v2)
            a = act(CA[2][:, :], CA[1][:, :], ACT.Ln, a, bias=1.0)
            v = stt(CA[3][:, :], CA[0][:, :], 0.0, CA[2][:, :], ALU.min, ALU.subtract, a)
            v0 = vset(CA[1][:, :], 1.0, a)
            v = DVE.do(lambda e: e.tensor_tensor_scan(CA[0][:, :], CA[1][:, :], CA[3][:, :], 0.0,
                                                      ALU.mult, ALU.subtract), v, v0)
            v = split(CR[0][:, :], CR[1][:, :], CA[0][:, :], v)
            for i in range(2):
                cd_tok.append(dma(f"cd{i}", cd[i], CR[i][:, :].bitcast(F32), v))

        PTH = at("PTH", F, [128, 4, T], F32R)
        PTL = at("PTL", F + 8, [128, 4, T], F32R)
        MH = at("MH", F + 16, [128, 8, T], F32R)
        ML = at("ML", F + 32, [128, 8, T], F32R)
        QK = [[at(f"QK{g}{i}", F + 48 + 16 * g + 4 * i, [128, 2, T], F32R) for i in range(4)] for g in range(2)]
        VV = [[at(f"VV{g}{i}", F + 80 + 4 * g + 2 * i, [128, 4, 128], F32R) for i in range(2)] for g in range(2)]
        fill = []
        for g in range(2):
            for i in range(4):
                fill.append(gp(lambda e, q=QK[g][i]: e.memset(q[64:128, :, :].bitcast(F32), 0.0), k_masks))
        ones_tok = [gp(lambda e, q=QK[g][i], one=one: e.memset(q[64:68, :, :].bitcast(F32), one), fill)
                    for g in range(2) for i, one in ((0, -1.0), (2, 1.0))]
        mtok = [[] for _ in range(8)]
        qk_tok, v_tok, qk_read, v_read = {}, {}, {}, {}
        tr = Banks([4, 5])
        owed = []
        ready = {"groups": 0}

        def dilated(g):
            return g < 4

        def place(g):
            return (g + 4) % 8

        def heads_in(g):
            q = QK[g % 2]
            toks = []
            for j in range(2):
                if g == 0:
                    b, t = 2 + j, first_qk[j]
                else:
                    b = j
                    t = feature_major(b, XH, XL, xtok)
                    if owed:
                        owed.pop()()
                before = qk_read[g - 2] if g >= 2 else k_masks
                for half in range(2):
                    toks += split(q[2 * j][0:64, half, :], q[2 * j + 1][0:64, half, :],
                                  P[b][64 * half:64 * half + 64, :], t, before, scale=None if j else -0.125)
                pfree[b] = toks[-4:]
            if g == 0:
                t = feature_major(0, XH, XL, xtok)
                i, u, f = Tb.take()
                a = copy(u[:, :], P[0][:, :], t, f)
                pfree[0] = [a]
            h0 = 2 * (g % 4)
            src, made = (adr, ad_tok) if dilated(g) else (cd, cd_tok)
            toks.append(dma("bq", q[0][64:66, :, :].bitcast(F32), src[:, h0:h0 + 2, :], made, ones_tok, before))
            toks.append(dma("bk", q[2][66:68, :, :].bitcast(F32), src[:, h0:h0 + 2, :], made, ones_tok, before))
            if g == 0:
                forget()
            qk_tok[g] = toks
            if g:
                t = feature_major(0, XH, XL, xtok)
                i, u, f = Tb.take()
                a = copy(u[:, :], P[0][:, :], t, f)
                pfree[0] = [a]

            def token_major():
                tb, bank, free = tr.next()
                for c in range(4):
                    t = turned(bank[:, 128 * c:128 * c + 128], u[:, 128 * c:128 * c + 128], a, free)
                Tb.free[i] = [t]
                v_tok[g] = split(VV[g % 2][0][:, :, :], VV[g % 2][1][:, :, :],
                                 bank[:, :].rearrange("p (b c) -> p b c", b=4), t,
                                 v_read[g - 2] if g >= 2 else k_masks)
                pfree[tb] = v_tok[g]
            owed.append(token_major)
            ready["groups"] = g + 1

        def attend():
            steps = [(g, h, qb) for g in range(8) for h in range(2) for qb in range(4)]
            sb = Banks([2, 3, 7])
            S, E, N, R, PT = {}, {}, {}, {}, {}
            pt_read = []

            def scores(n):
                g, h, qb = steps[n]
                q = QK[g % 2]
                kw = 128 * (qb + 1)
                b, bank, free = sb.next()
                qs = slice(qb * 128, qb * 128 + 128)
                PE.wait(free, qk_tok[g], fill)
                mm(bank[:, 0:kw], q[0][:, h, qs], q[2][:, h, 0:kw], True, False)
                mm(bank[:, 0:kw], q[0][:, h, qs], q[3][:, h, 0:kw], False, False)
                mm(bank[:, 0:kw], q[1][:, h, qs], q[2][:, h, 0:kw], False, False)
                mask = MDB if dilated(g) else MCB
                t = mm(bank[:, 0:kw], identb[:, :], mask[:, (3 - qb) * 128:T], False, True, last=True)
                qk_read[g] = [t]
                S[n] = (b, t)

            def soft(n):
                g, h, qb = steps[n]
                kw = 128 * (qb + 1)
                b, t = S[n]
                c = 4 * (n % 4)
                m = reduce(st[:, c:c + 1], P[b][:, 0:kw], ALU.min, t)
                i, pbuf, pf = Tb.take()
                kw_args = {} if dilated(g) else {"accum_out": st[:, c + 2:c + 3]}
                a = act(pbuf[:, 0:kw], P[b][:, 0:kw], ACT.Exp, m, pf, bias=st[:, c:c + 1], scale=-1.0, **kw_args)
                pfree[b] = [m, a]
                E[n] = (i, pbuf, a)

            def normal(n):
                g, h, qb = steps[n]
                kw = 128 * (qb + 1)
                i, pbuf, a = E[n]
                c = 4 * (n % 4)
                if dilated(g):
                    a = DVE.do(lambda e: e.tensor_tensor_reduce(
                        out=pbuf[:, 0:kw], in0=pbuf[:, 0:kw], in1=CNT[:, (3 - qb) * 128:T], scale=1.0,
                        scalar=0.0, op0=ALU.mult, op1=ALU.add, accum_out=st[:, c + 2:c + 3]), a)
                v = recip(st[:, c + 3:c + 4], st[:, c + 2:c + 3], a)
                v = ts(pbuf[:, 0:kw], pbuf[:, 0:kw], st[:, c + 3:c + 4], None, ALU.mult, None, v)
                N[n] = (i, pbuf, v)

            def turn(n):
                g, h, qb = steps[n]
                i, pbuf, v = N[n]
                b, bank, free = tr.next()
                for kb in range(qb + 1):
                    t = turned(bank[:, kb * 128:kb * 128 + 128], pbuf[:, kb * 128:kb * 128 + 128], v, free)
                Tb.free[i] = [t]
                src = bank[:, 0:128 * (qb + 1)].rearrange("p (k q) -> p k q", q=128)
                R[n] = (b, src, copy(PTH[:, 0:qb + 1, qb * 128:qb * 128 + 128], src, t, pt_read))

            def turn_low(n):
                g, h, qb = steps[n]
                b, src, a = R[n]
                d = (slice(None), slice(0, qb + 1), slice(qb * 128, qb * 128 + 128))
                v = tt(PTL[d], src, PTH[d].bitcast(F32), ALU.subtract, a, pt_read)
                pfree[b] = [v]
                PT[n] = [a, v]

            def values(n):
                nonlocal pt_read
                g, h, _ = steps[n]
                bank, free = take(6)
                PE.wait(free, PT[n - 3], PT[n - 2], PT[n - 1], PT[n], v_tok[g])
                vh, vl = VV[g % 2]
                for kb in range(4):
                    d = bank[:, kb * 128:T]
                    r = slice(kb * 128, T)
                    mm(d, vh[:, kb, :], PTH[:, kb, r], kb == 0, False)
                    mm(d, vh[:, kb, :], PTL[:, kb, r], False, False)
                    t = mm(d, vl[:, kb, :], PTH[:, kb, r], False, kb == 3, last=kb == 3)
                pt_read = [t]
                v_read[g] = [t]
                rows = slice(64 * h, 64 * h + 64)
                r = split(MH[rows, place(g), :], ML[rows, place(g), :], bank[rows, :], t, cd_tok)
                mtok[place(g)] += r
                pfree[6] = r

            ns = len(steps)
            for n in range(ns + 5):
                while n < ns and ready["groups"] <= steps[n][0]:
                    yield None
                if 0 <= n - 4 < ns:
                    turn_low(n - 4)
                if n < ns:
                    scores(n)
                if 0 <= n - 1 < ns:
                    soft(n - 1)
                if 0 <= n - 2 < ns:
                    normal(n - 2)
                yield 1.5
                if 0 <= n - 4 < ns and steps[n - 4][2] == 3:
                    values(n - 4)
                if 0 <= n - 3 < ns:
                    turn(n - 3)
                yield 1.4

        heads_in(0)
        PE.wait(k_masks)
        DVE.wait(k_masks)
        beside(attend())
        for g in range(1, 8):
            heads_in(g)

        owed.pop()()

        abreast = [(b, *take(b), next_unit()) for b in range(2)]
        for g in range(7):
            k = place(g)
            while len(mtok[k]) < 4:
                tick()
            PE.wait(mtok[k])
            for b, bank, free, unit in abreast:
                PE.wait(free)
                tile(bank, unit, k, MH[:, k, :], ML[:, k, :], g == 0, False, back=place(7))
                tick()
        finish_side()
        k = place(7)
        PE.wait(mtok[k])
        first_out = [tile(bank, unit, k, MH[:, k, :], ML[:, k, :], False, True, back=k)
                     for b, bank, free, unit in abreast]
        hT = at("hT", F, [128, 8, T], F32)
        hx = [dma(f"x{j}", hT[:, 2 * j:2 * j + 2, :], xt[:, 2 * j:2 * j + 2, :], mtok) for j in range(4)]
        rms = Rms(4)
        for m in range(8):
            t = first_out[m] if m < 2 else feature_major(m % 4, MH, ML, mtok)
            v = tt(hT[:, m, :], P[m % 4][:, :], hT[:, m, :], ALU.add, t, hx[m // 2])
            pfree[m % 4] = [v]
            rms.add(m, hT[:, m, :], v)
        split_ahead()
        factor = rms.end(5)
        everyone()
        xtok = norm_split(hT, factor, G2, None, 5)

        S = at("S", F + 16, [128, 16, 4, 128], F32)
        VAL = at("VAL", F + 48, [128, 4, 16, 16], F32)
        IDX = at("IDX", F + 52, [128, 4, 16, 16], U32)
        CSV = at("CSV", F + 56, [128, 4, 8, 16], F32)
        CIX = at("CIX", F + 58, [128, 4, 8, 16], U32)
        D1 = at("D1", F + 60, [128, 1024], F32)
        D2 = at("D2", F + 64, [128, 1024], F32)
        SKR = at("SKR", F + 68, [128, 2048], F32)
        SKH = at("SKH", F + 76, [128, 2048], F32R)
        SKL = at("SKL", F + 84, [128, 2048], F32R)
        QPH = [at(f"QPH{i}", F + 92 + 4 * i, [128, T], F32R) for i in range(2)]
        QPL = [at(f"QPL{i}", F + 94 + 4 * i, [128, T], F32R) for i in range(2)]
        k_sk = dma("c0", SKR[:, :], skt)
        sk = split(SKH[:, 0:1024], SKL[:, 0:1024], SKR[:, 0:1024], k_sk)
        sk += split(SKH[:, 1024:2048], SKL[:, 1024:2048], SKR[:, 1024:2048], k_sk)
        qfree = [[], []]
        stok = {}

        key_major = {}

        def key_scores(hp, qt):
            b = 4 + hp % 2
            bank, free = take(b)
            ks = slice(hp * 128, hp * 128 + 128)
            mm(bank[:, :], SKH[:, ks], QPH[hp % 2][:, :], True, False, free, qt, sk)
            mm(bank[:, :], SKL[:, ks], QPH[hp % 2][:, :], False, False)
            t = mm(bank[:, :], SKH[:, ks], QPL[hp % 2][:, :], False, True, last=True)
            qfree[hp % 2] = [t]
            i, u, f = Tb.take()
            a = copy(u[:, :], bank[:, :], t, f)
            pfree[b] = [a]
            key_major[hp] = i, u, a

        def token_scores(hp):
            i, u, a = key_major[hp]
            b = 6 + hp % 2
            bank, free = take(b)
            for tb in range(4):
                q = slice(tb * 128, tb * 128 + 128)
                t = turned(bank[:, q], u[:, q], a, free)
            Tb.free[i] = [t]
            a = copy(S[:, hp, :, :], bank[:, :].rearrange("p (b k) -> p b k", b=4), t)
            pfree[b] = [a]
            stok[hp] = a

        toptok = {}

        def top16(src, val, idx, tok):
            a = DVE.do(lambda e: e.max(val[:, 0:8], src), tok)
            b = DVE.do(lambda e: e.max_index(idx[:, 0:8], val[:, 0:8], src), a)
            c = DVE.do(lambda e: e.match_replace(src, val[:, 0:8], src, LOWEST), b)
            d = DVE.do(lambda e: e.max(val[:, 8:16], src), c)
            return DVE.do(lambda e: e.max_index(idx[:, 8:16], val[:, 8:16], src), d)

        def route():
            for hp in range(16):
                while hp not in stok:
                    yield None
                for tb in range(4):
                    toptok[hp, tb] = top16(S[:, hp, tb, :], VAL[:, tb, hp, :], IDX[:, tb, hp, :], stok[hp])
                    yield 2.3
            for tb in range(4):
                for h in range(8):
                    i, c, f = Tb.take()
                    c = c[:, 0:256]
                    v1 = VAL[:, tb, 2 * h, :].unsqueeze(2).to_broadcast([128, 16, 16])
                    v2 = VAL[:, tb, 2 * h + 1, :].unsqueeze(1).to_broadcast([128, 16, 16])
                    t = tt(c.rearrange("p (a b) -> p a b", a=16), v1, v2, ALU.add,
                           toptok[2 * h, tb], toptok[2 * h + 1, tb], f)
                    t = top16(c, CSV[:, tb, h, :], CIX[:, tb, h, :], t)
                    Tb.free[i] = [t]
                    toptok["c", tb, h] = t
                    yield 4.2

        GR = at("GR", F + 68, [128, 4, 128], F32)
        U1 = at("U1", F + 70, [128, 128], U32)
        AF = at("AF", F + 70.5, [128, 128], F32)
        IF = at("IF", F + 71, [128, 8, 16], F32)
        IS = at("IS", F + 71.5, [128, 2, 128], F32)
        IT = at("IT", F + 72.5, [128, 2, T], BF16)
        GT = at("GT", F + 74.5, [128, 3, T], BF16)
        IOT = at("IOT", F + 77.5, [128, 128, 4], BF16)
        GRT = at("GRT", F + 78.5, [128, 2, 128], F32)
        OE = [at(f"OE{i}", F + 79.5 + 2 * i, [128, 2, 128, 4], BF16) for i in range(3)]
        OM = [at(f"OM{i}", F + 85.5 + 3 * i, [128, 3, 128, 4], BF16) for i in range(2)]
        HID = Slots([at(f"HID{i}", F + 92.5 + 4 * i, [128, 2, T], F32) for i in range(2)])
        GS = [at(f"GS{i}", F + 16 + 16 * i, [128, 128, 32], F32) for i in range(2)]
        dg = nc.dram_tensor("gdram", [16, 128, 128, 32], F32, kind="Internal").ap()
        dh = nc.dram_tensor("hdram", [32, 128, 4, T], F32, kind="Internal").ap()
        dg_tok, dh_tok = [], {}

        def gates():
            ittok = []
            for tb in range(4):
                c = CSV[:, tb, :, :]
                gr = GR[:, tb, :].rearrange("p (h k) -> p h k", h=8)
                tops = [toptok["c", tb, h] for h in range(8)]
                v = tt(gr, c, CSV[:, tb, :, 0:1].to_broadcast([128, 8, 16]), ALU.subtract, tops)
                a = act(gr, gr, ACT.Exp, v)
                v = reduce(st[:, 32:40], gr, ALU.add, a)
                v = recip(st[:, 40:48], st[:, 32:40], v)
                vg = tt(gr, gr, st[:, 40:48].unsqueeze(2).to_broadcast([128, 8, 16]), ALU.mult, v)
                yield 3.0
                fin = []
                for p in range(2):
                    ci = CIX[:, tb, :, :].rearrange("p h k -> p (h k)")
                    if p == 0:
                        v = ts(U1[:, :], ci, 4, None, ALU.logical_shift_right, None)
                    else:
                        v = ts(U1[:, :], ci, 15, None, ALU.bitwise_and, None, v)
                    v1 = vcopy(AF[:, :], U1[:, :], v)
                    idv = IDX[:, tb, :, :].rearrange("p (h q) a -> p h q a", q=2)[:, :, p, :]
                    v2 = vcopy(IF[:, :, :], idv)
                    for hh in range(2):
                        d1v = D1[:, :].rearrange("p (s a) -> p s a", a=16)
                        v = tt(d1v, AF[:, 64 * hh:64 * hh + 64].unsqueeze(2).to_broadcast([128, 64, 16]),
                               iota[:, 0:16].unsqueeze(1).to_broadcast([128, 64, 16]), ALU.is_equal, v1)
                        d1q = D1[:, :].rearrange("p (h k a) -> p h k a", h=4, a=16)
                        d2q = D2[:, :].rearrange("p (h k a) -> p h k a", h=4, a=16)
                        v = tt(d2q, d1q, IF[:, 4 * hh:4 * hh + 4, :].unsqueeze(2).to_broadcast([128, 4, 16, 16]),
                               ALU.mult, v, v2)
                        v = reduce(IS[:, p, 64 * hh:64 * hh + 64],
                                   D2[:, :].rearrange("p (s a) -> p s a", a=16), ALU.add, v)
                        yield 7.5
                    fin.append(v)
                bank, free = take(6)
                t = None
                for n, s in enumerate((IS[:, 0, :], IS[:, 1, :], GR[:, tb, :])):
                    t = turned(bank[:, n * 128:n * 128 + 128], s, fin, vg, free)
                q = slice(tb * 128, tb * 128 + 128)
                a2 = copy(IT[:, :, q], bank[:, 0:256].rearrange("p (a b) -> p a b", a=2), t)
                v = vcopy(GT[:, 0, q], bank[:, 256:384], a2)
                v = tt(GRT[:, 0, :], bank[:, 256:384], GT[:, 0, q], ALU.subtract, v)
                pfree[6] = [a2, v]
                v = vcopy(GT[:, 1, q], GRT[:, 0, :], v)
                v = tt(GRT[:, 1, :], GRT[:, 0, :], GT[:, 1, q], ALU.subtract, v)
                v = vcopy(GT[:, 2, q], GRT[:, 1, :], v)
                DVE.wait(t)
                ittok.append([a2, v])
                yield 1.0
            oe_free, om_free = [[], [], []], [[], []]
            gs_free = [[], []]
            sdone = toptok["c", 3, 7]
            for j in range(4):
                v = vcopy(IOT[:, :, j], iota[:, :])
            same, scaled = {-1: v}, {}

            def hot(n):
                q = slice(4 * n, 4 * n + 4)
                same[n] = tt(OE[n % 3][:, :, :, :], IOT[:, :, :].unsqueeze(1).to_broadcast([128, 2, 128, 4]),
                             IT[:, :, q].unsqueeze(2).to_broadcast([128, 2, 128, 4]), ALU.is_equal,
                             same[-1], ittok[n // 32], oe_free[n % 3])

            def weigh(n):
                q = slice(4 * n, 4 * n + 4)
                scaled[n] = tt(OM[n % 2][:, :, :, :],
                               OE[n % 3][:, 0, :, :].unsqueeze(1).to_broadcast([128, 3, 128, 4]),
                               GT[:, :, q].unsqueeze(2).to_broadcast([128, 3, 128, 4]), ALU.mult,
                               same[n], om_free[n % 2])

            def grid(n):
                b = 6 + n % 2
                bank, free = take(b)
                PE.wait(scaled[n], free)
                for j in range(4):
                    d = bank[:, j * 128:j * 128 + 128]
                    for k in range(3):
                        tk = mm(d, OM[n % 2][:, k, :, j], OE[n % 3][:, 1, :, j], k == 0, k == 2, last=j == 3 and k == 2)
                oe_free[n % 3], om_free[n % 2] = [tk], [tk]
                g, o = n // 8, 4 * (n % 8)
                dst = GS[g % 2][:, :, o:o + 4].rearrange("p i t -> p t i")
                a = copy(dst, bank[:, :].rearrange("p (t i) -> p t i", t=4), tk, gs_free[g % 2], sdone)
                pfree[b] = [a]
                if n % 8 == 7:
                    tk = dma(f"g{g % 2}", dg[g], GS[g % 2][:, :, :], a)
                    gs_free[g % 2] = [tk]
                    dg_tok.append(tk)

            for n in range(130):
                if n < 128:
                    hot(n)
                if 0 <= n - 1 < 128:
                    weigh(n - 1)
                if n > 1:
                    grid(n - 2)
                yield 4.1

        def queries(hp, b, t):
            qt = split(QPH[hp % 2][:, :], QPL[hp % 2][:, :], P[b][:, :], t, qfree[hp % 2])
            pfree[b] = qt
            return hp, qt

        bg = route()
        ts3 = feature_major_abreast([0, 1, 2], XH, XL, xtok)
        behind = [queries(0, 0, ts3[0])]

        def follow(hp, b, t):
            now = queries(hp, b, t)
            key_scores(*behind[0])
            behind[0] = now
            if hp > 1:
                token_scores(hp - 2)

        follow(1, 1, ts3[1])
        follow(2, 2, ts3[2])
        beside(bg)
        for hp in range(3, 16):
            follow(hp, hp % 4, feature_major(hp % 4, XH, XL, xtok))

        def background():
            yield from bg
            for q in (PE, DVE, SC, GP):
                q.wait(wq_end)
            yield from gates()

        hb = Banks([0, 1, 2, 3])
        GI = [at(f"GI{i}", F + 16 + 8 * i, [128, 16, 128], F32) for i in range(2)]
        HI = [at(f"HI{i}", F + 32 + 8 * i, [128, 4, T], F32) for i in range(2)]
        AH = [at(f"AH{i}", F + 48 + 2 * i, [128, T], F32R) for i in range(3)]
        AL = [at(f"AL{i}", F + 54 + 2 * i, [128, T], F32R) for i in range(3)]
        ACC = at("ACC", F + 60, [128, 6144], F32)
        AC = [at(f"AC{i}", 60 + 12 * i, [128, 6144], BF16) for i in range(2)]
        ACa = at("ACa", 84, [128, 4096], BF16)
        ACb = at("ACb", F + 86, [128, 2048], BF16)
        ONE = at("ONE", F + 84, [128, 1], BF16)
        AW = [at(f"AW{i}", F + (86, 94)[i], [128, 1024], F32) for i in range(2)]
        gi_free = [[], []]
        gi_tok = {}
        a_free = [[], [], []]
        a_ready = {}

        def fetch(g):
            s = g % 2
            gi_tok[g] = [
                dma(f"gi{s}", GI[s][:, :, :], dg[:, :, 4 * g:4 * g + 4, :].rearrange("g p i t -> p g (i t)"),
                    gi_free[s], dg_tok),
                dma(f"hi{s}", HI[s][:, :, :], dh[g], gi_free[s], dh_tok[2 * g], dh_tok[2 * g + 1])]

        def activate(i2):
            g, j = divmod(i2, 4)
            if j == 0 and g + 1 < 32:
                fetch(g + 1)
            i, t, f = Tb.take()
            gv = GI[g % 2][:, :, 32 * j:32 * j + 32]
            v = tt(t[:, :].rearrange("p (g t) -> p g t", g=16),
                   HI[g % 2][:, j, :].rearrange("p (g t) -> p g t", g=16), gv, ALU.mult, gi_tok[g], f)
            if j == 3:
                gi_free[g % 2] = [v]
            r = split(AH[i2 % 3][:, :], AL[i2 % 3][:, :], t[:, :], v, a_free[i2 % 3])
            Tb.free[i] = r
            a_ready[i2] = r

        for i2 in range(128):
            if i2 == 124:
                finish_side()
                region = [(DVE.sem, DVE.n), (PE.sem, PE.n)]
                SC.wait(region)
                SP.wait(region)
                fetch(0)
            b, bank, free = hb.next()
            unit = next_unit()
            PE.wait(free)
            for k in range(8):
                PE.wait(xtok[k])
                t = tile(bank, unit, k, XH[:, k, :], XL[:, k, :], k == 0, k == 7)
                tick()
            if i2 % 2 == 0:
                hi, hbuf, hf = HID.take()
            if i2 == 0:
                key_scores(*behind[0])
                token_scores(14)
                token_scores(15)
                wq_end = [(PE.sem, PE.n), (DVE.sem, DVE.n), (SC.sem, SC.n)]
                beside(background())
                SC.wait(wq_end)
            a = act(hbuf[:, i2 % 2, :], bank[:, :], ACT.Gelu, t, hf)
            pfree[b] = [a]
            if i2 % 2 == 1:
                tk = dma(f"h{hi}", dh[i2 // 4, :, 2 * (i2 // 2 % 2):2 * (i2 // 2 % 2) + 2, :], hbuf[:, :, :], a)
                HID.free[hi] = [tk]
                dh_tok[i2 // 2] = tk
            if i2 == 126:
                activate(0)
                activate(1)
        u_end = (PE.sem, PE.n)

        acc_tok = {}
        k_cs = act(csil[:, :], CV, ACT.Silu, k_s)

        ach_tok = []

        def third(c):
            part, n = (ACa, c) if c < 8 else (ACb, c - 8)
            return part[:, 512 * n:512 * n + 512]

        def modulation():
            aw_free = [[], []]
            for k in range(8):
                for c in range(6):
                    s = c % 2
                    w = dma(f"aw{s}", AW[s][:, :], adaw[k, :, 1024 * c:1024 * c + 1024], aw_free[s], u_end)
                    dst = ACC[:, 1024 * c:1024 * c + 1024]
                    if k == 0:
                        v = ts(dst, AW[s][:, :], csil[:, 0:1], None, ALU.mult, None, w, k_cs, u_end)
                    else:
                        v = stt(dst, AW[s][:, :], csil[:, k:k + 1], dst, ALU.mult, ALU.add, w, acc_tok[c])
                    aw_free[s] = [v]
                    acc_tok[c] = v
                    yield 14
            for c in range(12):
                q = slice(512 * c, 512 * c + 512)
                v = acc_tok[c // 2]
                for i in range(2):
                    a = copy(AC[i][:, q], ACC[:, q], v, u_end)
                    v = tt(ACC[:, q], ACC[:, q], AC[i][:, q], ALU.subtract, a)
                    yield 4
                ach_tok.append([a, copy(third(c), ACC[:, q], v, list(acc_tok.values()))])

        COS = at("COS", F + 90, [128, T], F32)
        SIN = at("SIN", F + 92, [128, T], F32)
        PI = at("PI", F + 98, [128, T], I32)
        rot = {}

        def rotations():
            k_p = dma("c0", PI[:, :], pos.partition_broadcast(128), u_end)
            ia, ang, fa = Tb.take()
            ib, qn, fb = Tb.take()
            v = vcopy(ang[:, :], PI[:, :], k_p, fa)
            v = ts(ang[:, :], ang[:, :], invf[:, 0:1], None, ALU.mult, None, v)
            yield 8
            for dst, shift in ((SIN, 0.0), (COS, 0.25)):
                v = ts(qn[:, :], ang[:, :], float(1.0 / (2 * np.pi)), shift, ALU.mult, ALU.add, v, fb, u_end)
                v = ts(qn[:, :], qn[:, :], 12582912.0, None, ALU.add, None, v)
                v = ts(qn[:, :], qn[:, :], -12582912.0, None, ALU.add, None, v)
                yield 8
                v = stt(dst[:, :], qn[:, :], -6.28125, ang[:, :], ALU.mult, ALU.add, v)
                v = stt(dst[:, :], qn[:, :], -float(np.float32(0.0019350051879882812)), dst[:, :], ALU.mult, ALU.add, v)
                yield 8
                rest = 2 * np.pi - 6.28125 - 0.0019350051879882812
                v = stt(dst[:, :], qn[:, :], -float(rest), dst[:, :], ALU.mult, ALU.add, v)
                if shift:
                    v = ts(dst[:, :], dst[:, :], float(np.pi / 2), None, ALU.add, None, v)
                v = ts(dst[:, :], dst[:, :], float(np.float32(3.1415925)), float(np.float32(-3.1415925)),
                       ALU.min, ALU.max, v)
                a = act(dst[:, :], dst[:, :], ACT.Sin, v)
                yield 8
            rot["cos"] = a
            rot["sin"] = ts(SIN[64:128, :], SIN[64:128, :], -1.0, None, ALU.mult, None, a)
            Tb.free[ia] = [v]
            Tb.free[ib] = [v]

        def prepare():
            yield from rotations()
            yield from modulation()

        beside(prepare())
        banks = {}
        for i2 in range(128):
            unit = next_unit()
            s = i2 % 3
            PE.wait(a_ready[i2])
            ydone = []
            for d in range(8):
                if i2 == 0:
                    banks[d], free = take(d)
                    PE.wait(free)
                ydone.append(tile(banks[d], unit, d, AH[s][:, :], AL[s][:, :], i2 == 0, i2 == 127, last=i2 == 127))
                if i2 > 3:
                    tick()
            a_free[s] = [(PE.sem, PE.n)]
            if i2 + 2 < 128:
                activate(i2 + 2)
        finish_side()
        one = vset(ONE[:, :], 1.0)
        split_ahead()

        for d in range(8):
            v = tt(hT[:, d, :], P[d][:, :], hT[:, d, :], ALU.add, ydone[d])
            pfree[d] = [v]
            if d == 0:
                mbank, free = take(0)
                PE.wait(free, one, ach_tok)
                for n in range(48):
                    w = slice(n * 128, n * 128 + 128)
                    c, r = divmod(n, 4)
                    mm(mbank[:, n:n + 1], AC[0][:, w], ONE[:, :], True, False)
                    mm(mbank[:, n:n + 1], AC[1][:, w], ONE[:, :], False, False)
                    tm = mm(mbank[:, n:n + 1], third(c)[:, 128 * r:128 * r + 128], ONE[:, :], False, True, last=n == 47)
            if d == 1:
                rms1 = Rms(1, (2, 2, 2, 1, 1))
            if d == 2:
                rms2 = Rms(2, (2, 2, 2, 1, 1), GF)
                for k in range(2):
                    rms1.add(k, hT[:, k, :], v)
                    rms2.add(k, hT[:, k, :], v)
            if d > 1:
                rms1.add(d, hT[:, d, :], v)
                rms2.add(d, hT[:, d, :], v)
        everyone()
        v = tt(mod[:, :], mbank[:, 0:48], ADB, ALU.add, tm)
        pfree[0] = [v]
        p1, p2 = rms1.total(), rms2.total()
        i1_, q1, v1 = diagonal(1, 32, p1)
        i2_, q2, v2 = diagonal(2, 48, p2)
        va = ts(st[:, 36:40], st[:, 32:36], 1.0 / 1024, EPS, ALU.mult, ALU.add, v1)
        va = recip(st[:, 40:44], st[:, 36:40], va)
        vb = tt(st[:, 52:56], st[:, 48:52], st[:, 40:44], ALU.mult, va, v2)
        vb = ts(st[:, 52:56], st[:, 52:56], 1.0 / 1024, EPS, ALU.mult, ALU.add, vb)
        vb = recip(st[:, 56:60], st[:, 52:56], vb)
        vb = tt(st[:, 56:60], st[:, 56:60], st[:, 40:44], ALU.mult, vb)
        ab = act(st[:, 60:64], st[:, 56:60], ACT.Sqrt, vb)
        aa = act(st[:, 44:48], st[:, 40:44], ACT.Sqrt, va)
        v = ts(gmod[:, 0:8], mod[:, 8:16], 1.0, None, ALU.add, None, v)
        v = tt(gmod[:, 0:8], gmod[:, 0:8], GM, ALU.mult, v)
        v = tt(gmod[:, 0:8], gmod[:, 0:8], GF, ALU.mult, v)
        vn = ts(gmod[:, 8:16], mod[:, 32:40], 1.0, None, ALU.add, None, v)
        k_mod = tt(gmod[:, 8:16], gmod[:, 8:16], GN, ALU.mult, vn)
        SH_M, GT_M, SH_F, GT_F = mod[:, 0:8], mod[:, 16:24], mod[:, 24:32], mod[:, 40:48]
        bank, free = take(4)
        factor = bank, spread(4, (i2_, q2, diagonals(q2, 60, ab)), free)
        _, free = take(3)
        t_r1 = spread(3, (i1_, q1, diagonals(q1, 44, aa)), free)
        xtok = norm_split(hT, factor, gmod[:, 0:8], SH_M, 4, k_mod)
        h_read = xtok[-1]
        ir1, R1, f = Tb.take()
        t_r1 = copy(R1[:, :], P[3][:, :], t_r1, f)
        pfree[3] = [t_r1]

        VR = [[at(f"VR{i}{j}", F + 16 + 4 * i + 2 * j, [128, 4, 128], F32R) for j in range(2)] for i in range(2)]
        RH = at("RH", F + 32, [128, 8, T], F32R)
        RL = at("RL", F + 48, [128, 8, T], F32R)
        QR = [[at(f"QR{i}{j}", F + 64 + 8 * i + 2 * j, [128, T], F32R) for j in range(4)] for i in range(2)]
        offs = [0, 512, 896, 1152, 1280]
        SRH = at("SRH", F + 80, [128, 1280], F32R)
        SRL = at("SRL", F + 85, [128, 1280], F32R)
        DM = [at(f"DM{i}", F + 94 + 2 * i, [128, T], F32) for i in range(2)]

        qr_free, dm_free, vr_free = [[], []], [[], []], [[], []]
        rtok = [[] for _ in range(8)]
        heads = {}

        def rope(b, H, L, t, free):
            i, u, f = Tb.take()
            j, w, f2 = Tb.take()
            v1 = tt(u[:, :], P[b][:, :], COS[:, :], ALU.mult, t, f, rot["cos"])
            v2 = tt(w[0:64, :], P[b][64:128, :], SIN[64:128, :], ALU.mult, f2, rot["sin"])
            v3 = tt(w[64:128, :], P[b][0:64, :], SIN[0:64, :], ALU.mult)
            pfree[b] = [v3]
            v = tt(u[:, :], u[:, :], w[:, :], ALU.add, v1, v2, v3)
            Tb.free[j] = [v]
            r = split(H[:, :], L[:, :], u[:, :], v, free)
            Tb.free[i] = r
            return r

        def project(h):
            q = QR[h % 2]
            if h == 0:
                tq, tk, tv = feature_major_abreast([0, 1, 7], XH, XL, xtok)
                rq = rope(0, q[0], q[1], tq, qr_free[h % 2])
                rk = rope(1, q[2], q[3], tk, qr_free[h % 2])
                bv = 7
            else:
                tq = feature_major(0, XH, XL, xtok)
                rq = rope(0, q[0], q[1], tq, qr_free[h % 2])
                tk = feature_major(1, XH, XL, xtok)
                rk = rope(1, q[2], q[3], tk, qr_free[h % 2])
                tv = feature_major(0, XH, XL, xtok)
                bv = 0
            i, u, f = Tb.take()
            a = copy(u[:, :], P[bv][:, :], tv, f)
            pfree[bv] = [a]
            bs = 2 if h == 0 else 1
            t = feature_major(bs, XH, XL, xtok)
            bank, free = take(7)
            for c in range(4):
                tv = turned(bank[:, 128 * c:128 * c + 128], u[:, 128 * c:128 * c + 128], a, free)
            Tb.free[i] = [tv]
            b4 = bank[:, :].rearrange("p (b c) -> p b c", b=4)
            c = 8 * (h % 2)
            v = reduce(st[:, c:c + 4], b4, ALU.add, tv)
            v = ts(st[:, c + 4:c + 8], st[:, c:c + 4], -1.0 / 128, None, ALU.mult, None, v)
            i, u, f = Tb.take()
            u4 = u[:, :].rearrange("p (b c) -> p b c", b=4)
            v = tt(u4, b4, st[:, c + 4:c + 8].unsqueeze(2).to_broadcast([128, 4, 128]), ALU.add, v, f)
            pfree[7] = [v]
            rv = split(VR[h % 2][0][:, :, :], VR[h % 2][1][:, :, :], u4, v, vr_free[h % 2])
            Tb.free[i] = rv
            i, sg, f = Tb.take()
            a = act(sg[:, :], P[bs][:, :], ACT.Silu, t, f)
            pfree[bs] = [a]
            kd = dma(f"dm{h % 2}", DM[h % 2][:, :], dmat[:, T * h:T * h + T], dm_free[h % 2])
            heads[h] = (rq + rk, rv, i, sg, a, kd)

        def retain():
            sr_free = []
            sb = Banks([2, 3])
            ending = None

            def normal(h, i, y, part):
                def end():
                    _, free = take(6)
                    t = spread(6, part, free)
                    v = tt(y[:, :], y[:, :], P[6][:, :], ALU.mult, t)
                    pfree[6] = [v]
                    r = split(RH[:, h, :], RL[:, h, :], y[:, :], v)
                    Tb.free[i] = r
                    rtok[h] = r
                return end

            for h in range(8):
                while h not in heads:
                    yield None
                qk, rv, gi, sg, ga, kd = heads[h]
                q = QR[h % 2]
                lows, pts = None, []
                for kb in range(4):
                    n = T - 128 * kb
                    b, bank, free = sb.next()
                    ks = slice(128 * kb, 128 * kb + 128)
                    mm(bank[:, 0:n], q[2][:, ks], q[0][:, 128 * kb:T], True, False, free, qk)
                    mm(bank[:, 0:n], q[2][:, ks], q[1][:, 128 * kb:T], False, False)
                    t = mm(bank[:, 0:n], q[3][:, ks], q[0][:, 128 * kb:T], False, True, last=True)
                    if lows:
                        lows()
                    i, u, f = Tb.take()
                    v = tt(u[:, 0:n], bank[:, 0:n], DM[h % 2][:, 0:n], ALU.mult, t, f, kd)
                    pfree[b] = [v]
                    s = slice(offs[kb], offs[kb + 1])
                    a = copy(SRH[:, s], u[:, 0:n], v, sr_free)

                    def lows(i=i, u=u, s=s, n=n, a=a):
                        w = tt(SRL[:, s], u[:, 0:n], SRH[:, s].bitcast(F32), ALU.subtract, a, sr_free)
                        Tb.free[i] = [w]
                        pts.append([a, w])
                    if kb == 0 and ending:
                        ending()
                    if h in (1, 2):
                        k = 4 * (h - 1) + kb
                        v = stt(hT[:, k, :], hT[:, k, :], GF[:, k:k + 1], R1[:, :], ALU.mult, ALU.mult, t_r1, h_read)
                        Tb.free[ir1] = [v] if k == 7 else None
                    yield 4.1
                lows()
                qr_free[h % 2] = [t]
                dm_free[h % 2] = [v]
                yield 4.1
                bank, free = take(4)
                PE.wait(free, rv)
                vh, vl = VR[h % 2]
                for kb in range(4):
                    d = bank[:, 128 * kb:T]
                    s = slice(offs[kb], offs[kb + 1])
                    mm(d, vh[:, kb, :], SRH[:, s], kb == 0, False, pts[kb])
                    mm(d, vh[:, kb, :], SRL[:, s], False, False)
                    t = mm(d, vl[:, kb, :], SRH[:, s], False, kb == 3, last=kb == 3)
                sr_free = [t]
                vr_free[h % 2] = [t]
                j, sq, f = Tb.take()
                a = act(sq[:, :], bank[:, :], ACT.Square, t, f)
                v = tt(sg[:, :], bank[:, :], sg[:, :], ALU.mult, ga, a)
                pfree[4] = [a, v]
                yield 6.0
                bank, free = take(5)
                t = mm(bank[:, :], ones[:, :], sq[:, :], True, True, a, free, last=True)
                Tb.free[j] = [t]
                ending = normal(h, gi, sg, inverse_root(5, 1.0 / 128, t))
                yield 4.1
            ending()

        project(0)
        beside(retain())
        for h in range(1, 8):
            project(h)

        CH = at("CH", F + 64, [128, 8, T], F32R)
        CL = at("CL", F + 80, [128, 8, T], F32R)
        U = [at(f"UC{i}", F + 96 + 2.0625 * i, [128, 516], F32) for i in range(2)]
        MG = at("MG", F + 16, [128, 8, T], F32)
        mgt = [None] * 8
        ctok = []
        uf = [[], []]
        for m in range(8):
            bb, bc, bu = ((0, 1, 7), (2, 3, 4), (0, 1, 5))[0 if m == 0 else 2 - m % 2]
            tb_ = feature_major(bb, XH, XL, xtok)
            tc = feature_major(bc, XH, XL, xtok)
            i, c, f = Tb.take()
            a = copy(c[:, :], P[bc][:, :], tc, f)
            pfree[bc] = [a]
            tu = feature_major(bu, XH, XL, xtok)
            if m == 0:
                finish_side()
                over = [(PE.sem, PE.n), (DVE.sem, DVE.n), (SC.sem, SC.n)]
                DVE.wait(over)
                SC.wait(over)
                uz = [vset(U[i][:, 0:2], 0.0) for i in range(2)]
            u = U[m % 2]
            v = tt(u[:, 2:514], P[bu][:, :], c[:, :], ALU.mult, tu, a, uf[m % 2], uz)
            pfree[bu] = [v]
            v = ts(c[:, :], u[:, 0:512], CW[:, m:m + 1], None, ALU.mult, None, v)
            v = stt(c[:, :], u[:, 1:513], CW[:, 8 + m:9 + m], c[:, :], ALU.mult, ALU.add, v)
            v = stt(c[:, :], u[:, 2:514], CW[:, 16 + m:17 + m], c[:, :], ALU.mult, ALU.add, v)
            uf[m % 2] = [v]
            v = tt(c[:, :], P[bb][:, :], c[:, :], ALU.mult, v, tb_)
            pfree[bb] = [v]
            r = split(CH[:, m, :], CL[:, m, :], c[:, :], v)
            Tb.free[i] = r
            ctok.append(r)

        def gate(b):
            t = feature_major(b, XH, XL, xtok)
            i, sg, f = Tb.take()
            a = act(sg[:, :], P[b][:, :], ACT.Sigmoid, t, f)
            pfree[b] = [a]
            return i, sg, a

        def merge(m):
            b = 4 * (m % 2)
            ia, sa, aa = gate(b)
            if m == 7:
                ib, sb_, ab = gate(b + 2)
                x_read = [(PE.sem, PE.n)]
                for n in range(7):
                    merged(n, x_read)
            t = feature_major(b + 1, RH, RL, rtok)
            v1 = tt(MG[:, m, :], P[b + 1][:, :], sa[:, :], ALU.mult, t, aa)
            pfree[b + 1] = [v1]
            Tb.free[ia] = [v1]
            if m < 7:
                ib, sb_, ab = gate(b + 2)
            t = feature_major(b + 3, CH, CL, ctok)
            v = tt(sb_[:, :], P[b + 3][:, :], sb_[:, :], ALU.mult, t, ab)
            pfree[b + 3] = [v]
            mgt[m] = tt(MG[:, m, :], MG[:, m, :], sb_[:, :], ALU.add, v, v1)
            Tb.free[ib] = [mgt[m]]
            if m == 7:
                split_ahead()
                merged(7, x_read)

        gtok = []

        def merged(m, x_read):
            gtok.append(split(XH[:, m, :], XL[:, m, :], MG[:, m, :], mgt[m], x_read))

        for m in range(7):
            merge(m)
        merge(7)
        rms = Rms(4)
        hb = Banks([0, 1, 2, 3])
        for m in range(8):
            b = m % 4
            if m == 0:
                ts3 = feature_major_abreast([0, 1, 2], XH, XL, gtok)
            t = ts3[m] if m < 3 else feature_major(b, XH, XL, gtok)
            v = stt(hT[:, m, :], P[b][:, :], GT_M[:, m:m + 1], hT[:, m, :], ALU.mult, ALU.add, t)
            pfree[b] = [v]
            rms.add(m, hT[:, m, :], v)

        split_ahead()
        factor = rms.end(5)
        everyone()
        xtok = norm_split(hT, factor, gmod[:, 8:16], SH_F, 5)
        FH = at("FH", F + 16, [128, 11, T], F32R)
        FL = at("FL", F + 38, [128, 11, T], F32R)
        NF = 22
        FHb = at("FHb", F + 60, [128, 11, T], F32R)
        FLb = [at(f"FLb{i}", F + 82 + 2 * i, [128, 1, T], F32R) for i in range(9)]
        ftok = []

        def fpart(k):
            if k < 11:
                return FH[:, k, :], FL[:, k, :]
            if k - 11 < 9:
                return FHb[:, k - 11, :], FLb[k - 11][:, 0, :]
            return FHb[:, k - 11, :], tail[k - 20]

        tail = []
        for _ in range(2):
            i, t_, f = Tb.take()
            tail.append((i, f))
        tl = [at(f"TL{n}", 92 + 2 * i, [128, T], F32R) for n, (i, f) in enumerate(tail)]
        tl_free = [f for _, f in tail]
        keep = sorted(i for i, _ in tail)
        rest = [i for i in range(7) if i not in keep]
        sub = Slots([Tb.bufs[i] for i in rest])
        sub.free = [Tb.free[i] for i in rest]
        tail = [tl[0][:, :], tl[1][:, :]]
        for m in range(NF):
            b = 2 * (m % 2)
            if m == 0:
                t3 = feature_major_abreast([0, 1, 2], XH, XL, xtok)
            t = t3[2 * m] if m < 2 else feature_major(b, XH, XL, xtok)
            i, g_, f = sub.take()
            a = act(g_[:, :], P[b][:, :], ACT.Silu, t, f)
            pfree[b] = [a]
            t = t3[1] if m == 0 else feature_major(b + 1, XH, XL, xtok)
            v = tt(g_[:, :], P[b + 1][:, :], g_[:, :], ALU.mult, t, a)
            pfree[b + 1] = [v]
            H, L = fpart(m)
            r = split(H, L, g_[:, :], v, tl_free)
            sub.free[i] = r
            ftok.append(r)
        n = 0
        for i, f in zip(rest, sub.free):
            Tb.free[i] = f
        rms = Rms(4)
        for m in range(8):
            bank, free = take(m % 4)
            PE.wait(free)
            for k in range(NF):
                if n % 8 == 0:
                    unit = next_unit()
                H, L = fpart(k)
                PE.wait(ftok[k])
                t = tile(bank, unit, n % 8, H, L, k == 0, k == NF - 1, last=k == NF - 1)
                n += 1
            v = stt(hT[:, m, :], bank[:, :], GT_F[:, m:m + 1], hT[:, m, :], ALU.mult, ALU.add, t)
            pfree[m % 4] = [v]
            rms.add(m, hT[:, m, :], v)

        r, s_ = rms.end(5)
        ot = out.rearrange("(k p) t -> p k t", p=128)
        last = []
        for k in range(8):
            v = stt(hT[:, k, :], hT[:, k, :], GE[:, k:k + 1], r[:, :], ALU.mult, ALU.mult, s_)
            last.append(dma(f"o{k % 4}", ot[:, k, :], hT[:, k, :], v))
        SP.wait(last)

        block = ctx.enter_context(nc.Block())

        @block.sync
        def _(e):
            SP.play(e)

        @block.tensor
        def _(e):
            PE.play(e)

        @block.vector
        def _(e):
            DVE.play(e)

        @block.scalar
        def _(e):
            SC.play(e)

        @block.gpsimd
        def _(e):
            GP.play(e)


def feature_units(w):
    k, n = w.shape
    return w.reshape(k // 128, 128, n // 128, 128).transpose(2, 1, 0, 3).reshape(n // 128, 128, k)


def columns(g):
    return g.reshape(-1, 128).T


def constants():
    i = np.arange(128)[:, None]
    j = np.arange(512)[None, :]
    d = i + 384 - j
    count = ((d >= 0) & (d <= 128)).astype(np.float32)
    count += (d >= 0) & (d % 4 == 0)
    count += (d >= 0) & (d % 16 == 0)
    c = np.zeros((128, 1793), np.float32)
    c[:, 0:128] = np.eye(128)
    c[:, 128:256] = np.arange(128)[None, :]
    c[:, 256:768] = count
    c[:, 768:1280] = np.where(count > 0, 0.0, FAR)
    c[:, 1280:1792] = np.where(d >= 0, 0.0, FAR)
    inv = 1.0 / (np.float32(10000.0) ** (np.arange(0, 128, 2, dtype=np.float32) / np.float32(128)))
    c[:, 1792] = np.concatenate([inv, inv])
    lg = np.log(1.0 - 2.0 ** (-5.0 - np.arange(8)))
    rel = np.arange(512)[None, :] - np.arange(128)[:, None]
    dm = np.where(rel[None] >= 0, np.exp(lg[:, None, None] * np.maximum(rel, 0)[None]), 0.0) * 128 ** -0.5
    dm = dm.transpose(1, 0, 2).reshape(128, 8 * 512).astype(np.float32)
    slope = 2.0 ** -np.arange(1, 9, dtype=np.float32)[:, None]
    t = np.arange(512, dtype=np.float32)[None, :]
    return c, dm, slope * t


def kernel(**inputs):
    import concourse.bacc as bacc
    from concourse.bass_utils import run_bass_kernel_spmd as run

    a = {k: np.asarray(v) for k, v in inputs.items()}
    w = a["w_in"][0]
    fq, fk, fv, ff = w[:, 0:512], w[:, 512:1024], w[:, 1024:1536], w[:, 1536:1544]
    dq, dk, dv = w[:, 1544:2056], w[:, 2056:2568], w[:, 2568:3080]
    col = lambda m, h: m[:, 128 * h:128 * h + 128]
    parts = [feature_units(np.pad(ff, ((0, 0), (0, 120))))]
    for trio in ((dq, dk, dv), (fq, fk, fv)):
        for g in range(4):
            parts += [feature_units(col(m, g)) for m in trio]
    parts += [feature_units(a["w_out"][0]), feature_units(a["peer_wq"][0])]
    w2 = a["w_in_2"][0]
    q, k, v, gr, b, c, u, ga, gb = (w2[:, 1024 * i:1024 * i + 1024] for i in range(9))
    for h in range(8):
        parts += [feature_units(col(m, h)) for m in (q, k, v, gr)]
    for h in range(8):
        parts += [feature_units(col(m, h)) for m in (b, c, u)]
    ro, co = a["ret_w_out_2"][0], a["conv_w_out_2"][0]
    for h in range(8):
        order = (ga, gb, ro, co) if h == 7 else (ga, ro, gb, co)
        parts += [feature_units(col(m, h)) for m in order]
    parts.append(feature_units(a["mix_w_out_2"][0]))
    for h in range(22):
        parts += [feature_units(col(a["ffn_w_gate_2"][0], h)), feature_units(col(a["ffn_w_up_2"][0], h))]
    down = feature_units(a["ffn_w_down_2"][0])
    down = down.reshape(8, 128, 22, 128).transpose(0, 2, 1, 3).reshape(22, 8, 128, 128)
    parts.append(down.transpose(0, 2, 1, 3).reshape(22, 128, 1024))
    wts = np.concatenate(parts)
    ut = np.ascontiguousarray(a["peer_u"][0].reshape(128, 128, 8, 128).transpose(1, 3, 2, 0)).reshape(128, 128, 1024)
    vt = np.ascontiguousarray(a["peer_v"][0].reshape(128, 128, 1024).transpose(1, 0, 2))
    skt = a["peer_subkeys"][0].reshape(16, 128, 128).transpose(2, 0, 1).reshape(128, 2048)
    small = np.zeros((128, 144), np.float32)
    for n, name in enumerate(("norm1_g", "norm2_g", "normf_g", "norm_mix_g_2", "norm_ffn_g_2", "final_norm_g_2")):
        small[:, 8 * n:8 * n + 8] = columns(a[name])
    small[:, 48:96] = columns(a["ada_b_2"])
    small[:, 96:120] = columns(a["conv_w_2"])
    small[:, 120:128] = columns(a["c_2"])
    small[0:8, 128] = a["b_forget"][0]
    cst, dmat, augd = constants()
    feeds = {
        "x": a["x"][0].T, "wts": wts, "ut": ut, "vt": vt, "skt": skt, "small": small, "cst": cst,
        "dmat": dmat, "augd": augd, "pos": a["positions_2"][0], "adaw": a["ada_w_2"][0].reshape(8, 128, 6144),
    }
    feeds = {n: np.ascontiguousarray(v) for n, v in feeds.items()}
    nc = bacc.Bacc("TRN2", target_bir_lowering=False, num_devices=1)
    args = [nc.dram_tensor(n, v.shape, mybir.dt.from_np(v.dtype), kind="ExternalInput").ap()
            for n, v in feeds.items()]
    out = nc.dram_tensor("out", (1024, T), F32, kind="ExternalOutput").ap()
    build_program(nc, *args, out)
    r = run(nc, [feeds], core_ids=[0])
    return np.ascontiguousarray(r.results[0]["out"].T)[None]
```
